# Optimizing a Trainium2 kernel written in Bass

```python
import jax, jax.numpy as jnp
from jax import lax
import numpy as np

D_MODEL = 1024
BATCH = 1
SEQ = 512
DEPTH = 1
DEC_BATCH = 8
DEC_SEQ = 1
PAST_LEN = 4096
PAGE_SIZE = 128

MIX_DIM = D_MODEL
CONV_DIM = MIX_DIM // 2
CONV_GROUPS = 8
CONV_WIDTH = 3
RET_DIM = MIX_DIM - CONV_DIM
RET_HEADS = 4
RET_DK = RET_DIM // RET_HEADS
RET_DV = RET_DIM // RET_HEADS
RET_CHUNK = 128
ROPE_BASE = 10000.0
IN_PROJ_DIM = 3 * CONV_DIM + 4 * RET_DIM
N_GROUPS = 4
EXPERTS_PER_GROUP = 8
N_EXPERTS = N_GROUPS * EXPERTS_PER_GROUP
TOP_K_INNER = 2
D_FF_EXPERT = D_MODEL // 2
PLE_DIM = 256
EPS = 1e-6

kernel_name = 'hymba_conv_retention_hmoe_step'

def rmsnorm(x, g):
    xf = x.astype(jnp.float32)
    y = xf * lax.rsqrt(jnp.mean(xf * xf, axis=-1, keepdims=True) + EPS)
    return (y * g.astype(jnp.float32)).astype(x.dtype)

def rope(x, pos):
    d = x.shape[-1]
    inv = 1.0 / (ROPE_BASE ** (jnp.arange(0, d, 2, dtype=jnp.float32) / d))
    ang = pos.astype(jnp.float32)[:, None] * inv[None, :]
    cos = jnp.cos(ang)[None, :, None, :]
    sin = jnp.sin(ang)[None, :, None, :]
    x1, x2 = x[..., : d // 2], x[..., d // 2:]
    return jnp.concatenate([x1 * cos - x2 * sin, x1 * sin + x2 * cos], axis=-1)

def short_conv(z, buf, w):
    T = z.shape[1]
    zc = jnp.concatenate([buf.astype(z.dtype), z], axis=1)
    wz = w.astype(z.dtype)
    y = wz[0] * zc[:, 0:T]
    for i in range(1, CONV_WIDTH):
        y = y + wz[i] * zc[:, i:i + T]
    return y, zc[:, T:]

def retention(q, k, v, s0, log_gamma):
    B, T, H, dk = q.shape
    dv = v.shape[-1]
    C = RET_CHUNK if T % RET_CHUNK == 0 else T
    n = T // C
    idx = jnp.arange(C, dtype=jnp.float32)
    diff = idx[:, None] - idx[None, :]
    lg = log_gamma[:, None, None]
    dmask = jnp.where((diff >= 0.0)[None], jnp.exp(lg * jnp.maximum(diff, 0.0)[None]), 0.0)
    q_dec = jnp.exp(log_gamma[None, :] * (idx[:, None] + 1.0))
    k_dec = jnp.exp(log_gamma[None, :] * (C - 1.0 - idx[:, None]))
    c_dec = jnp.exp(log_gamma * C)

    def to_chunks(a):
        return a.reshape(B, n, C, H, a.shape[-1]).transpose(1, 0, 2, 3, 4)

    def step(s, inp):
        qc, kc, vc = inp
        scores = jnp.einsum('bihd,bjhd->bhij', qc, kc) * dmask[None]
        o = (jnp.einsum('bhij,bjhe->bihe', scores, vc)
             + jnp.einsum('bihd,bhde->bihe', qc * q_dec[None, :, :, None], s))
        s_new = (s * c_dec[None, :, None, None]
                 + jnp.einsum('bjhd,bjhe->bhde', kc * k_dec[None, :, :, None], vc))
        return s_new, o

    s_fin, o = lax.scan(step, s0, (to_chunks(q), to_chunks(k), to_chunks(v)))
    o = o.transpose(1, 0, 2, 3, 4).reshape(B, T, H, dv)
    return o, s_fin

def mixer(u, conv_buf, ret_state, pos, log_gamma, w_in, conv_w, ret_gn, w_o):
    B, T, _ = u.shape
    f32 = jnp.float32
    proj = u @ w_in.astype(u.dtype)
    cuts = [CONV_DIM, 2 * CONV_DIM, 3 * CONV_DIM,
            3 * CONV_DIM + RET_DIM, 3 * CONV_DIM + 2 * RET_DIM, 3 * CONV_DIM + 3 * RET_DIM]
    gb, gc, hc, q, k, v, g = jnp.split(proj, cuts, axis=-1)
    yc, new_buf = short_conv(gc * hc, conv_buf, conv_w)
    yc = gb * yc
    qh = rope(q.astype(f32).reshape(B, T, RET_HEADS, RET_DK), pos)
    kh = rope(k.astype(f32).reshape(B, T, RET_HEADS, RET_DK), pos) * (RET_DK ** -0.5)
    vh = v.astype(f32).reshape(B, T, RET_HEADS, RET_DV)
    o, s_new = retention(qh, kh, vh, ret_state.astype(f32), log_gamma)
    mu = jnp.mean(o, axis=-1, keepdims=True)
    oc = o - mu
    o = oc * lax.rsqrt(jnp.mean(oc * oc, axis=-1, keepdims=True) + EPS)
    o = o.reshape(B, T, RET_DIM) * ret_gn.astype(f32) * jax.nn.silu(g.astype(f32))
    out = jnp.concatenate([yc, o.astype(u.dtype)], axis=-1) @ w_o.astype(u.dtype)
    return out, new_buf, s_new

def hier_moe(u, w_rg, b_rg, w_re, b_re, w_gate, w_up, w_down):
    f32 = jnp.float32
    B, T, D = u.shape
    x = u.reshape(B * T, D)
    g_prob = jax.nn.softmax((x @ w_rg.astype(x.dtype)).astype(f32) + b_rg.astype(f32), axis=-1)
    g_top, g_idx = lax.top_k(g_prob, 1)
    e_logits = (x @ w_re.astype(x.dtype)).astype(f32).reshape(-1, N_GROUPS, EXPERTS_PER_GROUP) + b_re.astype(f32)
    e_sel = jnp.einsum('nge,ng->ne', e_logits, jax.nn.one_hot(g_idx[:, 0], N_GROUPS, dtype=f32))
    e_top, e_idx = lax.top_k(jax.nn.softmax(e_sel, axis=-1), TOP_K_INNER)
    wk = g_top * e_top / jnp.sum(e_top, axis=-1, keepdims=True)
    eid = g_idx * EXPERTS_PER_GROUP + e_idx
    cw = jnp.sum(jax.nn.one_hot(eid, N_EXPERTS, dtype=f32) * wk[..., None], axis=1)
    y = jnp.zeros((B * T, D), f32)
    for e in range(N_EXPERTS):
        h = jax.nn.silu(x @ w_gate[e].astype(x.dtype)) * (x @ w_up[e].astype(x.dtype))
        y = y + cw[:, e:e + 1] * (h @ w_down[e].astype(x.dtype)).astype(f32)
    return y.astype(u.dtype).reshape(B, T, D)

def block(h, p, conv_buf, ret_state, pos, log_gamma, g_mix, w_in, conv_w, ret_gn, w_o, g_ffn,
          w_rg, b_rg, w_re, b_re, w_gate, w_up, w_down, g_ple, w_ple_proj, w_ple_gate):
    m, new_buf, new_state = mixer(rmsnorm(h, g_mix), conv_buf, ret_state, pos, log_gamma,
                                  w_in, conv_w, ret_gn, w_o)
    h = h + m
    h = h + hier_moe(rmsnorm(h, g_ffn), w_rg, b_rg, w_re, b_re, w_gate, w_up, w_down)
    gate = jax.nn.sigmoid(rmsnorm(h, g_ple) @ w_ple_gate.astype(h.dtype))
    h = h + (p.astype(h.dtype) @ w_ple_proj.astype(h.dtype)) * gate
    return h, new_buf, new_state

def setup_inputs(seed: int = 0) -> dict:
    key = jax.random.key(seed)
    ks = jax.random.split(key, 24)
    nrm = jax.random.normal
    f32 = jnp.float32
    D = D_MODEL
    return {
        'x_prompt': nrm(ks[0], (BATCH, SEQ, D), f32),
        'x_sample': nrm(ks[1], (DEC_BATCH, DEC_SEQ, D), f32),
        'state_conv': nrm(ks[2], (DEPTH, DEC_BATCH, CONV_WIDTH - 1, CONV_DIM), f32),
        'state_ret': 0.5 * nrm(ks[3], (DEPTH, DEC_BATCH, RET_HEADS, RET_DK, RET_DV), f32),
        'p_prompt': nrm(ks[4], (DEPTH, BATCH, SEQ, PLE_DIM), f32),
        'p_sample': nrm(ks[5], (DEPTH, DEC_BATCH, DEC_SEQ, PLE_DIM), f32),
        'g_mix': 1.0 + 0.01 * nrm(ks[6], (DEPTH, D), f32),
        'w_in': nrm(ks[7], (DEPTH, D, IN_PROJ_DIM), f32) * D ** -0.5,
        'conv_w': nrm(ks[8], (DEPTH, CONV_WIDTH, CONV_DIM), f32) * CONV_WIDTH ** -0.5,
        'ret_gn': 1.0 + 0.01 * nrm(ks[9], (DEPTH, RET_DIM), f32),
        'w_o': nrm(ks[10], (DEPTH, MIX_DIM, D), f32) * MIX_DIM ** -0.5,
        'g_ffn': 1.0 + 0.01 * nrm(ks[11], (DEPTH, D), f32),
        'w_router_group': nrm(ks[12], (DEPTH, D, N_GROUPS), f32) * D ** -0.5,
        'b_router_group': 0.01 * nrm(ks[13], (DEPTH, N_GROUPS), f32),
        'w_router_expert': nrm(ks[14], (DEPTH, D, N_EXPERTS), f32) * D ** -0.5,
        'b_router_expert': 0.01 * nrm(ks[15], (DEPTH, N_GROUPS, EXPERTS_PER_GROUP), f32),
        'w_gate': nrm(ks[16], (DEPTH, N_EXPERTS, D, D_FF_EXPERT), f32) * D ** -0.5,
        'w_up': nrm(ks[17], (DEPTH, N_EXPERTS, D, D_FF_EXPERT), f32) * D ** -0.5,
        'w_down': nrm(ks[18], (DEPTH, N_EXPERTS, D_FF_EXPERT, D), f32) * D_FF_EXPERT ** -0.5,
        'g_ple': 1.0 + 0.01 * nrm(ks[19], (DEPTH, D), f32),
        'w_ple_proj': nrm(ks[20], (DEPTH, PLE_DIM, D), f32) * PLE_DIM ** -0.5,
        'w_ple_gate': nrm(ks[21], (DEPTH, D, D), f32) * D ** -0.5,
        'g_final': 1.0 + 0.01 * nrm(ks[22], (D,), f32),
    }

def reference(x_prompt, x_sample, state_conv, state_ret, p_prompt, p_sample, g_mix, w_in, conv_w,
              ret_gn, w_o, g_ffn, w_router_group, b_router_group, w_router_expert, b_router_expert,
              w_gate, w_up, w_down, g_ple, w_ple_proj, w_ple_gate, g_final):
    log_gamma = jnp.log(1.0 - 2.0 ** (-5.0 - jnp.arange(RET_HEADS, dtype=jnp.float32)))
    bp, tp = x_prompt.shape[0], x_prompt.shape[1]
    bs, ts = x_sample.shape[0], x_sample.shape[1]
    pos_prompt = jnp.arange(tp, dtype=jnp.int32)
    pos_sample = PAST_LEN + jnp.arange(ts, dtype=jnp.int32)
    hp, hs = x_prompt, x_sample
    conv_p, ret_p, conv_s, ret_s = [], [], [], []
    for l in range(DEPTH):
        layer = (g_mix[l], w_in[l], conv_w[l], ret_gn[l], w_o[l], g_ffn[l],
                 w_router_group[l], b_router_group[l], w_router_expert[l], b_router_expert[l],
                 w_gate[l], w_up[l], w_down[l], g_ple[l], w_ple_proj[l], w_ple_gate[l])
        buf0 = jnp.zeros((bp, CONV_WIDTH - 1, CONV_DIM), x_prompt.dtype)
        st0 = jnp.zeros((bp, RET_HEADS, RET_DK, RET_DV), jnp.float32)
        hp, cb, rs = block(hp, p_prompt[l], buf0, st0, pos_prompt, log_gamma, *layer)
        hs, cbs, rss = block(hs, p_sample[l], state_conv[l], state_ret[l], pos_sample, log_gamma, *layer)
        conv_p.append(cb.astype(state_conv.dtype))
        ret_p.append(rs.astype(state_ret.dtype))
        conv_s.append(cbs.astype(state_conv.dtype))
        ret_s.append(rss.astype(state_ret.dtype))
    y_prompt = rmsnorm(hp, g_final)
    y_sample = rmsnorm(hs, g_final)
    new_conv_prompt = jnp.stack(conv_p, axis=0)
    new_ret_prompt = jnp.stack(ret_p, axis=0)
    new_conv_sample = jnp.stack(conv_s, axis=0)
    new_ret_sample = jnp.stack(ret_s, axis=0)
    return (y_prompt, y_sample, new_conv_prompt, new_ret_prompt, new_conv_sample, new_ret_sample)


_drawn_inputs = setup_inputs


def setup_inputs(seed=0):
    import zlib

    import numpy as np

    out = dict(_drawn_inputs(seed))
    spreads = {}
    factors = {'ret_gn': 5.629,
     'g_ffn': 3.086,
     'b_router_group': 7.672,
     'b_router_expert': 4.426,
     'g_ple': 8.0,
     'g_final': 5.586}
    for name, (base, spread) in spreads.items():
        noise = np.random.default_rng([zlib.crc32(name.encode()), seed]).standard_normal(out[name].shape)
        drawn = base * np.exp(spread * noise) if base else spread * noise
        out[name] = __import__('jax').numpy.asarray(drawn.astype(out[name].dtype))
    for name, factor in factors.items():
        out[name] = (out[name] * factor).astype(out[name].dtype)
    return out
```

```python
from contextlib import ExitStack

import numpy as np

import concourse.bass as bass
from concourse import mybir

F32 = mybir.dt.float32
F16 = mybir.dt.float16
I32 = mybir.dt.int32
ALU = mybir.AluOpType
ACT = mybir.ActivationFunctionType
AX = mybir.AxisListType

P = 128
D = 1024
KD = D // P
SEQ = 512
NB = 8
T = SEQ + NB
HALF = T // 2
TILES = [(t * P, min(P, T - t * P)) for t in range(5)]
NT = len(TILES)
PAST = 4096
H = 4
CC = 4
WIN_UNITS = 7
NG, EPG = 4, 8
NE = NG * EPG
NR = NG + NE
FF = 512
PLE = 256
EPS = 1e-6
ROWS = 64
OVER = 2 * T // ROWS
NTILE = NE + OVER
NOWHERE = 4096.0
RING = 6
UNIT = 4096
HEAD_UNITS = WIN_UNITS + 2 + 1
SCALE = float(P) ** -0.5


def job_list():
    jobs = [("buf", 0)] + [("x", t) for t in range(NT)]
    jobs += [("q", h) for h in range(H)] + [("k", h) for h in range(H)] + [("v", t) for t in range(NT)]
    for b in range(NB):
        jobs.append(("vb", b))
        if b % 2:
            jobs.append(("g", b // 2))
        if b:
            jobs.append(("so", b - 1))
    jobs.append(("so", NB - 1))
    conv = iter([(k, c) for c in range(CC) for k in ("gc", "hc", "gb")])
    for s in range(H + 3):
        if s < H:
            jobs += [("scA", s), ("scB", s), ("kt", s)]
        if 0 <= s - 1 < H:
            jobs += [("pv", s - 1), ("st", s - 1)]
        if 0 <= s - 2 < H:
            jobs.append(("mn", s - 2))
        if 0 <= s - 3 < H:
            jobs.append(("vr", s - 3))
        if s >= H:
            jobs += [next(conv) for _ in range(3)]
    jobs += list(conv)
    jobs.append(("co", 0))
    for t in range(NT + 1):
        if t < NT:
            jobs.append(("wo", t))
        if t >= 1:
            jobs.append(("xt", t - 1))
    jobs += [("rt", 0), ("lg", 0), ("lgs", 0), ("pt", 0), ("pt", 1), ("pp", 0), ("pp", 1), ("rk", 0), ("tot", 0),
             ("pp", 2), ("pp", 3), ("pp", 4), ("ix", 0)]
    return jobs


READERS = dict(buf="D", x="D", q="AD", k="AD", v="A", g="A", vb="D", so="D", scA="D", scB="D", kt="D", pv="A",
               st="A", mn="DA", vr="AD", gc="A", hc="D", gb="D", co="A", wo="DA", xt="A", rt="A", lg="D", lgs="D",
               pt="A", pp="A", rk="D", tot="D", ix="D", u="D", pg="AD")
JOBS = job_list()
TAIL = [("u", 0)]
for _t in range(NT):
    TAIL += ([("u", _t + 1)] if _t + 1 < NT else []) + [("pg", _t)]


class Plan:

    def __init__(self, jobs):
        self.jobs = jobs
        self.at = {j: n for n, j in enumerate(jobs)}

    def pe(self, job):
        return self.at[job] + 1

    def count(self, engine, n):
        return sum(engine in READERS[k] for k, _ in self.jobs[:n + 1])

    def done(self, engine, job):
        return self.count(engine, self.at[job])

    def free(self, n):
        return (self.jobs[n - 4], READERS[self.jobs[n - 4][0]]) if n >= 4 else (None, "")


HEAD, REST = Plan(JOBS), Plan(TAIL)
LAST_READER = [("q", 3), ("k", 3), ("v", 4), ("g", 3), ("gc", 3), ("hc", 3), ("gb", 3), ("wo", 4), ("wo", 4), ("pp", 4)]


def build(nc, a, o):
    y_rows = nc.dram_tensor("y_rows", [2 * T, D], F32, kind="Internal").ap()
    xn_rows = nc.dram_tensor("xn_rows", [T, D], F32, kind="Internal").ap()
    y_half = y_rows.rearrange("r (n c) -> (r n) c", n=2)
    xn_half = xn_rows.rearrange("r (n c) -> (r n) c", n=2)
    y_tok = y_rows.rearrange("(t k) c -> t (k c)", k=2)

    with ExitStack() as ctx:
        def sb(name, shape, dt=F32):
            return ctx.enter_context(nc.sbuf_tensor(name, shape, dt))

        def sem(name):
            return ctx.enter_context(nc.semaphore(name))

        ps = ctx.enter_context(nc.psum_tensor("ps", [P, 8, 512], F32))
        psf = ps[:, :, :].rearrange("p b c -> p (b c)")

        def pair(n):
            return psf[:, (n % 4) * 1024:(n % 4) * 1024 + 1024]

        def halves(ap):
            return ap.rearrange("p (b c) -> p b c", b=2)[:, :, 0:HALF]

        ring = sb("ring", [P, RING, UNIT])
        xh = sb("xh", [P, NT, D])
        region_u = sb("region_u", [P, KD * T])
        region_m = sb("region_m", [P, KD * T])
        region_q = sb("region_q", [P, 12 * T])
        region_v = sb("region_v", [P, NT * 512])
        region_z = sb("region_z", [P, 2128])
        cos_t = sb("cos_t", [P, T])
        sin_t = sb("sin_t", [P, T])
        region_d = sb("region_d", [P, H * SEQ])
        ident = sb("ident", [P, P])
        meanw = sb("meanw", [P, P])
        w_r = sb("w_r", [P, KD, NR])
        small = sb("small", [P, 256])
        stats = sb("stats", [P, 48])
        conv_hist = sb("conv_hist", [P, CC, NB, 2])
        new_z = sb("new_z", [P, CC, 10])
        wk = sb("wk", [P, NT, 2])
        index = sb("index", [P, 2 * NTILE], I32)
        over_expert = sb("over_expert", [1, OVER + 1], I32)
        gcol = sb("gcol", [P, 2], I32)
        scol = sb("scol", [P, 2], I32)

        cuts = dict(gmix=8, gple=8, convw=12, gn=4, kdec=16, gam=4, bias=36, desc4=4, desc8=8, thr=8, tokp=10,
                    valp=10, nh2=1, eps=1, io48=NTILE)
        at, col = 0, {}
        for name, width in cuts.items():
            col[name] = small[:, at:at + width]
            at += width
        assert at <= 256

        uT = region_u[:, :].rearrange("p (k t) -> p k t", k=KD)
        mixT = region_m[:, :].rearrange("p (k t) -> p k t", k=KD)
        qk = region_q[:, 0:8 * T].rearrange("p (h t) -> p h t", h=8)
        gT = region_q[:, 8 * T:12 * T].rearrange("p (h t) -> p h t", h=4)
        pp = region_q[:, 0:NT * D].rearrange("p (t c) -> p t c", t=NT)
        v_rows = region_v[:, :].rearrange("p (t c) -> p t c", t=NT)
        xs = [region_m[:, i * D:(i + 1) * D] for i in range(2)]
        junk = region_q[:, 0:D]
        buf_rows = region_v[0:16, 0:512]
        rot = [region_z[:, i * T:(i + 1) * T] for i in range(2)]
        state = [region_m[:, 4 * T + i * 512:4 * T + (i + 1) * 512] for i in range(4)]
        kv_tmp = region_z[:, 1280:1792]
        masked = [region_z[:, 0:1280], region_m[:, 0:1280]]
        kd = [region_z[:, 1280:1792], region_m[:, 1280:1792]]
        decay = region_d[:, :].rearrange("p (h r) -> p h r", h=H)
        gate_c = [region_z[:, i * T:(i + 1) * T] for i in range(2)]
        zc = [region_z[:, 1040 + i * 538:1040 + (i + 1) * 538] for i in range(2)]
        xn = [region_z[:, i * D:(i + 1) * D] for i in range(2)]
        g_ffn_b = region_d[:, 0:D]
        g_fin_b = region_d[:, D:2 * D]
        p_rows = region_v[:, 0:NT * PLE].rearrange("p (t c) -> p t c", t=NT)
        pT = region_v[:, NT * PLE:NT * PLE + 2 * T].rearrange("p (k t) -> p k t", k=2)
        st_out = cos_t[:, 0:512].rearrange("p (h e) -> p h e", h=H)
        co_out = sin_t[0:10, 0:512]

        cursor = [0]

        def scratch(n, dt=F32):
            words = n if dt == F32 else (n + 1) // 2
            ap = region_m[:, cursor[0]:cursor[0] + words]
            cursor[0] += words
            if dt != F32:
                ap = ap.bitcast(dt)
            return ap

        log_t = scratch(T)[0:NR, :]
        logit = scratch(NT * NR).rearrange("p (t c) -> p t c", t=NT)
        w4 = [scratch(NT * NG).rearrange("p (t c) -> p t c", t=NT) for _ in range(3)]
        w8 = [scratch(NT * EPG).rearrange("p (t c) -> p t c", t=NT) for _ in range(5)]
        w1 = [scratch(NT).rearrange("p (t c) -> p t c", t=NT) for _ in range(6)]
        w32 = scratch(NT * NE).rearrange("p (t c) -> p t c", t=NT)
        pick = [scratch(NT * NE).rearrange("p (t c) -> p t c", t=NT) for _ in range(2)]
        rank = scratch(NT * NE).rearrange("p (t c) -> p t c", t=NT)
        chosen = scratch(NT * NE, dt=F16).rearrange("p (t c) -> p t c", t=NT)
        total = scratch(NE)
        over8 = scratch(NE * 8).rearrange("p (e c) -> p e c", c=8)
        scan = [scratch(16 + NE) for _ in range(2)]
        over_n = scratch(NE)
        sel = [scratch(NT * 2).rearrange("p (t k) -> p t k", k=2) for _ in range(5)]
        sel8 = scratch(NT * 2 * 8).rearrange("p (n c) -> p n c", c=8)
        ovx = scratch(OVER * NE)[0:1, :].rearrange("p (n e) -> p n e", e=NE)
        ovc = scratch(OVER + 1)[0:1, :]
        row_hot = region_u[:, 1024:1664].bitcast(F16).rearrange("p (n c) -> p n c", c=P)
        tile_hot = region_u[:, 1664:2144].bitcast(F16).rearrange("p (n k c) -> p n k c", k=2, c=NTILE)
        ixf = [scratch(2 * NTILE) for _ in range(2)]
        io128 = scratch(P)
        io32 = scratch(NE)
        lt16 = scratch(2 * P, dt=F16).rearrange("p (s c) -> p s c", s=2)
        io16 = scratch(OVER)
        assert cursor[0] <= KD * T, cursor[0]

        moe = 0
        xg, xgT, hs, sg, hT = [], [], [], [], []
        for lst, width in ((xg, 512), (xgT, 512), (sg, 256), (hs, 256), (hT, 256)):
            for _ in range(2):
                lst.append(region_u[:, moe:moe + width])
                moe += width
        assert moe <= KD * T
        out_sb = [region_v[:, i * 512:(i + 1) * 512] for i in range(2)]

        y_buf = [region_v[:, 0:2048], region_m[:, 0:2048]]
        u3T = [region_u[:, i * D:(i + 1) * D] for i in range(2)]
        gate = [region_u[:, 2 * D + i * D:3 * D + i * D] for i in range(2)]
        xs3 = xn

        slot_filled = [sem(f"slot_filled{i}") for i in range(RING)]
        x_loaded = [sem(f"x_loaded{i}") for i in range(NT)]
        consts_loaded = sem("consts_loaded")
        decay_loaded = sem("decay_loaded")
        state_loaded = [sem(f"state_loaded{i}") for i in range(4)]
        state_scaled = sem("state_scaled")
        state_stored = [sem(f"state_stored{i}") for i in range(4)]
        late_loaded = sem("late_loaded")
        route_loaded = sem("route_loaded")
        xn_stored = [sem(f"xn_stored{i}") for i in range(2)]
        misc_stored = sem("misc_stored")
        root_done = sem("root_done")
        rstd_done = sem("rstd_done")
        xs_done = sem("xs_done")
        act_step = sem("act_step")
        dve_step = sem("dve_step")
        pool_step = sem("pool_step")
        pool_turn, sp_turn = sem("pool_turn"), sem("sp_turn")
        pe_jobs, act_jobs, dve_jobs = sem("pe_jobs"), sem("act_jobs"), sem("dve_jobs")
        half_copied = sem("half_copied")
        h_done = sem("h_done")
        lg_ready, ex_done = sem("lg_ready"), sem("ex_done")
        chosen_done, hot_done, index_done = sem("chosen_done"), sem("hot_done"), sem("index_done")
        xg_cleared = sem("xg_cleared")
        xg_loaded = [sem(f"xg_loaded{i}") for i in range(2)]
        out_stored = [sem(f"out_stored{i}") for i in range(2)]
        xt_done, xgT_ready, gu_done, silu_done = sem("xt_done"), sem("xgT_ready"), sem("gu_done"), sem("silu_done")
        hs_done, ht_done, hT_ready, down_done, out_ready = (
            sem("hs_done"), sem("ht_done"), sem("hT_ready"), sem("down_done"), sem("out_ready"))
        ov = {n: sem("over_" + n) for n in ("w", "xg", "xt", "xgT", "gu", "silu", "hs", "ht", "hT", "down", "out",
                                            "stored")}
        y_loaded = [sem(f"y_loaded{i}") for i in range(2)]
        hy_done, hy_sq, hy_root, hy_rstd, u_ready = (
            sem("hy_done"), sem("hy_sq"), sem("hy_root"), sem("hy_rstd"), sem("u_ready"))
        pe_tail, act_tail, dve_tail = sem("pe_tail"), sem("act_tail"), sem("dve_tail")
        f_done, f_sq, f_root, y_done, y_stored = (
            sem("f_done"), sem("f_sq"), sem("f_root"), sem("y_done"), sem("y_stored"))

        def unit(n):
            return ring[:, n % RING, :]

        def unit_wait(eng, n):
            eng.wait_ge(slot_filled[n % RING], 16 * (n // RING + 1))

        U_Q, U_K, U_V, U_G, U_GC, U_HC, U_GB, U_O, U_PP = 0, 1, 2, 3, 4, 5, 6, 7, 9
        U_GATE = HEAD_UNITS + 3 * NE

        block = ctx.enter_context(nc.Block())

        @block.sync
        def _(sp):
            for t, (r0, m) in enumerate(TILES[:2]):
                sp.dma_start(xh[0:m, t, :], a["x"][r0:r0 + m, :]).then_inc(x_loaded[t], 16)

            def head_unit(n):
                if n >= RING:
                    sp.wait_ge(pe_jobs, HEAD.pe(LAST_READER[n - RING]))
                if n < WIN_UNITS:
                    src, width = a["w_in"][n], UNIT
                elif n < WIN_UNITS + 2:
                    src, width = a["w_o"][n - WIN_UNITS], UNIT
                else:
                    src, width = a["w_ple_proj"], 2 * D
                sp.dma_start(unit(n)[:, 0:width], src).then_inc(slot_filled[n % RING], 16)

            head_unit(0)
            for t, (r0, m) in list(enumerate(TILES))[2:]:
                sp.dma_start(xh[0:m, t, :], a["x"][r0:r0 + m, :]).then_inc(x_loaded[t], 16)
            for n in range(1, HEAD_UNITS):
                head_unit(n)
            for j in range(6):
                n = HEAD_UNITS + j
                sp.wait_ge(pe_jobs, HEAD.pe(LAST_READER[n - RING]))
                sp.dma_start(unit(n), a["w_exp"][j]).then_inc(slot_filled[n % RING], 16)
            with sp.Fori(1, NE // 2) as i:
                for j in range(6):
                    n = HEAD_UNITS + j
                    sp.wait_ge(down_done if j % 3 == 2 else gu_done, i * 2 + (j // 3 - 1))
                    src = a["w_exp"][bass.ds(i * 6 + j, 1)].rearrange("a p c -> (a p) c")
                    sp.dma_start(unit(n), src).then_inc(slot_filled[n % RING], 16)
            for n in (U_GATE, U_GATE + 1):
                sp.wait_ge(gu_done, NE - 1)
                sp.dma_start(unit(n), a["w_ple_gate"][n - U_GATE]).then_inc(slot_filled[n % RING], 16)

            sp.wait_ge(index_done, 1)
            sp.wait_ge(down_done, NE)
            n_over = sp.value_load(over_expert[0:1, OVER:OVER + 1], min_val=0, max_val=OVER)
            with sp.If(n_over > 0):
                with sp.Fori(0, OVER) as q:
                    e = sp.value_load(over_expert[0:1, bass.ds(q, 1)], min_val=0, max_val=NE - 1)
                    for j in range(3):
                        src = a["w_exp"][bass.ds(e * 3 + j, 1)].rearrange("a p c -> (a p) c")
                        sp.dma_start(ring[:, j, :], src).then_inc(ov["w"], 16)
                    sp.wait_ge(ov["down"], q + 1)
                    sp.sem_inc(sp_turn, 1)
                sp.wait_ge(ov["stored"], 16 * OVER)
            with sp.Else():
                sp.wait_ge(index_done, 1)

            sp.wait_ge(out_stored[0], 16 * (NE // 2))
            sp.wait_ge(out_stored[1], 16 * (NE // 2))
            for t, (r0, m) in enumerate(TILES):
                if t >= 2:
                    sp.wait_ge(hy_done, t - 1)
                sp.dma_start(y_buf[t % 2][0:m, :], y_tok[r0:r0 + m, :]).then_inc(y_loaded[t % 2], 16)
            for t, (r0, m) in enumerate(TILES):
                sp.wait_ge(y_done, t + 1)
                sp.dma_start(o["y"][r0:r0 + m, :], xh[0:m, t, :]).then_inc(y_stored, 16)
            sp.wait_ge(y_stored, 16 * NT)
            sp.wait_ge(misc_stored, 16 * 4)
            for i in range(4):
                sp.wait_ge(state_stored[i], 32)

        @block.gpsimd
        def _(pool):
            def load_state(b):
                if b >= 4:
                    pool.wait_ge(state_stored[b % 4], 16 * (b // 4))
                    pool.wait_ge(pe_jobs, HEAD.pe(("so", b - 4)))
                pool.dma_start(state[b % 4].rearrange("p (h e) -> p h e", h=H), a["state_ret"][b].rearrange(
                    "h d e -> d h e")).then_inc(state_loaded[b % 4], 16)

            for b in range(4):
                load_state(b)
            gam = col["gam"].unsqueeze(2).to_broadcast([P, H, P])
            pool.wait_ge(consts_loaded, 16 * 5)
            for b in range(NB):
                s3 = state[b % 4].rearrange("p (h e) -> p h e", h=H)
                pool.wait_ge(state_loaded[b % 4], 16 * (b // 4 + 1))
                nc.gpsimd.tensor_tensor(s3, s3, gam, ALU.mult).then_inc(state_scaled, 1)
                if b >= 2:
                    c = b - 2
                    pool.wait_ge(dve_jobs, HEAD.done("D", ("vb", c)))
                    pool.dma_start(o["ret_s"][c].rearrange("h d e -> d h e"),
                                   state[c % 4].rearrange("p (h e) -> p h e", h=H)).then_inc(state_stored[c % 4], 16)
                if b >= 2 and b + 2 < NB:
                    load_state(b + 2)
            for c in (NB - 2, NB - 1):
                pool.wait_ge(dve_jobs, HEAD.done("D", ("vb", c)))
                pool.dma_start(o["ret_s"][c].rearrange("h d e -> d h e"),
                               state[c % 4].rearrange("p (h e) -> p h e", h=H)).then_inc(state_stored[c % 4], 16)

            pool.wait_ge(dve_jobs, HEAD.done("D", ("scB", H - 1)))
            pool.dma_start(g_ffn_b, a["g_ffn"].to_broadcast([P, D])).then_inc(late_loaded, 16)
            pool.dma_start(g_fin_b, a["g_final"].to_broadcast([P, D])).then_inc(late_loaded, 16)
            pool.wait_ge(pe_jobs, HEAD.pe(("st", H - 1)))
            pool.dma_start(p_rows[:, 0:4, :], a["p"][0:SEQ].rearrange("(t p) c -> p t c", p=P)).then_inc(late_loaded, 16)
            pool.dma_start(p_rows[0:NB, 4, :], a["p"][SEQ:T]).then_inc(late_loaded, 16)
            pool.wait_ge(act_jobs, HEAD.done("A", ("st", H - 1)))
            pool.dma_start(o["ret_p"].rearrange("h d e -> d h e"), st_out).then_inc(misc_stored, 16)
            pool.dma_start(o["conv_s"][:, 0, :], a["state_conv"][:, 1, :]).then_inc(misc_stored, 16)
            pool.wait_ge(act_jobs, HEAD.done("A", ("co", 0)))
            pool.dma_start(o["conv_p"], co_out[0:2, :]).then_inc(misc_stored, 16)
            pool.dma_start(o["conv_s"][:, 1, :], co_out[2:10, :]).then_inc(misc_stored, 16)
            for t, (r0, m) in enumerate(TILES):
                pool.wait_ge(dve_jobs, HEAD.done("D", ("wo", t)))
                pool.dma_start(xn_rows[r0:r0 + m, :], xn[t % 2][0:m, :]).then_inc(xn_stored[t % 2], 16)
            pool.wait_ge(pe_jobs, HEAD.pe(("wo", NT - 1)))
            for dst, name in ((io128, "io128"), (io32, "io32"), (io16, "io16"), (lt16, "lt16")):
                pool.dma_start(dst, a[name]).then_inc(route_loaded, 16)

            pool.wait_ge(pe_jobs, HEAD.pe(("rt", 0)))
            nc.gpsimd.memset(xg[0], 0.0).then_inc(xg_cleared, 1)
            nc.gpsimd.memset(xg[1], 0.0).then_inc(xg_cleared, 1)
            pool.wait_ge(xg_cleared, 2)
            pool.wait_ge(xn_stored[0], 16 * 3)
            pool.wait_ge(xn_stored[1], 16 * 2)
            pool.wait_ge(index_done, 1)

            steps = [0]

            def copied(ins):
                steps[0] += 1
                ins.then_inc(pool_step, 1)
                pool.wait_ge(pool_step, steps[0])

            def start_gather(b, loaded):
                pool.sem_inc(pool_turn, 1)
                pool.indirect_dma_start(out=xg[b], out_offset=None, in_=xn_half,
                                        in_offset=bass.IndirectOffsetOnAxis(ap=gcol[:, b:b + 1], axis=0),
                                        bounds_check=2 * T - 1, oob_is_err=False).then_inc(loaded, 16)

            def start_scatter(b, stored):
                pool.sem_inc(pool_turn, 1)
                pool.indirect_dma_start(out=y_half, out_offset=bass.IndirectOffsetOnAxis(ap=scol[:, b:b + 1], axis=0),
                                        in_=out_sb[b], in_offset=None,
                                        bounds_check=4 * T - 1, oob_is_err=False).then_inc(stored, 16)

            for b in range(2):
                copied(nc.gpsimd.tensor_copy(gcol[:, b:b + 1], index[:, b:b + 1]))
                start_gather(b, xg_loaded[b])

            def pair_of_experts(i, more):
                for b in range(2):
                    e = i * 2 + b
                    if more:
                        pool.wait_ge(xt_done, e + 1)
                        pool.wait_ge(xg_loaded[b], i * 16 + 16)
                        nc.gpsimd.tensor_copy(gcol[:, b:b + 1], index[:, bass.ds(e + 2, 1)]).then_inc(pool_step, 1)
                        pool.wait_ge(pool_step, e * 2 + 3)
                        start_gather(b, xg_loaded[b])
                    if not isinstance(i, int) or i > 0:
                        pool.wait_ge(out_stored[b], i * 16)
                    nc.gpsimd.tensor_copy(scol[:, b:b + 1], index[:, bass.ds(e + NTILE, 1)]).then_inc(pool_step, 1)
                    pool.wait_ge(pool_step, e * 2 + 4 if more else e + NE + 1)
                    pool.wait_ge(out_ready, e + 1)
                    start_scatter(b, out_stored[b])

            pair_of_experts(0, True)
            with pool.Fori(1, NE // 2 - 1) as i:
                pair_of_experts(i, True)
            pair_of_experts(NE // 2 - 1, False)
            base = 2 * NE

            n_over = pool.value_load(over_expert[0:1, OVER:OVER + 1], min_val=0, max_val=OVER)
            with pool.If(n_over > 0):
                pool.wait_ge(out_stored[0], 16 * (NE // 2))
                pool.wait_ge(xg_loaded[0], 16 * (NE // 2))
                with pool.Fori(0, OVER) as q:
                    nc.gpsimd.tensor_copy(gcol[:, 0:1], index[:, bass.ds(q + NE, 1)]).then_inc(pool_step, 1)
                    nc.gpsimd.tensor_copy(scol[:, 0:1], index[:, bass.ds(q + NE + NTILE, 1)]).then_inc(pool_step, 1)
                    pool.wait_ge(pool_step, q * 2 + (base + 2))
                    start_gather(0, ov["xg"])
                    pool.wait_ge(ov["out"], q + 1)
                    start_scatter(0, ov["stored"])
                    pool.wait_ge(ov["stored"], q * 16 + 16)
            with pool.Else():
                pool.wait_ge(index_done, 1)

        @block.scalar
        def _(act):
            act.dma_start(small[:, 0:a["small"].shape[1]], a["small"]).then_inc(consts_loaded, 16)
            act.dma_start(ident[:, :], a["ident"]).then_inc(consts_loaded, 16)
            act.dma_start(buf_rows, a["state_conv"].rearrange("b r c -> (b r) c")).then_inc(consts_loaded, 16)
            act.dma_start(cos_t[:, :], a["cos"]).then_inc(consts_loaded, 16)
            act.dma_start(sin_t[:, :], a["sin"]).then_inc(consts_loaded, 16)
            act.dma_start(region_d[:, :], a["decay"]).then_inc(decay_loaded, 16)
            act.dma_start(meanw[:, :], a["meanw"]).then_inc(decay_loaded, 16)
            act.dma_start(w_r[:, :, :], a["w_r"]).then_inc(decay_loaded, 16)

            steps = [0]

            def link(ins):
                steps[0] += 1
                ins.then_inc(act_step, 1)
                act.wait_ge(act_step, steps[0])

            eps = col["eps"]
            for t, (r0, m) in enumerate(TILES):
                act.wait_ge(x_loaded[t], 16)
                if t == 0:
                    act.wait_ge(consts_loaded, 16 * 5)
                    act.wait_ge(dve_step, 1)
                link(nc.scalar.activation(junk[0:m, :], xh[0:m, t, :], ACT.Square, accum_out=stats[0:m, t:t + 1]))
                nc.scalar.activation(stats[0:m, 5 + t:6 + t], stats[0:m, t:t + 1], ACT.Sqrt, scale=1.0 / D,
                                     bias=eps[0:m, :]).then_inc(root_done, 1)
                act.wait_ge(rstd_done, t + 1)
                if t >= 2:
                    act.wait_ge(pe_jobs, HEAD.pe(("x", t - 2)))
                nc.scalar.activation(xs[t % 2][0:m, :], xh[0:m, t, :], ACT.Copy,
                                     scale=stats[0:m, 10 + t:11 + t]).then_inc(xs_done, 1)

            done = 0
            for n, (kind, c) in enumerate(JOBS):
                if "A" not in READERS[kind]:
                    continue
                b = pair(n)
                if (kind, c) == ("pt", 0):
                    for s, w in ((1, w4[0]), (2, w8[0])):
                        act.wait_ge(lg_ready, s)
                        nc.scalar.activation(w, w, ACT.Exp).then_inc(ex_done, 1)
                act.wait_ge(pe_jobs, n + 1)
                if done:
                    act.wait_ge(act_jobs, done)
                done += 1
                if kind in "qk":
                    turn = c if kind == "q" else H + c
                    if turn >= 2:
                        prev = ("q", turn - 2) if turn - 2 < H else ("k", turn - 2 - H)
                        act.wait_ge(dve_jobs, HEAD.done("D", prev))
                    r = rot[turn % 2].rearrange("p (b c) -> p b c", b=2)
                    nc.scalar.activation(r[0:64], halves(b)[64:128], ACT.Copy).then_inc(half_copied, 1)
                    nc.scalar.activation(r[64:128], halves(b)[0:64], ACT.Copy).then_inc(act_jobs, 1)
                elif kind == "v":
                    m = TILES[c][1]
                    if c == 0:
                        act.wait_ge(pe_jobs, HEAD.pe(("buf", 0)))
                    nc.scalar.activation(v_rows[0:m, c, :], b[0:m, 0:512], ACT.Copy).then_inc(act_jobs, 1)
                elif kind == "g":
                    nc.scalar.activation(gT[:, c, :].rearrange("p (b c) -> p b c", b=2), halves(b),
                                         ACT.Silu).then_inc(act_jobs, 1)
                elif kind == "pv":
                    act.wait_ge(dve_jobs, HEAD.done("D", ("so", NB - 1)))
                    nc.scalar.activation(qk[:, c, 0:SEQ], b[:, 0:SEQ], ACT.Copy).then_inc(act_jobs, 1)
                elif kind == "st":
                    act.wait_ge(dve_jobs, HEAD.done("D", ("k", H - 1)))
                    nc.scalar.activation(st_out[:, c, :], b[:, 0:P], ACT.Copy).then_inc(act_jobs, 1)
                elif kind == "mn":
                    act.wait_ge(dve_jobs, HEAD.done("D", ("mn", c)))
                    nc.scalar.activation(qk[:, H + c, :], qk[:, c, :], ACT.Square).then_inc(act_jobs, 1)
                elif kind == "vr":
                    nc.scalar.activation(qk[:, H + c, :].rearrange("p (b c) -> p b c", b=2), halves(b), ACT.Sqrt,
                                         bias=eps).then_inc(act_jobs, 1)
                elif kind == "gc":
                    if c >= 2:
                        act.wait_ge(dve_jobs, HEAD.done("D", ("hc", c - 2)))
                    nc.scalar.activation(gate_c[c % 2].rearrange("p (b c) -> p b c", b=2), halves(b),
                                         ACT.Copy).then_inc(act_jobs, 1)
                elif kind == "co":
                    nc.scalar.activation(co_out, b[0:10, 0:512], ACT.Copy).then_inc(act_jobs, 1)
                elif kind == "wo":
                    m = TILES[c][1]
                    act.wait_ge(h_done, c + 1)
                    link(nc.scalar.activation(junk[0:m, :], xh[0:m, c, :], ACT.Square,
                                              accum_out=stats[0:m, 15 + c:16 + c]))
                    nc.scalar.activation(stats[0:m, 20 + c:21 + c], stats[0:m, 15 + c:16 + c], ACT.Sqrt,
                                         scale=1.0 / D, bias=eps[0:m, :]).then_inc(act_jobs, 1)
                elif kind == "xt":
                    r0, m = TILES[c]
                    nc.scalar.activation(uT[:, :, r0:r0 + m], b.rearrange("p (k t) -> p k t", k=KD)[:, :, 0:m],
                                         ACT.Copy).then_inc(act_jobs, 1)
                elif kind == "rt":
                    nc.scalar.activation(log_t.rearrange("p (b c) -> p b c", b=2), halves(b)[0:NR],
                                         ACT.Copy).then_inc(act_jobs, 1)
                elif kind == "pt":
                    if c == 0:
                        nc.scalar.activation(pT[:, :, 0:SEQ], b.rearrange("p (k t) -> p k t", k=2),
                                             ACT.Copy).then_inc(act_jobs, 1)
                    else:
                        nc.scalar.activation(pT[:, :, SEQ:T], b[:, 0:2 * NB].rearrange("p (k t) -> p k t", k=2),
                                             ACT.Copy).then_inc(act_jobs, 1)
                elif kind == "pp":
                    m = TILES[c][1]
                    nc.scalar.activation(pp[0:m, c, :], b[0:m, :], ACT.Copy).then_inc(act_jobs, 1)

            def evac_rows(b, count, t_done, out_sem):
                act.wait_ge(t_done, count)
                nc.scalar.activation(xgT[b], ps[:, b, :], ACT.Copy).then_inc(out_sem, 1)

            def silu(b, count, g_sem, out_sem):
                act.wait_ge(g_sem, count)
                nc.scalar.activation(sg[b], ps[:, 2 + b, 0:256], ACT.Silu).then_inc(out_sem, 1)

            def evac_out(b, count, d_sem, out_sem):
                act.wait_ge(d_sem, count)
                nc.scalar.activation(out_sb[b], ps[:, 6 + b, :], ACT.Copy).then_inc(out_sem, 1)

            def pair_of_experts(i, first, last):
                for b in range(2):
                    e = i * 2 + b
                    if not (last and b == 1):
                        evac_rows(1 - b, e + 2, xt_done, xgT_ready)
                    silu(b, e + 1, gu_done, silu_done)
                    if not first:
                        act.wait_ge(out_stored[b], i * 16)
                    evac_out(b, e + 1, down_done, out_ready)

            evac_rows(0, 1, xt_done, xgT_ready)
            pair_of_experts(0, True, False)
            with act.Fori(1, NE // 2 - 1) as i:
                pair_of_experts(i, False, False)
            pair_of_experts(NE // 2 - 1, False, True)

            n_over = act.value_load(over_expert[0:1, OVER:OVER + 1], min_val=0, max_val=OVER)
            with act.If(n_over > 0):
                act.wait_ge(out_stored[0], 16 * (NE // 2))
                with act.Fori(0, OVER) as q:
                    evac_rows(0, q + 1, ov["xt"], ov["xgT"])
                    silu(0, q + 1, ov["gu"], ov["silu"])
                    evac_out(0, q + 1, ov["down"], ov["out"])
            with act.Else():
                act.wait_ge(index_done, 1)

            act.wait_ge(out_ready, NE)

            def row_norm(t):
                m = TILES[t][1]
                act.wait_ge(hy_done, t + 1)
                if t:
                    act.wait_ge(hy_sq, t)
                nc.scalar.activation(xs3[t % 2][0:m, :], xh[0:m, t, :], ACT.Square,
                                     accum_out=stats[0:m, 25 + t:26 + t]).then_inc(hy_sq, 1)
                act.wait_ge(hy_sq, t + 1)
                nc.scalar.activation(stats[0:m, 30 + t:31 + t], stats[0:m, 25 + t:26 + t], ACT.Sqrt, scale=1.0 / D,
                                     bias=eps[0:m, :]).then_inc(hy_root, 1)
                act.wait_ge(hy_rstd, t + 1)
                nc.scalar.activation(xs3[t % 2][0:m, :], xh[0:m, t, :], ACT.Copy,
                                     scale=stats[0:m, 35 + t:36 + t]).then_inc(u_ready, 1)

            row_norm(0)
            for n, (kind, t) in enumerate(TAIL):
                if kind != "pg":
                    if t + 1 < NT:
                        if t:
                            act.wait_ge(pe_tail, REST.pe(("u", t - 1)))
                        row_norm(t + 1)
                    continue
                m = TILES[t][1]
                act.wait_ge(pe_tail, n + 1)
                if t >= 2:
                    act.wait_ge(f_done, t - 1)
                nc.scalar.activation(gate[t % 2][0:m, :], pair(n)[0:m, :], ACT.Sigmoid).then_inc(act_tail, 1)
                act.wait_ge(f_done, t + 1)
                link(nc.scalar.activation(gate[t % 2][0:m, :], xh[0:m, t, :], ACT.Square,
                                          accum_out=stats[0:m, t:t + 1]))
                nc.scalar.activation(stats[0:m, 5 + t:6 + t], stats[0:m, t:t + 1], ACT.Sqrt, scale=1.0 / D,
                                     bias=eps[0:m, :]).then_inc(f_root, 1)

        @block.vector
        def _(dve):
            steps = [0]

            def link(ins):
                steps[0] += 1
                ins.then_inc(dve_step, 1)
                dve.wait_ge(dve_step, steps[0])

            V = nc.vector
            link(V.memset(stats[:, :], 1.0))

            def wide(ap, shape):
                return ap.unsqueeze(2).to_broadcast(shape)

            def route_choose():
                lgt, bias = logit, col["bias"].unsqueeze(1).to_broadcast([P, NT, NR])
                link(V.tensor_tensor(lgt, lgt, bias, ALU.add))
                lg4 = lgt[:, :, 0:NG]
                link(V.tensor_reduce(w1[0], lg4, AX.X, ALU.max))
                V.tensor_tensor(w4[0], lg4, w1[0].to_broadcast([P, NT, NG]), ALU.subtract).then_inc(lg_ready, 1)
                d4 = col["desc4"].unsqueeze(1).to_broadcast([P, NT, NG])
                link(V.tensor_tensor(w4[1], lg4, w1[0].to_broadcast([P, NT, NG]), ALU.is_equal))
                link(V.tensor_tensor(w4[1], w4[1], d4, ALU.mult))
                link(V.tensor_reduce(w1[1], w4[1], AX.X, ALU.max))
                link(V.tensor_tensor(w4[1], w4[1], w1[1].to_broadcast([P, NT, NG]), ALU.is_equal))
                lg8 = lgt[:, :, NG:NR].rearrange("p t (g e) -> p t g e", g=NG)
                hot_g = w4[1].unsqueeze(3).to_broadcast([P, NT, NG, EPG])
                w32v = w32.rearrange("p t (g e) -> p t g e", g=NG)
                link(V.tensor_tensor(w32v, lg8, hot_g, ALU.mult))
                link(V.tensor_tensor(w8[0], w32[:, :, 0:8], w32[:, :, 8:16], ALU.add))
                link(V.tensor_tensor(w8[1], w32[:, :, 16:24], w32[:, :, 24:32], ALU.add))
                link(V.tensor_tensor(w8[0], w8[0], w8[1], ALU.add))
                link(V.tensor_reduce(w1[2], w8[0], AX.X, ALU.max))
                V.tensor_tensor(w8[0], w8[0], w1[2].to_broadcast([P, NT, EPG]), ALU.subtract).then_inc(lg_ready, 1)
                dve.wait_ge(ex_done, 2)
                link(V.tensor_reduce(w1[3], w4[0], AX.X, ALU.add))
                link(V.reciprocal(w1[3], w1[3]))
                link(V.tensor_reduce(w1[4], w8[0], AX.X, ALU.add))
                link(V.reciprocal(w1[4], w1[4]))
                link(V.tensor_tensor(w8[0], w8[0], w1[4].to_broadcast([P, NT, EPG]), ALU.mult))
                d8 = col["desc8"].unsqueeze(1).to_broadcast([P, NT, EPG])

                def first_largest(src, top, hot):
                    link(V.tensor_reduce(top, src, AX.X, ALU.max))
                    link(V.tensor_tensor(hot, src, top.to_broadcast([P, NT, EPG]), ALU.is_equal))
                    link(V.tensor_tensor(hot, hot, d8, ALU.mult))
                    link(V.tensor_reduce(w1[1], hot, AX.X, ALU.max))
                    link(V.tensor_tensor(hot, hot, w1[1].to_broadcast([P, NT, EPG]), ALU.is_equal))

                first_largest(w8[0], w1[0], w8[1])
                link(V.scalar_tensor_tensor(w8[3], w8[1], -2.0, w8[0], ALU.mult, ALU.add))
                first_largest(w8[3], w1[2], w8[2])
                link(V.tensor_tensor(w1[4], w1[0], w1[2], ALU.add))
                link(V.reciprocal(w1[4], w1[4]))
                link(V.tensor_tensor(w1[4], w1[4], w1[3], ALU.mult))
                link(V.tensor_tensor(wk[:, :, 0:1], w1[0], w1[4], ALU.mult))
                link(V.tensor_tensor(wk[:, :, 1:2], w1[2], w1[4], ALU.mult))
                for k in range(2):
                    hot_e = w8[1 + k].unsqueeze(2).to_broadcast([P, NT, NG, EPG])
                    link(V.tensor_tensor(pick[k].rearrange("p t (g e) -> p t g e", g=NG), hot_g, hot_e, ALU.mult))
                link(V.memset(w32, 0.0))
                link(V.tensor_tensor(w32[:, 0:4, :], pick[0][:, 0:4, :], pick[1][:, 0:4, :], ALU.add))
                link(V.tensor_tensor(w32[0:NB, 4, :], pick[0][0:NB, 4, :], pick[1][0:NB, 4, :], ALU.add))
                V.tensor_copy(chosen, w32).then_inc(chosen_done, 1)
                dve.wait_ge(chosen_done, 1)

            def route_places():
                tv = total.unsqueeze(2).to_broadcast([P, NE, 8])
                thr = col["thr"].unsqueeze(1).to_broadcast([P, NE, 8])
                link(V.tensor_tensor(over8, tv, thr, ALU.is_gt))
                link(V.tensor_reduce(over_n.unsqueeze(2), over8, AX.X, ALU.add))
                link(V.memset(scan[0][:, 0:16], 0.0))
                link(V.memset(scan[1][:, 0:16], 0.0))
                link(V.tensor_copy(scan[0][:, 16:16 + NE], over_n))
                src, dst = 0, 1
                for s in (1, 2, 4, 8, 16):
                    link(V.tensor_tensor(scan[dst][:, 16:16 + NE], scan[src][:, 16:16 + NE],
                                         scan[src][:, 16 - s:16 + NE - s], ALU.add))
                    src, dst = dst, src
                incl = scan[src][:, 16:16 + NE]
                link(V.tensor_tensor(ovx, incl[0:1, :].unsqueeze(1).to_broadcast([1, OVER, NE]),
                                     io16[0:1, :].unsqueeze(2).to_broadcast([1, OVER, NE]), ALU.is_le))
                link(V.tensor_reduce(ovc[:, 0:OVER].unsqueeze(2), ovx, AX.X, ALU.add))
                link(V.tensor_scalar(ovc[:, 0:OVER], ovc[:, 0:OVER], float(NE - 1), None, ALU.min))
                link(V.tensor_copy(ovc[:, OVER:OVER + 1], incl[0:1, NE - 1:NE]))
                link(V.tensor_copy(over_expert[:, :], ovc))
                excl = scan[dst][:, 0:NE]
                link(V.tensor_tensor(excl, incl, over_n, ALU.subtract))
                tables = (rank, io32.unsqueeze(1).to_broadcast([P, NT, NE]), excl.unsqueeze(1).to_broadcast([P, NT, NE]))
                for k in range(2):
                    for s, table in enumerate(tables):
                        link(V.tensor_tensor(w32, pick[k], table, ALU.mult))
                        link(V.tensor_reduce(sel[s][:, :, k:k + 1], w32, AX.X, ALU.add))
                flat = [x.rearrange("p t k -> p (t k)") for x in sel]
                tenth = [P, NT * 2, 8]
                link(V.tensor_tensor(sel8, flat[0].unsqueeze(2).to_broadcast(tenth),
                                     col["thr"].unsqueeze(1).to_broadcast(tenth), ALU.is_ge))
                link(V.tensor_reduce(flat[3].unsqueeze(2), sel8, AX.X, ALU.add))
                link(V.scalar_tensor_tensor(flat[0], flat[3], -float(ROWS), flat[0], ALU.mult, ALU.add))
                link(V.scalar_tensor_tensor(flat[2], flat[3], float(NE - 1), flat[2], ALU.add, ALU.add))
                link(V.tensor_tensor(flat[2], flat[2], flat[1], ALU.subtract))
                link(V.tensor_scalar(flat[4], flat[3], 0.0, None, ALU.is_gt))
                link(V.tensor_tensor(flat[2], flat[2], flat[4], ALU.mult))
                link(V.tensor_tensor(flat[2], flat[2], flat[1], ALU.add))
                n10 = NT * 2
                link(V.tensor_tensor(row_hot, flat[0].unsqueeze(2).to_broadcast([P, n10, P]),
                                     io128.unsqueeze(1).to_broadcast([P, n10, P]), ALU.is_equal))
                for k, name in enumerate(("tokp", "valp")):
                    hot = tile_hot[:, :, k, :]
                    link(V.tensor_tensor(hot, flat[2].unsqueeze(2).to_broadcast([P, n10, NTILE]),
                                         col["io48"].unsqueeze(1).to_broadcast([P, n10, NTILE]), ALU.is_equal))
                    ins = V.tensor_tensor(hot, hot, col[name].unsqueeze(2).to_broadcast([P, n10, NTILE]), ALU.mult)
                    if k == 0:
                        link(ins)
                ins.then_inc(hot_done, 1)
                dve.wait_ge(hot_done, 1)

            dve.wait_ge(consts_loaded, 16 * 5)
            for t in range(NT):
                dve.wait_ge(root_done, t + 1)
                m = TILES[t][1]
                V.reciprocal(stats[0:m, 10 + t:11 + t], stats[0:m, 5 + t:6 + t]).then_inc(rstd_done, 1)

            done = 0
            for n, (kind, c) in enumerate(JOBS):
                if "D" not in READERS[kind]:
                    continue
                b = pair(n)
                dve.wait_ge(pe_jobs, n + 1)
                if done:
                    dve.wait_ge(dve_jobs, done)
                done += 1
                if kind == "buf":
                    V.tensor_copy(conv_hist[:, :, :, :].rearrange("p c b r -> p c (b r)"),
                                  b[:, 0:CC * 16].rearrange("p (c n) -> p c n", c=CC)).then_inc(dve_jobs, 1)
                elif kind == "x":
                    r0, m = TILES[c]
                    V.tensor_tensor(uT[:, :, r0:r0 + m], b.rearrange("p (k t) -> p k t", k=KD)[:, :, 0:m],
                                    wide(col["gmix"], [P, KD, m]), ALU.mult).then_inc(dve_jobs, 1)
                elif kind in "qk":
                    turn = c if kind == "q" else H + c
                    r, dst = rot[turn % 2], qk[:, turn, :]
                    two = "p (b c) -> p b c"
                    if turn == 0:
                        dve.wait_ge(xs_done, NT)
                    dve.wait_ge(act_jobs, HEAD.done("A", (kind, c)))
                    dve.wait_ge(half_copied, turn + 1)
                    link(V.tensor_tensor(dst.rearrange(two, b=2), halves(b), cos_t[:, :].rearrange(two, b=2), ALU.mult))
                    link(V.tensor_tensor(r, r, sin_t[:, :], ALU.mult))
                    V.tensor_tensor(dst, dst, r, ALU.add).then_inc(dve_jobs, 1)
                elif kind == "vb":
                    s3 = state[c % 4].rearrange("p (h e) -> p h e", h=H)
                    kv = kv_tmp.rearrange("p (h e) -> p h e", h=H)
                    kcol = qk[:, H:2 * H, SEQ + c:SEQ + c + 1].to_broadcast([P, H, P])
                    link(V.tensor_tensor(kv, b[:, 0:512].rearrange("p (h e) -> p h e", h=H), kcol, ALU.mult))
                    dve.wait_ge(state_scaled, c + 1)
                    V.scalar_tensor_tensor(state[c % 4], kv_tmp, SCALE, state[c % 4], ALU.mult,
                                           ALU.add).then_inc(dve_jobs, 1)
                elif kind == "so":
                    V.tensor_copy(qk[:, 0:H, SEQ + c:SEQ + c + 1], b[:, 0:H].unsqueeze(2)).then_inc(dve_jobs, 1)
                elif kind in ("scA", "scB"):
                    if (kind, c) == ("scA", 0):
                        dve.wait_ge(decay_loaded, 16 * 3)
                    dst = masked[c % 2]
                    if kind == "scA":
                        link(V.tensor_tensor(dst[:, 0:512], b[:, 0:512], decay[:, c, 0:512], ALU.mult))
                        V.tensor_tensor(dst[:, 512:896], b[:, 512:896], decay[:, c, 0:384],
                                        ALU.mult).then_inc(dve_jobs, 1)
                    else:
                        link(V.tensor_tensor(dst[:, 896:1152], b[:, 0:256], decay[:, c, 0:256], ALU.mult))
                        V.tensor_tensor(dst[:, 1152:1280], b[:, 512:640], decay[:, c, 0:128],
                                        ALU.mult).then_inc(dve_jobs, 1)
                elif kind == "kt":
                    V.tensor_tensor(kd[c % 2].rearrange("p (t d) -> p t d", t=4),
                                    b[:, 0:512].rearrange("p (t d) -> p t d", t=4),
                                    wide(col["kdec"][:, 4 * c:4 * c + 4], [P, 4, P]), ALU.mult).then_inc(dve_jobs, 1)
                elif kind == "mn":
                    o3 = qk[:, c, :].rearrange("p (b c) -> p b c", b=2)
                    V.tensor_tensor(o3, o3, halves(b), ALU.subtract).then_inc(dve_jobs, 1)
                elif kind == "vr":
                    r = qk[:, H + c, :]
                    dve.wait_ge(act_jobs, HEAD.done("A", ("vr", c)))
                    if c == 0:
                        for i in range(4):
                            dve.wait_ge(state_stored[i], 32)
                    link(V.reciprocal(r, r))
                    link(V.tensor_tensor(r, r, qk[:, c, :], ALU.mult))
                    V.scalar_tensor_tensor(mixT[:, CC + c, :], r, col["gn"][:, c:c + 1], gT[:, c, :], ALU.mult,
                                           ALU.mult).then_inc(dve_jobs, 1)
                elif kind == "hc":
                    z = zc[c % 2]
                    zs = z[:, 514:538].rearrange("p (b r) -> p b r", r=3)
                    link(V.memset(z[:, 0:2], 0.0))
                    link(V.tensor_copy(zs[:, :, 0:2], conv_hist[:, c, :, :]))
                    dve.wait_ge(act_jobs, HEAD.done("A", ("gc", c)))
                    g = gate_c[c % 2]
                    link(V.tensor_tensor(z[:, 2:262], b[:, 0:260], g[:, 0:260], ALU.mult))
                    link(V.tensor_tensor(z[:, 262:514], b[:, 512:764], g[:, 260:512], ALU.mult))
                    link(V.tensor_tensor(zs[:, :, 2:3], b[:, 764:772].unsqueeze(2), g[:, 512:520].unsqueeze(2),
                                         ALU.mult))
                    link(V.tensor_copy(new_z[:, c, 0:2], z[:, 512:514]))
                    V.tensor_copy(new_z[:, c, 2:10].unsqueeze(2), zs[:, :, 2:3]).then_inc(dve_jobs, 1)
                elif kind == "gb":
                    z, y = zc[c % 2], mixT[:, c, :]
                    zs = z[:, 514:538].rearrange("p (b r) -> p b r", r=3)
                    ys = y[:, SEQ:T].unsqueeze(2)
                    w = col["convw"][:, 3 * c:3 * c + 3]
                    link(V.tensor_scalar(y[:, 0:SEQ], z[:, 0:SEQ], w[:, 0:1], None, ALU.mult))
                    link(V.tensor_scalar(ys, zs[:, :, 0:1], w[:, 0:1], None, ALU.mult))
                    for r in (1, 2):
                        link(V.scalar_tensor_tensor(y[:, 0:SEQ], z[:, r:r + SEQ], w[:, r:r + 1], y[:, 0:SEQ],
                                                    ALU.mult, ALU.add))
                        link(V.scalar_tensor_tensor(ys, zs[:, :, r:r + 1], w[:, r:r + 1], ys, ALU.mult, ALU.add))
                    V.tensor_tensor(y.rearrange("p (b c) -> p b c", b=2), y.rearrange("p (b c) -> p b c", b=2),
                                    halves(b), ALU.mult).then_inc(dve_jobs, 1)
                elif kind == "wo":
                    m = TILES[c][1]
                    V.tensor_tensor(xh[0:m, c, :], xh[0:m, c, :], b[0:m, :], ALU.add).then_inc(h_done, 1)
                    dve.wait_ge(act_jobs, HEAD.done("A", ("wo", c)))
                    link(V.reciprocal(stats[0:m, 10 + c:11 + c], stats[0:m, 20 + c:21 + c]))
                    if c == 0:
                        dve.wait_ge(late_loaded, 16 * 4)
                    if c >= 2:
                        dve.wait_ge(pe_jobs, HEAD.pe(("xt", c - 2)))
                        dve.wait_ge(xn_stored[c % 2], 16 * (c // 2))
                    dve.wait_ge(h_done, c + 1)
                    V.scalar_tensor_tensor(xn[c % 2][0:m, :], xh[0:m, c, :], stats[0:m, 10 + c:11 + c],
                                           g_ffn_b[0:m, :], ALU.mult, ALU.mult).then_inc(dve_jobs, 1)
                elif kind == "lg":
                    dve.wait_ge(route_loaded, 16 * 4)
                    link(V.memset(logit, 0.0))
                    V.tensor_copy(logit[:, 0:4, :], b[:, 0:4 * NR].rearrange("p (t c) -> p t c", t=4)).then_inc(dve_jobs, 1)
                elif kind == "lgs":
                    V.tensor_copy(logit[0:NB, 4, :], b[0:NB, 0:NR]).then_inc(dve_jobs, 1)
                    dve.wait_ge(dve_jobs, done)
                    route_choose()
                elif kind == "rk":
                    V.tensor_copy(rank, b[:, 0:NT * NE].rearrange("p (t c) -> p t c", t=NT)).then_inc(dve_jobs, 1)
                elif kind == "tot":
                    V.tensor_copy(total, b[:, 0:NE]).then_inc(dve_jobs, 1)
                    dve.wait_ge(dve_jobs, done)
                    route_places()
                elif kind == "ix":
                    V.tensor_copy(ixf[0], b[:, 0:2 * NTILE]).then_inc(dve_jobs, 1)
                    dve.wait_ge(dve_jobs, done)
                    link(V.tensor_scalar(ixf[1], ixf[0], 0.0, NOWHERE, ALU.is_equal, ALU.mult))
                    link(V.tensor_scalar(ixf[0], ixf[0], 2.0, col["nh2"], ALU.mult, ALU.add))
                    link(V.tensor_tensor(ixf[0], ixf[0], ixf[1], ALU.add))
                    V.tensor_copy(index[:, :], ixf[0]).then_inc(index_done, 1)

            def mult_up(b, count, s_sem, out_sem):
                dve.wait_ge(s_sem, count)
                V.tensor_tensor(hs[b], sg[b], ps[:, 2 + b, 256:512], ALU.mult).then_inc(out_sem, 1)

            def evac_h(b, count, t_sem, out_sem):
                dve.wait_ge(t_sem, count)
                V.tensor_copy(hT[b], ps[:, 4 + b, 0:256]).then_inc(out_sem, 1)

            with dve.Fori(0, NE // 2) as i:
                for b in range(2):
                    e = i * 2 + b
                    mult_up(b, e + 1, silu_done, hs_done)
                    evac_h(b, e + 1, ht_done, hT_ready)

            n_over = dve.value_load(over_expert[0:1, OVER:OVER + 1], min_val=0, max_val=OVER)
            with dve.If(n_over > 0):
                with dve.Fori(0, OVER) as q:
                    mult_up(0, q + 1, ov["silu"], ov["hs"])
                    evac_h(0, q + 1, ov["ht"], ov["hT"])
            with dve.Else():
                dve.wait_ge(index_done, 1)

            def combine(t):
                m = TILES[t][1]
                dve.wait_ge(y_loaded[t % 2], 16 * (t // 2 + 1))
                yb, h = y_buf[t % 2], xh[0:m, t, :]
                link(V.scalar_tensor_tensor(h, yb[0:m, 0:D], wk[0:m, t, 0:1], h, ALU.mult, ALU.add))
                V.scalar_tensor_tensor(h, yb[0:m, D:2 * D], wk[0:m, t, 1:2], h, ALU.mult, ALU.add).then_inc(hy_done, 1)
                dve.wait_ge(hy_root, t + 1)
                V.reciprocal(stats[0:m, 35 + t:36 + t], stats[0:m, 30 + t:31 + t]).then_inc(hy_rstd, 1)

            combine(0)
            evicted = 0
            for n, (kind, t) in enumerate(TAIL):
                m = TILES[t][1]
                if kind == "u":
                    if t + 1 < NT:
                        combine(t + 1)
                    dve.wait_ge(pe_tail, n + 1)
                    if t >= 2:
                        dve.wait_ge(pe_tail, REST.pe(("pg", t - 2)))
                    V.tensor_tensor(u3T[t % 2].rearrange("p (k t) -> p k t", k=KD)[:, :, 0:m],
                                    pair(n).rearrange("p (k t) -> p k t", k=KD)[:, :, 0:m],
                                    wide(col["gple"], [P, KD, m]), ALU.mult).then_inc(dve_tail, 1)
                else:
                    h = xh[0:m, t, :]
                    dve.wait_ge(act_tail, t + 1)
                    dve.wait_ge(hy_done, t + 1)
                    link(V.tensor_tensor(pp[0:m, t, :], pp[0:m, t, :], gate[t % 2][0:m, :], ALU.mult))
                    V.tensor_tensor(h, h, pp[0:m, t, :], ALU.add).then_inc(f_done, 1)
                    dve.wait_ge(f_root, t + 1)
                    link(V.reciprocal(stats[0:m, 10 + t:11 + t], stats[0:m, 5 + t:6 + t]))
                    dve.wait_ge(f_done, t + 1)
                    V.scalar_tensor_tensor(h, h, stats[0:m, 10 + t:11 + t], g_fin_b[0:m, :], ALU.mult,
                                           ALU.mult).then_inc(y_done, 1)

        @block.tensor
        def _(pe):
            mm, tr = nc.tensor.matmul, nc.tensor.transpose

            def over_tokens(out, w_of, src, ks, m=P):
                for half in range(2):
                    for k in range(ks):
                        last = mm(halves(out)[0:m, half, :], w_of(k), src(k, half * HALF), start=(k == 0), stop=(k == ks - 1))
                return last

            def u_cols(k, c0):
                return uT[:, k, c0:c0 + HALF]

            pe.wait_ge(consts_loaded, 16 * 5)
            for n, (kind, c) in enumerate(JOBS):
                b = pair(n)
                prev, readers = HEAD.free(n)
                if "A" in readers:
                    pe.wait_ge(act_jobs, HEAD.done("A", prev))
                if "D" in readers:
                    pe.wait_ge(dve_jobs, HEAD.done("D", prev))

                def after(engine, job):
                    pe.wait_ge(act_jobs if engine == "A" else dve_jobs, HEAD.done(engine, job))

                if kind == "buf":
                    for k in range(CC):
                        last = tr(b[:, 16 * k:16 * k + 16], buf_rows[:, k * P:(k + 1) * P], ident[0:16, 0:16])
                elif kind == "x":
                    m = TILES[c][1]
                    pe.wait_ge(xs_done, c + 1)
                    for k in range(KD):
                        last = tr(b[:, k * P:k * P + m], xs[c % 2][0:m, k * P:(k + 1) * P], ident[0:m, 0:m])
                elif kind in ("q", "k", "g", "gc", "hc", "gb"):
                    u = dict(q=U_Q, k=U_K, g=U_G, gc=U_GC, hc=U_HC, gb=U_GB)[kind]
                    if (kind, c) == ("q", 0):
                        after("D", ("x", NT - 1))
                    unit_wait(pe, u)
                    w = unit(u).rearrange("p (k c) -> p k c", k=KD)
                    last = over_tokens(b, lambda k: w[:, k, c * P:(c + 1) * P], u_cols, KD)
                elif kind == "v":
                    r0, m = TILES[c]
                    unit_wait(pe, U_V)
                    w = unit(U_V).rearrange("p (k c) -> p k c", k=KD)
                    for k in range(KD):
                        last = mm(b[0:m, 0:512], uT[:, k, r0:r0 + m], w[:, k, :], start=(k == 0), stop=(k == KD - 1))
                elif kind == "vb":
                    after("A", ("v", NT - 1))
                    last = mm(b[:, 0:512], ident[0:NB, c:c + 1].to_broadcast([NB, P]), v_rows[0:NB, 4, :],
                              start=True, stop=True)
                elif kind == "so":
                    after("D", ("vb", c))
                    for h in range(H):
                        last = mm(b[:, h:h + 1], state[c % 4][:, h * P:(h + 1) * P], qk[:, h, SEQ + c:SEQ + c + 1],
                                  start=True, stop=True)
                elif kind in ("scA", "scB"):
                    kT, qT = qk[:, H + c, :], qk[:, c, :]
                    for half, j in enumerate((0, 1) if kind == "scA" else (2, 3)):
                        width = SEQ - j * P
                        last = mm(b[:, half * 512:half * 512 + width], kT[:, j * P:(j + 1) * P], qT[:, j * P:SEQ],
                                  start=True, stop=True)
                elif kind == "kt":
                    for j in range(4):
                        last = tr(b[:, j * P:(j + 1) * P], qk[:, H + c, j * P:(j + 1) * P], ident[:, :])
                elif kind == "pv":
                    after("D", ("scB", c))
                    at = 0
                    for j in range(4):
                        width = SEQ - j * P
                        last = mm(b[:, j * P:SEQ], v_rows[:, j, c * P:(c + 1) * P], masked[c % 2][:, at:at + width],
                                  start=(j == 0), stop=(j == 3))
                        at += width
                elif kind == "st":
                    after("D", ("kt", c))
                    for j in range(4):
                        last = mm(b[:, 0:P], kd[c % 2][:, j * P:(j + 1) * P], v_rows[:, j, c * P:(c + 1) * P],
                                  start=(j == 0), stop=(j == 3))
                elif kind == "mn":
                    if c == 0:
                        pe.wait_ge(decay_loaded, 16 * 3)
                    after("A", ("pv", c))
                    last = over_tokens(b, lambda k: meanw[:, :], lambda k, c0: qk[:, c, c0:c0 + HALF], 1)
                elif kind == "vr":
                    after("A", ("mn", c))
                    last = over_tokens(b, lambda k: meanw[:, :], lambda k, c0: qk[:, H + c, c0:c0 + HALF], 1)
                elif kind == "co":
                    after("D", ("gb", CC - 1))
                    for k in range(CC):
                        last = tr(b[0:10, k * P:(k + 1) * P], new_z[:, k, :], ident[:, :])
                elif kind == "wo":
                    r0, m = TILES[c]
                    for half in range(2):
                        unit_wait(pe, U_O + half)
                        w = unit(U_O + half).rearrange("p (k c) -> p k c", k=KD)
                        for k in range(KD):
                            last = mm(b[0:m, half * 512:half * 512 + 512], mixT[:, k, r0:r0 + m], w[:, k, :],
                                      start=(k == 0), stop=(k == KD - 1))
                elif kind == "xt":
                    m = TILES[c][1]
                    after("D", ("wo", c))
                    for k in range(KD):
                        last = tr(b[:, k * P:k * P + m], xn[c % 2][0:m, k * P:(k + 1) * P], ident[0:m, 0:m])
                elif kind == "rt":
                    after("A", ("xt", NT - 1))
                    last = over_tokens(b, lambda k: w_r[:, k, :], u_cols, KD, m=NR)
                elif kind == "lg":
                    after("A", ("rt", 0))
                    for t in range(4):
                        last = tr(b[:, t * NR:(t + 1) * NR], log_t[:, t * P:(t + 1) * P], ident[0:NR, 0:NR])
                elif kind == "lgs":
                    last = tr(b[0:NB, 0:NR], log_t[:, SEQ:T], ident[0:NR, 0:NR])
                elif kind == "pt":
                    if c == 0:
                        pe.wait_ge(late_loaded, 16 * 4)
                        for t in range(4):
                            for k in range(2):
                                last = tr(b[:, k * 512 + t * P:k * 512 + (t + 1) * P], p_rows[:, t, k * P:(k + 1) * P],
                                          ident[:, :])
                    else:
                        for k in range(2):
                            last = tr(b[:, k * NB:(k + 1) * NB], p_rows[0:NB, 4, k * P:(k + 1) * P],
                                      ident[0:NB, 0:NB])
                elif kind == "pp":
                    r0, m = TILES[c]
                    after("A", ("pt", 1))
                    unit_wait(pe, U_PP)
                    w = unit(U_PP)[:, 0:2 * D].rearrange("p (k c) -> p k c", k=2)
                    for half in range(2):
                        for k in range(2):
                            last = mm(b[0:m, half * 512:half * 512 + 512], pT[:, k, r0:r0 + m],
                                      w[:, k, half * 512:half * 512 + 512], start=(k == 0), stop=(k == 1))
                elif kind == "rk":
                    pe.wait_ge(chosen_done, 1)
                    for t in range(NT):
                        for s in range(t + 1):
                            last = mm(b[:, t * NE:(t + 1) * NE], lt16[:, int(s < t), :], chosen[:, s, :],
                                      start=(s == 0), stop=(s == t))
                elif kind == "tot":
                    for s in range(NT):
                        last = mm(b[:, 0:NE], lt16[:, 1, :], chosen[:, s, :], start=(s == 0), stop=(s == NT - 1))
                elif kind == "ix":
                    pe.wait_ge(hot_done, 1)
                    for s in range(2 * NT):
                        last = mm(b[:, 0:2 * NTILE], row_hot[:, s, :], tile_hot[:, s, :, :].rearrange(
                            "p k c -> p (k c)"), start=(s == 0), stop=(s == 2 * NT - 1))
                last.then_inc(pe_jobs, 1)

            def rows_t(b, in_wait, out_sem):
                pe.wait_ge(*in_wait)
                for k in range(4):
                    last = tr(ps[:, b, k * P:(k + 1) * P], xg[b][:, k * P:(k + 1) * P], ident[:, :])
                last.then_inc(out_sem, 1)

            def gate_up(b, slots, out_sem):
                xv = xgT[b].rearrange("p (k h r) -> p h k r", h=2, r=ROWS)
                for k in range(KD):
                    for side in range(2):
                        w = slots[side].rearrange("p (k c) -> p k c", k=KD)
                        last = mm(ps[side * 64:side * 64 + 64, 2 + b, :], xv[:, k // 4, k % 4, :], w[:, k, :],
                                  start=(k == 0), stop=(k == KD - 1))
                last.then_inc(out_sem, 1)

            def hidden_t(b, out_sem):
                for k in range(2):
                    last = tr(ps[:, 4 + b, k * P:(k + 1) * P], hs[b][:, k * P:(k + 1) * P], ident[:, :])
                last.then_inc(out_sem, 1)

            def down(b, slot, out_sem):
                w = slot.rearrange("p (k c) -> p k c", k=4)
                for q in range(4):
                    side_in, k = divmod(q, 2)
                    hv = hT[b][:, k * P + side_in * 64:k * P + side_in * 64 + 64]
                    for side in range(2):
                        last = mm(ps[side * 64:side * 64 + 64, 6 + b, :], hv, w[:, q, side * 512:side * 512 + 512],
                                  start=(q == 0), stop=(q == 3))
                last.then_inc(out_sem, 1)

            def pair_of_experts(i, first, last):
                for b in range(2):
                    e = i * 2 + b
                    if not (last and b == 1):
                        rows_t(1 - b, (xg_loaded[1 - b], i * 16 + 16 * (1 + b)), xt_done)
                    pe.wait_ge(xgT_ready, e + 1)
                    slots = []
                    for j in range(3):
                        n = HEAD_UNITS + 3 * b + j
                        slots.append(unit(n))
                        if j < 2:
                            pe.wait_ge(slot_filled[n % RING], i * 16 + 16 * (n // RING + 1))
                    gate_up(b, slots[0:2], gu_done)
                    pe.wait_ge(hs_done, e + 1)
                    hidden_t(b, ht_done)
                    pe.wait_ge(hT_ready, e + 1)
                    n = HEAD_UNITS + 3 * b + 2
                    pe.wait_ge(slot_filled[n % RING], i * 16 + 16 * (n // RING + 1))
                    if not first:
                        pe.wait_ge(out_ready, e - 1)
                    down(b, slots[2], down_done)

            pe.wait_ge(act_jobs, HEAD.count("A", len(JOBS)))
            pe.wait_ge(dve_jobs, HEAD.count("D", len(JOBS)))
            rows_t(0, (xg_loaded[0], 16), xt_done)
            pair_of_experts(0, True, False)
            with pe.Fori(1, NE // 2 - 1) as i:
                pair_of_experts(i, False, False)
            pair_of_experts(NE // 2 - 1, False, True)

            n_over = pe.value_load(over_expert[0:1, OVER:OVER + 1], min_val=0, max_val=OVER)
            with pe.If(n_over > 0):
                pe.wait_ge(out_ready, NE)
                with pe.Fori(0, OVER) as q:
                    rows_t(0, (ov["xg"], q * 16 + 16), ov["xt"])
                    pe.wait_ge(ov["xgT"], q + 1)
                    pe.wait_ge(ov["w"], q * 48 + 48)
                    gate_up(0, [ring[:, 0, :], ring[:, 1, :]], ov["gu"])
                    pe.wait_ge(ov["hs"], q + 1)
                    hidden_t(0, ov["ht"])
                    pe.wait_ge(ov["hT"], q + 1)
                    down(0, ring[:, 2, :], ov["down"])
                    pe.wait_ge(ov["out"], q + 1)
            with pe.Else():
                pe.wait_ge(index_done, 1)

            pe.wait_ge(out_ready, NE)
            for n, (kind, t) in enumerate(TAIL):
                b = pair(n)
                m = TILES[t][1]
                prev, readers = REST.free(n)
                if prev:
                    if prev[0] == "u":
                        pe.wait_ge(dve_tail, prev[1] + 1)
                    else:
                        pe.wait_ge(act_tail, prev[1] + 1)
                if kind == "u":
                    pe.wait_ge(u_ready, t + 1)
                    for k in range(KD):
                        last = tr(b[:, k * P:k * P + m], xs3[t % 2][0:m, k * P:(k + 1) * P], ident[0:m, 0:m])
                else:
                    pe.wait_ge(dve_tail, t + 1)
                    uv = u3T[t % 2].rearrange("p (k t) -> p k t", k=KD)
                    for half in range(2):
                        unit_wait(pe, U_GATE + half)
                        w = unit(U_GATE + half).rearrange("p (k c) -> p k c", k=KD)
                        for k in range(KD):
                            last = mm(b[0:m, half * 512:half * 512 + 512], uv[:, k, 0:m], w[:, k, :],
                                      start=(k == 0), stop=(k == KD - 1))
                last.then_inc(pe_tail, 1)


def small_constants():
    p = np.arange(P, dtype=np.float32)
    lg = np.log(np.float32(1.0) - np.float32(2.0) ** (np.float32(-5.0) - np.arange(H, dtype=np.float32)))
    lg = lg.astype(np.float32)
    inv = np.float32(1.0) / np.float32(10000.0) ** (np.arange(0, P, 2, dtype=np.float32) / np.float32(P))
    pos = np.concatenate([np.arange(SEQ), np.full(NB, PAST)]).astype(np.float32)
    ang = (pos[None, :] * inv.astype(np.float32)[:, None]).astype(np.float32)
    cos = np.cos(ang).astype(np.float32)
    sin = np.sin(ang).astype(np.float32)
    diff = np.arange(SEQ)[None, :] - np.arange(P)[:, None]
    decay = np.stack([np.where(diff >= 0, np.exp(np.float64(g) * np.maximum(diff, 0)), 0.0) for g in lg], 1) * SCALE
    left = (SEQ - 1 - np.arange(SEQ)).reshape(4, P).T
    kdec = np.stack([np.exp(np.float64(g) * left) for g in lg], 1) * SCALE
    token = np.zeros((P, NT), np.float32)
    for t, (r0, m) in enumerate(TILES):
        token[:m, t] = r0 + np.arange(m) + 1
    two = np.arange(2)[None, None, :]
    live = (token > 0)[:, :, None]
    c = dict(
        kdec=kdec.reshape(P, 16), gam=np.tile(np.exp(lg.astype(np.float64)), (P, 1)),
        desc4=np.tile(np.arange(NG, 0, -1), (P, 1)), desc8=np.tile(np.arange(EPG, 0, -1), (P, 1)),
        thr=np.tile(np.arange(1, 9) * ROWS, (P, 1)),
        tokp=np.repeat(token, 2, 1), valp=(np.where(live, (token[:, :, None] - 1) * 2 + two + 1, 0)).reshape(P, 10),
        nh2=(np.arange(P) // 64 - 2).reshape(P, 1), eps=np.full((P, 1), EPS), io48=np.tile(np.arange(NTILE), (P, 1)))
    c = {k: x.astype(np.float32) for k, x in c.items()}
    big = dict(
        cos=np.concatenate([cos, cos]), sin=np.concatenate([-sin, sin]),
        decay=decay.reshape(P, H * SEQ).astype(np.float32), ident=np.eye(P, dtype=np.float32),
        meanw=np.full((P, P), 1.0 / P, np.float32),
        lt16=np.stack([(p[:, None] < p[None, :]), np.ones((P, P))], 1).astype(np.float16),
        io128=np.tile(np.arange(P) % ROWS, (P, 1)).astype(np.float32),
        io32=np.tile(np.arange(NE), (P, 1)).astype(np.float32),
        io16=np.tile(np.arange(OVER), (P, 1)).astype(np.float32))
    return c, big


def columns(vector):
    return np.ascontiguousarray(vector.reshape(-1, P).T)


def k_major(w, width):
    k, n = w.shape
    return np.ascontiguousarray(w.reshape(k // P, P, n // width, width).transpose(2, 1, 0, 3).reshape(
        n // width, P, (k // P) * width))


def layout(i):
    c, arrays = small_constants()
    g = lambda name: np.asarray(i[name])
    c["gmix"], c["gple"] = columns(g("g_mix")[0]), columns(g("g_ple")[0])
    c["convw"] = g("conv_w")[0].reshape(3, CC, P).transpose(2, 1, 0).reshape(P, 12)
    c["gn"] = columns(g("ret_gn")[0])
    bias = np.concatenate([g("b_router_group")[0], g("b_router_expert")[0].reshape(-1)])
    c["bias"] = np.broadcast_to(bias, (P, NR))
    order = ["gmix", "gple", "convw", "gn", "kdec", "gam", "bias", "desc4", "desc8", "thr", "tokp", "valp", "nh2",
             "eps", "io48"]
    arrays["small"] = np.ascontiguousarray(np.concatenate([c[k] for k in order], 1))
    arrays["x"] = np.concatenate([g("x_prompt")[0], g("x_sample")[:, 0]], 0)
    arrays["p"] = np.concatenate([g("p_prompt")[0, 0], g("p_sample")[0, :, 0]], 0)
    arrays["state_conv"] = np.ascontiguousarray(g("state_conv")[0])
    arrays["state_ret"] = np.ascontiguousarray(g("state_ret")[0])
    w_in = k_major(g("w_in")[0], 512)
    arrays["w_in"] = np.ascontiguousarray(w_in[[3, 4, 5, 6, 1, 2, 0]])
    arrays["w_o"] = k_major(g("w_o")[0], 512)
    arrays["w_ple_gate"] = k_major(g("w_ple_gate")[0], 512)
    arrays["w_ple_proj"] = k_major(g("w_ple_proj")[0], D)[0]
    w_r = np.concatenate([g("w_router_group")[0], g("w_router_expert")[0]], 1)
    arrays["w_r"] = np.ascontiguousarray(w_r.reshape(KD, P, NR).transpose(1, 0, 2))
    exp = np.empty((NE, 3, P, UNIT), np.float32)
    gu = exp[:, :2].reshape(NE, 2, P, KD, 2, 256)
    for s, name in enumerate(("w_gate", "w_up")):
        gu[:, :, :, :, s, :] = g(name)[0].reshape(NE, KD, P, 2, 256).transpose(0, 3, 2, 1, 4)
    exp[:, 2] = g("w_down")[0].reshape(NE, 4, P, D).transpose(0, 2, 1, 3).reshape(NE, P, UNIT)
    arrays["w_exp"] = exp.reshape(NE * 3, P, UNIT)
    arrays["g_ffn"] = g("g_ffn")
    arrays["g_final"] = g("g_final").reshape(1, D)
    return arrays


OUTS = dict(y=(T, D), conv_p=(2, 512), ret_p=(H, P, P), conv_s=(NB, 2, 512), ret_s=(NB, H, P, P))


def kernel(**inputs):
    import concourse.bacc as bacc
    from concourse.bass_utils import run_bass_kernel_spmd

    nc = bacc.Bacc("TRN2", target_bir_lowering=False, num_devices=1)
    arrays = {f"in_{k}": v for k, v in layout(inputs).items()}
    ins = {k[3:]: nc.dram_tensor(k, v.shape, mybir.dt.from_np(v.dtype), kind="ExternalInput").ap()
           for k, v in arrays.items()}
    outs = {k: nc.dram_tensor(f"out_{k}", s, F32, kind="ExternalOutput").ap() for k, s in OUTS.items()}
    build(nc, ins, outs)
    r = run_bass_kernel_spmd(nc, [arrays], core_ids=[0]).results[0]
    y = r["out_y"]
    return (y[:SEQ].reshape(1, SEQ, D), y[SEQ:].reshape(NB, 1, D), r["out_conv_p"].reshape(1, 1, 2, 512),
            r["out_ret_p"].reshape(1, 1, H, P, P), r["out_conv_s"].reshape(1, NB, 2, 512),
            r["out_ret_s"].reshape(1, NB, H, P, P))
```

```python
from contextlib import ExitStack

import numpy as np

import concourse.bass as bass
from concourse import mybir

F32 = mybir.dt.float32
F32R = mybir.dt.float32r
F16 = mybir.dt.float16
I32 = mybir.dt.int32
ALU = mybir.AluOpType
ACT = mybir.ActivationFunctionType
AX = mybir.AxisListType

P = 128
D = 1024
KD = D // P
SEQ = 512
NB = 8
T = SEQ + NB
HALF = T // 2
TILES = [(t * P, min(P, T - t * P)) for t in range(5)]
NT = len(TILES)
PAST = 4096
H = 4
CC = 4
WIN_UNITS = 7
NG, EPG = 4, 8
NE = NG * EPG
NR = NG + NE
FF = 512
PLE = 256
EPS = 1e-6
ROWS = 64
OVER = 2 * T // ROWS
NTILE = NE + OVER
NOWHERE = 4096.0
RING = 6
UNIT = 4096
SCALE = float(P) ** -0.5


def job_list():
    jobs = [("buf", 0)] + [("x", t) for t in range(NT)]
    jobs += [(kind, h) for kind in "qkv" for h in range(H)] + [("g", 0)] + [("vt", t) for t in range(NT)]
    jobs += [("vb", b) for b in range(4)] + [("g", 1)] + [("so", b) for b in range(4)] + [("g", 2), ("g", 3)]
    jobs += [("vb", b) for b in range(4, NB)]
    conv = iter([(k, c) for c in range(CC) for k in ("gc", "hc", "gb")])
    for s in range(H + 3):
        if s < H:
            jobs += [("scA", s), ("scB", s), ("kt", s)]
        if s < 2:
            jobs += [("so", 4 + 2 * s), ("so", 5 + 2 * s)]
        if 0 <= s - 1 < H:
            jobs += [("pv", s - 1), ("st", s - 1)]
        if 0 <= s - 2 < H:
            jobs.append(("mn", s - 2))
        if 0 <= s - 3 < H:
            jobs.append(("vr", s - 3))
        if s >= H:
            jobs += [next(conv) for _ in range(3)]
    jobs += list(conv)
    jobs += [("wo", 4), ("wo", 0), ("co", 0), ("xt", 4), ("wo", 1), ("xt", 0), ("wo", 2), ("xt", 1), ("wo", 3),
             ("xt", 2), ("rt", 0), ("pt", 0), ("pt", 1), ("xt", 3), ("rt", 1), ("lg", 0), ("tot", 0), ("rk", 0),
             ("pp", 0), ("pp", 1), ("ix", 0), ("pp", 2), ("pp", 3), ("pp", 4)]
    return jobs


READERS = dict(buf="D", x="D", q="AD", k="AD", v="A", vt="A", g="A", vb="D", so="D", scA="D", scB="D", kt="D", pv="A",
               st="A", mn="DA", vr="AD", gc="A", hc="D", gb="D", co="A", wo="DA", xt="A", rt="A", lg="D",
               pt="A", pp="A", rk="D", tot="D", ix="D", u="D", pg="AD")
JOBS = job_list()
CHUNKS = [j for j in JOBS if j[0] in ("q", "k", "v", "g", "gc", "hc", "gb")]
UNIT_OF = dict(q=0, k=1, v=2, g=3, gc=4, hc=5, gb=6)
TAIL = [("u", 0)]
for _t in range(NT):
    TAIL += ([("u", _t + 1)] if _t + 1 < NT else []) + [("pg", _t)]


class Plan:

    def __init__(self, jobs):
        self.jobs = jobs
        self.at = {j: n for n, j in enumerate(jobs)}

    def pe(self, job):
        return self.at[job] + 1

    def count(self, engine, n):
        return sum(engine in READERS[k] for k, _ in self.jobs[:n + 1])

    def done(self, engine, job):
        return self.count(engine, self.at[job])

    def free(self, n):
        return (self.jobs[n - 4], READERS[self.jobs[n - 4][0]]) if n >= 4 else (None, "")


HEAD, REST = Plan(JOBS), Plan(TAIL)
HEAD_SLOT = [0, 1, 2, 3, 0, 1, 2, 3, 0]
EXPERT_SLOTS = [4, 5, 1, 2, 3, 0]
WO_ORDER = [4, 0, 1, 2, 3]


def build(nc, a, o):
    y_rows = nc.dram_tensor("y_rows", [2 * T, D], F32, kind="Internal").ap()
    xn_rows = nc.dram_tensor("xn_rows", [T, D], F32, kind="Internal").ap()
    y_half = y_rows.rearrange("r (n c) -> (r n) c", n=2)
    xn_half = xn_rows.rearrange("r (n c) -> (r n) c", n=2)
    y_tok = y_rows.rearrange("(t k) c -> t (k c)", k=2)

    with ExitStack() as ctx:
        def sb(name, shape, dt=F32):
            return ctx.enter_context(nc.sbuf_tensor(name, shape, dt))

        def sem(name):
            return ctx.enter_context(nc.semaphore(name))

        ps = ctx.enter_context(nc.psum_tensor("ps", [P, 8, 512], F32))
        psf = ps[:, :, :].rearrange("p b c -> p (b c)")

        def pair(n):
            return psf[:, (n % 4) * 1024:(n % 4) * 1024 + 1024]

        def halves(ap):
            return ap.rearrange("p (b c) -> p b c", b=2)[:, :, 0:HALF]

        ring_at = -(-nc.sbuf_base // 32) * 32
        arena = sb("arena", [P, RING * UNIT + 64])
        ring = arena[:, 0:RING * UNIT].rearrange("p (s c) -> p s c", s=RING)
        xh = sb("xh", [P, NT, D])
        region_u_at = -(-nc.sbuf_base // 32) * 32
        region_u = sb("region_u", [P, KD * T])
        region_m = sb("region_m", [P, KD * T])
        region_q = sb("region_q", [P, 12 * T])
        region_v = sb("region_v", [P, NT * 512])
        region_z = sb("region_z", [P, 2128])
        cos_t = sb("cos_t", [P, T])
        sin_t = sb("sin_t", [P, T])
        region_d = sb("region_d", [P, H * SEQ])
        ident = sb("ident", [P, P])
        meanw = sb("meanw", [P, P])
        w_r = sb("w_r", [P, KD, NR])
        small = sb("small", [P, 256])
        stats = sb("stats", [P, 48])
        conv_hist = sb("conv_hist", [P, CC, NB, 2])
        new_z = sb("new_z", [P, CC, 10])
        wk = sb("wk", [P, NT, 2])
        index = sb("index", [P, 2 * NTILE], I32)
        over_expert = sb("over_expert", [1, OVER + 1], I32)
        gcol = sb("gcol", [P, 2], I32)
        scol = sb("scol", [P, 2], I32)

        cuts = dict(gmix=8, gple=8, convw=12, gn=4, kdec=16, gam=4, bias=36, desc4=4, desc8=8, thr=8, live=5,
                    valp=10, half=1, nh2=1, eps=1, io48=NTILE)
        at, col = 0, {}
        for name, width in cuts.items():
            col[name] = small[:, at:at + width]
            at += width
        assert at <= 256

        uT = region_u[:, :].rearrange("p (k t) -> p k t", k=KD)
        def at_r(name, n, offset):
            return nc.alloc_sbuf_tensor_at(name, [P, n], F32R, offset=offset)

        u_hi = at_r("u_hi", KD * T, region_u_at)[:, :].rearrange("p (k t) -> p k t", k=KD)
        high = ring_at + 4 * UNIT * 4
        u_lo = at_r("u_lo", KD * T, high)[:, :].rearrange("p (k t) -> p k t", k=KD)
        high += KD * T * 4
        w_hi = [at_r(f"w_hi{i}", D, high + i * D * 4)[:, :] for i in range(2)]
        w_lo = [at_r(f"w_lo{i}", D, high + (2 + i) * D * 4)[:, :] for i in range(2)]
        mixT = region_m[:, :].rearrange("p (k t) -> p k t", k=KD)
        qk = region_q[:, 0:8 * T].rearrange("p (h t) -> p h t", h=8)
        gT = region_q[:, 8 * T:12 * T].rearrange("p (h t) -> p h t", h=4)
        pp = region_q[:, 0:NT * D].rearrange("p (t c) -> p t c", t=NT)
        v_rows = region_v[:, :].rearrange("p (t c) -> p t c", t=NT)
        xs = [region_m[:, i * D:(i + 1) * D] for i in range(2)]
        junk = region_q[:, 0:D]
        u_tmp = [region_q[:, (1 + i) * D:(2 + i) * D] for i in range(2)]
        vT = region_m[:, 0:4 * T].rearrange("p (h t) -> p h t", h=H)
        buf_rows = region_v[0:16, 0:512]
        rot = [region_z[:, i * T:(i + 1) * T] for i in range(2)]
        state = [region_m[:, 4 * T + i * 512:4 * T + (i + 1) * 512] for i in range(4)]
        kv_tmp = region_z[:, 1280:1792]
        masked = [region_z[:, 0:1280], region_m[:, 0:1280]]
        kd = [region_z[:, 1280:1792], region_m[:, 1280:1792]]
        decay = region_d[:, :].rearrange("p (h r) -> p h r", h=H)
        gate_c = [region_z[:, i * T:(i + 1) * T] for i in range(2)]
        zc = [region_z[:, 1040 + i * 538:1040 + (i + 1) * 538] for i in range(2)]
        xn = [region_z[:, i * D:(i + 1) * D] for i in range(2)]
        g_ffn_b = region_d[:, 0:D]
        g_fin_b = region_d[:, D:2 * D]
        p_rows = region_v[:, 0:NT * PLE].rearrange("p (t c) -> p t c", t=NT)
        pT = region_v[:, NT * PLE:NT * PLE + 2 * T].rearrange("p (k t) -> p k t", k=2)
        st_out = cos_t[:, 0:512].rearrange("p (h e) -> p h e", h=H)
        co_out = sin_t[0:10, 0:512]

        cursor = [0]

        def scratch(n, dt=F32):
            words = n if dt == F32 else (n + 1) // 2
            ap = region_m[:, cursor[0]:cursor[0] + words]
            cursor[0] += words
            if dt != F32:
                ap = ap.bitcast(dt)
            return ap

        log_t = scratch(T)[0:NR, :]
        logit = scratch(NT * NR).rearrange("p (t c) -> p t c", t=NT)
        w4 = [scratch(NT * NG).rearrange("p (t c) -> p t c", t=NT) for _ in range(3)]
        w8 = [scratch(NT * EPG).rearrange("p (t c) -> p t c", t=NT) for _ in range(5)]
        w1 = [scratch(NT).rearrange("p (t c) -> p t c", t=NT) for _ in range(6)]
        w32 = scratch(NT * NE).rearrange("p (t c) -> p t c", t=NT)
        pick = scratch(2 * NT * NE).rearrange("p (k t e) -> p k t e", k=2, t=NT)
        w64 = scratch(2 * NT * NE).rearrange("p (k t e) -> p k t e", k=2, t=NT)
        rank = scratch(NT * NE).rearrange("p (t c) -> p t c", t=NT)
        chosen = scratch(NT * NE, dt=F16).rearrange("p (t c) -> p t c", t=NT)
        total = scratch(NE)
        over8 = scratch(NE * 8).rearrange("p (e c) -> p e c", c=8)
        scan = [scratch(16 + NE) for _ in range(2)]
        over_n = scratch(NE)
        sel = [scratch(NT * 2) for _ in range(4)]
        sel8 = scratch(NT * 2 * 8).rearrange("p (n c) -> p n c", c=8)
        ovx = scratch(OVER * NE)[0:1, :].rearrange("p (n e) -> p n e", e=NE)
        ovc = scratch(OVER + 1)[0:1, :]
        row_hot = region_u[:, 1024:1664].bitcast(F16).rearrange("p (n c) -> p n c", c=P)
        tile_hot = region_u[:, 1664:1904].bitcast(F16).rearrange("p (n c) -> p n c", c=NTILE)
        ixf = [scratch(2 * NTILE) for _ in range(2)]
        io128 = scratch(P)
        io32 = scratch(NE)
        lt16 = scratch(2 * P, dt=F16).rearrange("p (s c) -> p s c", s=2)
        io16 = scratch(OVER)
        assert cursor[0] <= KD * T, cursor[0]

        moe = 0
        xg, xgT, hs, sg, hT = [], [], [], [], []
        for lst, width in ((xg, 512), (xgT, 512), (sg, 256), (hs, 256), (hT, 256)):
            for _ in range(2):
                lst.append(region_u[:, moe:moe + width])
                moe += width
        assert moe <= KD * T
        out_sb = [region_v[:, i * 512:(i + 1) * 512] for i in range(2)]

        y_buf = [region_v[:, 0:2048], region_m[:, 0:2048]]
        u3T = [region_u[:, i * D:(i + 1) * D] for i in range(2)]
        gate = [region_u[:, 2 * D + i * D:3 * D + i * D] for i in range(2)]
        xs3 = xn

        slot_filled = [sem(f"slot_filled{i}") for i in range(RING)]
        x_loaded = [sem(f"x_loaded{i}") for i in range(NT)]
        first_chunk = [sem(f"first_chunk{i}") for i in range(4)]
        pp_loaded = sem("pp_loaded")
        rope_loaded = sem("rope_loaded")
        w_hi_ready, w_lo_ready = sem("w_hi_ready"), sem("w_lo_ready")
        u_split = sem("u_split")
        consts_loaded = sem("consts_loaded")
        decay_loaded = sem("decay_loaded")
        state_loaded = [sem(f"state_loaded{i}") for i in range(4)]
        state_scaled = sem("state_scaled")
        state_stored = [sem(f"state_stored{i}") for i in range(4)]
        late_loaded = sem("late_loaded")
        route_loaded = sem("route_loaded")
        xn_stored = [sem(f"xn_stored{i}") for i in range(2)]
        misc_stored = sem("misc_stored")
        root_done = sem("root_done")
        rstd_done = sem("rstd_done")
        xs_done = sem("xs_done")
        act_step = sem("act_step")
        dve_step = sem("dve_step")
        pool_step = sem("pool_step")
        pool_turn, sp_turn = sem("pool_turn"), sem("sp_turn")
        pe_jobs, act_jobs, dve_jobs = sem("pe_jobs"), sem("act_jobs"), sem("dve_jobs")
        half_copied = sem("half_copied")
        h_done = sem("h_done")
        lg_ready, ex_done = sem("lg_ready"), sem("ex_done")
        chosen_done, hot_done, index_done = sem("chosen_done"), sem("hot_done"), sem("index_done")
        xg_cleared = sem("xg_cleared")
        xg_loaded = [sem(f"xg_loaded{i}") for i in range(2)]
        out_stored = [sem(f"out_stored{i}") for i in range(2)]
        xt_done, xgT_ready, gu_done, silu_done = sem("xt_done"), sem("xgT_ready"), sem("gu_done"), sem("silu_done")
        hs_done, ht_done, hT_ready, down_done, out_ready = (
            sem("hs_done"), sem("ht_done"), sem("hT_ready"), sem("down_done"), sem("out_ready"))
        ov = {n: sem("over_" + n) for n in ("w", "xg", "xt", "xgT", "gu", "silu", "hs", "ht", "hT", "down", "out",
                                            "stored")}
        y_loaded = [sem(f"y_loaded{i}") for i in range(2)]
        hy_done, hy_sq, hy_root, hy_rstd, u_ready = (
            sem("hy_done"), sem("hy_sq"), sem("hy_root"), sem("hy_rstd"), sem("u_ready"))
        pe_tail, act_tail, dve_tail = sem("pe_tail"), sem("act_tail"), sem("dve_tail")
        f_done, f_sq, f_root, y_done, y_stored = (
            sem("f_done"), sem("f_sq"), sem("f_root"), sem("y_done"), sem("y_stored"))

        def head_slot(n):
            return ring[:, HEAD_SLOT[n], :]

        def head_wait(eng, n):
            eng.wait_ge(slot_filled[HEAD_SLOT[n]], 16 * HEAD_SLOT[1:n + 1].count(HEAD_SLOT[n]))

        def chunk_of(n):
            kind, c = CHUNKS[n]
            return head_slot(UNIT_OF[kind])[:, c * D:(c + 1) * D]

        def exp_slot(j):
            return EXPERT_SLOTS[j]

        def exp_fills(j):
            return HEAD_SLOT[1:].count(exp_slot(j)) + 1

        U_O = WIN_UNITS
        GATE_SLOTS = (exp_slot(0), exp_slot(1))
        OVER_SLOTS = (exp_slot(2), exp_slot(3), exp_slot(4))
        w_pp = region_z[:, 0:2 * D]

        block = ctx.enter_context(nc.Block())

        @block.sync
        def _(sp):
            for t, (r0, m) in enumerate(TILES):
                sp.dma_start(xh[0:m, t, :], a["x"][r0:r0 + m, :]).then_inc(x_loaded[t], 16)
            for c in range(4):
                sp.dma_start(head_slot(0)[:, c * D:(c + 1) * D], a["w_in"][0, :, c * D:(c + 1) * D]).then_inc(
                    first_chunk[c], 16)
            sp.dma_start(cos_t[:, :], a["cos"]).then_inc(rope_loaded, 16)
            sp.dma_start(sin_t[:, :], a["sin"]).then_inc(rope_loaded, 16)
            for n in range(1, len(HEAD_SLOT)):
                before = [m for m in range(n) if HEAD_SLOT[m] == HEAD_SLOT[n]]
                if before:
                    last = max(i for i, (kind, _) in enumerate(CHUNKS) if UNIT_OF[kind] == before[-1])
                    sp.wait_ge(w_lo_ready, last + 1)
                src = a["w_in"][n] if n < WIN_UNITS else a["w_o"][n - WIN_UNITS]
                sp.dma_start(head_slot(n), src).then_inc(slot_filled[HEAD_SLOT[n]], 16)
            for j in range(6):
                slot = exp_slot(j)
                if slot in HEAD_SLOT[WIN_UNITS:]:
                    sp.wait_ge(pe_jobs, HEAD.pe(("wo", WO_ORDER[-1])))
                else:
                    sp.wait_ge(pe_jobs, HEAD.pe(CHUNKS[-1]))
                sp.dma_start(ring[:, slot, :], a["w_exp"][j]).then_inc(slot_filled[slot], 16)
                if j == 3:
                    sp.wait_ge(pe_jobs, HEAD.pe(("xt", WO_ORDER[-1])))
                    sp.wait_ge(xn_stored[0], 16 * 3)
                    sp.wait_ge(xn_stored[1], 16 * 2)
                    sp.dma_start(w_pp, a["w_ple_proj"]).then_inc(pp_loaded, 16)
            with sp.Fori(1, NE // 2) as i:
                for j in range(6):
                    slot = exp_slot(j)
                    sp.wait_ge(down_done if j % 3 == 2 else gu_done, i * 2 + (j // 3 - 1))
                    src = a["w_exp"][bass.ds(i * 6 + j, 1)].rearrange("a p c -> (a p) c")
                    sp.dma_start(ring[:, slot, :], src).then_inc(slot_filled[slot], 16)
            for n, slot in enumerate(GATE_SLOTS):
                sp.wait_ge(gu_done, NE - 1)
                sp.dma_start(ring[:, slot, :], a["w_ple_gate"][n]).then_inc(slot_filled[slot], 16)

            sp.wait_ge(index_done, 1)
            sp.wait_ge(down_done, NE)
            n_over = sp.value_load(over_expert[0:1, OVER:OVER + 1], min_val=0, max_val=OVER)
            with sp.If(n_over > 0):
                with sp.Fori(0, OVER) as q:
                    e = sp.value_load(over_expert[0:1, bass.ds(q, 1)], min_val=0, max_val=NE - 1)
                    for j in range(3):
                        src = a["w_exp"][bass.ds(e * 3 + j, 1)].rearrange("a p c -> (a p) c")
                        sp.dma_start(ring[:, OVER_SLOTS[j], :], src).then_inc(ov["w"], 16)
                    sp.wait_ge(ov["down"], q + 1)
                    sp.sem_inc(sp_turn, 1)
                sp.wait_ge(ov["stored"], 16 * OVER)
            with sp.Else():
                sp.wait_ge(index_done, 1)

            sp.wait_ge(out_stored[0], 16 * (NE // 2))
            sp.wait_ge(out_stored[1], 16 * (NE // 2))
            for t, (r0, m) in enumerate(TILES):
                if t >= 2:
                    sp.wait_ge(hy_done, t - 1)
                sp.dma_start(y_buf[t % 2][0:m, :], y_tok[r0:r0 + m, :]).then_inc(y_loaded[t % 2], 16)
            for t, (r0, m) in enumerate(TILES):
                sp.wait_ge(y_done, t + 1)
                sp.dma_start(o["y"][r0:r0 + m, :], xh[0:m, t, :]).then_inc(y_stored, 16)
            sp.wait_ge(y_stored, 16 * NT)
            sp.wait_ge(misc_stored, 16 * 4)
            for i in range(4):
                sp.wait_ge(state_stored[i], 32)

        @block.gpsimd
        def _(pool):
            def load_state(b):
                if b >= 4:
                    pool.wait_ge(state_stored[b % 4], 16 * (b // 4))
                    pool.wait_ge(pe_jobs, HEAD.pe(("so", b - 4)))
                pool.dma_start(state[b % 4].rearrange("p (h e) -> p h e", h=H), a["state_ret"][b].rearrange(
                    "h d e -> d h e")).then_inc(state_loaded[b % 4], 16)

            def low_half(n):
                pool.wait_ge(w_hi_ready, n + 1)
                if n >= 2:
                    pool.wait_ge(pe_jobs, HEAD.pe(CHUNKS[n - 2]))
                nc.gpsimd.tensor_tensor(w_lo[n % 2], chunk_of(n), w_hi[n % 2], ALU.subtract).then_inc(w_lo_ready, 1)

            gam = col["gam"].unsqueeze(2).to_broadcast([P, H, P])

            def scale_state(b):
                s3 = state[b % 4].rearrange("p (h e) -> p h e", h=H)
                pool.wait_ge(state_loaded[b % 4], 16 * (b // 4 + 1))
                nc.gpsimd.tensor_tensor(s3, s3, gam, ALU.mult).then_inc(state_scaled, 1)

            def store_state(b):
                pool.wait_ge(dve_jobs, HEAD.done("D", ("vb", b)))
                pool.dma_start(o["ret_s"][b].rearrange("h d e -> d h e"),
                               state[b % 4].rearrange("p (h e) -> p h e", h=H)).then_inc(state_stored[b % 4], 16)

            for n in range(len(CHUNKS)):
                low_half(n)
                if n < 4:
                    load_state(n)
                if n == 4:
                    pool.wait_ge(consts_loaded, 16 * 3)
                if 4 <= n < 8:
                    scale_state(n - 4)
                if n == 14:
                    for b in range(4):
                        store_state(b)
                if n == 15:
                    for b in range(4, NB):
                        load_state(b)
                    for b in range(4, NB):
                        scale_state(b)
                if n == 17:
                    for b in range(4, NB):
                        store_state(b)

            pool.wait_ge(dve_jobs, HEAD.done("D", ("scB", H - 1)))
            pool.dma_start(g_ffn_b, a["g_ffn"].to_broadcast([P, D])).then_inc(late_loaded, 16)
            pool.dma_start(g_fin_b, a["g_final"].to_broadcast([P, D])).then_inc(late_loaded, 16)
            pool.wait_ge(pe_jobs, HEAD.pe(("st", H - 1)))
            pool.dma_start(p_rows[:, 0:4, :], a["p"][0:SEQ].rearrange("(t p) c -> p t c", p=P)).then_inc(late_loaded, 16)
            pool.dma_start(p_rows[0:NB, 4, :], a["p"][SEQ:T]).then_inc(late_loaded, 16)
            pool.wait_ge(act_jobs, HEAD.done("A", ("st", H - 1)))
            pool.dma_start(o["ret_p"].rearrange("h d e -> d h e"), st_out).then_inc(misc_stored, 16)
            pool.dma_start(o["conv_s"][:, 0, :], a["state_conv"][:, 1, :]).then_inc(misc_stored, 16)
            pool.wait_ge(act_jobs, HEAD.done("A", ("co", 0)))
            pool.dma_start(o["conv_p"], co_out[0:2, :]).then_inc(misc_stored, 16)
            pool.dma_start(o["conv_s"][:, 1, :], co_out[2:10, :]).then_inc(misc_stored, 16)
            for n, t in enumerate(WO_ORDER):
                r0, m = TILES[t]
                pool.wait_ge(dve_jobs, HEAD.done("D", ("wo", t)))
                pool.dma_start(xn_rows[r0:r0 + m, :], xn[n % 2][0:m, :]).then_inc(xn_stored[n % 2], 16)
            pool.wait_ge(pe_jobs, HEAD.pe(("wo", WO_ORDER[-1])))
            for dst, name in ((io128, "io128"), (io32, "io32"), (io16, "io16"), (lt16, "lt16")):
                pool.dma_start(dst, a[name]).then_inc(route_loaded, 16)

            pool.wait_ge(pe_jobs, HEAD.pe(("rt", 1)))
            nc.gpsimd.memset(xg[0], 0.0).then_inc(xg_cleared, 1)
            nc.gpsimd.memset(xg[1], 0.0).then_inc(xg_cleared, 1)
            pool.wait_ge(xg_cleared, 2)
            pool.wait_ge(xn_stored[0], 16 * 3)
            pool.wait_ge(xn_stored[1], 16 * 2)
            pool.wait_ge(index_done, 1)

            steps = [0]

            def copied(ins):
                steps[0] += 1
                ins.then_inc(pool_step, 1)
                pool.wait_ge(pool_step, steps[0])

            def start_gather(b, loaded):
                pool.sem_inc(pool_turn, 1)
                pool.indirect_dma_start(out=xg[b], out_offset=None, in_=xn_half,
                                        in_offset=bass.IndirectOffsetOnAxis(ap=gcol[:, b:b + 1], axis=0),
                                        bounds_check=2 * T - 1, oob_is_err=False).then_inc(loaded, 16)

            def start_scatter(b, stored):
                pool.sem_inc(pool_turn, 1)
                pool.indirect_dma_start(out=y_half, out_offset=bass.IndirectOffsetOnAxis(ap=scol[:, b:b + 1], axis=0),
                                        in_=out_sb[b], in_offset=None,
                                        bounds_check=4 * T - 1, oob_is_err=False).then_inc(stored, 16)

            for b in range(2):
                copied(nc.gpsimd.tensor_copy(gcol[:, b:b + 1], index[:, b:b + 1]))
                start_gather(b, xg_loaded[b])

            def pair_of_experts(i, more):
                for b in range(2):
                    e = i * 2 + b
                    if more:
                        pool.wait_ge(xt_done, e + 1)
                        pool.wait_ge(xg_loaded[b], i * 16 + 16)
                        nc.gpsimd.tensor_copy(gcol[:, b:b + 1], index[:, bass.ds(e + 2, 1)]).then_inc(pool_step, 1)
                        pool.wait_ge(pool_step, e * 2 + 3)
                        start_gather(b, xg_loaded[b])
                    if not isinstance(i, int) or i > 0:
                        pool.wait_ge(out_stored[b], i * 16)
                    nc.gpsimd.tensor_copy(scol[:, b:b + 1], index[:, bass.ds(e + NTILE, 1)]).then_inc(pool_step, 1)
                    pool.wait_ge(pool_step, e * 2 + 4 if more else e + NE + 1)
                    pool.wait_ge(out_ready, e + 1)
                    start_scatter(b, out_stored[b])

            pair_of_experts(0, True)
            with pool.Fori(1, NE // 2 - 1) as i:
                pair_of_experts(i, True)
            pair_of_experts(NE // 2 - 1, False)
            base = 2 * NE

            n_over = pool.value_load(over_expert[0:1, OVER:OVER + 1], min_val=0, max_val=OVER)
            with pool.If(n_over > 0):
                pool.wait_ge(out_stored[0], 16 * (NE // 2))
                pool.wait_ge(xg_loaded[0], 16 * (NE // 2))
                with pool.Fori(0, OVER) as q:
                    nc.gpsimd.tensor_copy(gcol[:, 0:1], index[:, bass.ds(q + NE, 1)]).then_inc(pool_step, 1)
                    nc.gpsimd.tensor_copy(scol[:, 0:1], index[:, bass.ds(q + NE + NTILE, 1)]).then_inc(pool_step, 1)
                    pool.wait_ge(pool_step, q * 2 + (base + 2))
                    start_gather(0, ov["xg"])
                    pool.wait_ge(ov["out"], q + 1)
                    start_scatter(0, ov["stored"])
                    pool.wait_ge(ov["stored"], q * 16 + 16)
            with pool.Else():
                pool.wait_ge(index_done, 1)

        @block.scalar
        def _(act):
            act.dma_start(small[:, 0:a["small"].shape[1]], a["small"]).then_inc(consts_loaded, 16)
            act.dma_start(ident[:, :], a["ident"]).then_inc(consts_loaded, 16)
            act.dma_start(buf_rows, a["state_conv"].rearrange("b r c -> (b r) c")).then_inc(consts_loaded, 16)

            steps = [0]

            def link(ins):
                steps[0] += 1
                ins.then_inc(act_step, 1)
                act.wait_ge(act_step, steps[0])

            eps = col["eps"]
            for t, (r0, m) in enumerate(TILES):
                act.wait_ge(x_loaded[t], 16)
                if t == 0:
                    act.wait_ge(dve_step, 1)
                link(nc.scalar.activation(junk[0:m, :], xh[0:m, t, :], ACT.Square, accum_out=stats[0:m, t:t + 1]))
                if t == 0:
                    act.wait_ge(consts_loaded, 16 * 3)
                nc.scalar.activation(stats[0:m, 5 + t:6 + t], stats[0:m, t:t + 1], ACT.Sqrt, scale=1.0 / D,
                                     bias=eps[0:m, :]).then_inc(root_done, 1)
                act.wait_ge(rstd_done, t + 1)
                if t >= 2:
                    act.wait_ge(pe_jobs, HEAD.pe(("x", t - 2)))
                nc.scalar.activation(xs[t % 2][0:m, :], xh[0:m, t, :], ACT.Copy,
                                     scale=stats[0:m, 10 + t:11 + t]).then_inc(xs_done, 1)

            act.dma_start(region_d[:, :], a["decay"]).then_inc(decay_loaded, 16)
            act.dma_start(meanw[:, :], a["meanw"]).then_inc(decay_loaded, 16)
            act.dma_start(w_r[:, :, :], a["w_r"]).then_inc(decay_loaded, 16)

            def high_half(n):
                if n < 4:
                    act.wait_ge(first_chunk[n], 16)
                else:
                    head_wait(act, UNIT_OF[CHUNKS[n][0]])
                if n >= 2:
                    act.wait_ge(pe_jobs, HEAD.pe(CHUNKS[n - 2]))
                    act.wait_ge(w_lo_ready, n - 1)
                nc.scalar.activation(w_hi[n % 2], chunk_of(n), ACT.Copy).then_inc(w_hi_ready, 1)

            high_half(0)
            high_half(1)
            done = 0
            for n, (kind, c) in enumerate(JOBS):
                chunk = CHUNKS.index((kind, c)) if (kind, c) in CHUNKS else None
                if chunk is not None and chunk + 2 < len(CHUNKS):
                    high_half(chunk + 2)
                if "A" not in READERS[kind]:
                    continue
                b = pair(n)
                if (kind, c) == ("pp", 0):
                    for s, w in ((1, w4[0]), (2, w8[3])):
                        act.wait_ge(lg_ready, s)
                        nc.scalar.activation(w, w, ACT.Exp).then_inc(ex_done, 1)
                act.wait_ge(pe_jobs, n + 1)
                if done:
                    act.wait_ge(act_jobs, done)
                done += 1
                if kind in "qk":
                    turn = c if kind == "q" else H + c
                    if turn >= 2:
                        prev = ("q", turn - 2) if turn - 2 < H else ("k", turn - 2 - H)
                        act.wait_ge(dve_jobs, HEAD.done("D", prev))
                    r = rot[turn % 2].rearrange("p (b c) -> p b c", b=2)
                    nc.scalar.activation(r[0:64], halves(b)[64:128], ACT.Copy).then_inc(half_copied, 1)
                    nc.scalar.activation(r[64:128], halves(b)[0:64], ACT.Copy).then_inc(act_jobs, 1)
                elif kind == "v":
                    nc.scalar.activation(vT[:, c, :].rearrange("p (b c) -> p b c", b=2), halves(b),
                                         ACT.Copy).then_inc(act_jobs, 1)
                elif kind == "vt":
                    m = TILES[c][1]
                    nc.scalar.activation(v_rows[0:m, c, :], b[0:m, 0:512], ACT.Copy).then_inc(act_jobs, 1)
                elif kind == "g":
                    nc.scalar.activation(gT[:, c, :].rearrange("p (b c) -> p b c", b=2), halves(b),
                                         ACT.Silu).then_inc(act_jobs, 1)
                elif kind == "pv":
                    nc.scalar.activation(qk[:, c, 0:SEQ], b[:, 0:SEQ], ACT.Copy).then_inc(act_jobs, 1)
                elif kind == "st":
                    act.wait_ge(dve_jobs, HEAD.done("D", ("k", H - 1)))
                    nc.scalar.activation(st_out[:, c, :], b[:, 0:P], ACT.Copy).then_inc(act_jobs, 1)
                elif kind == "mn":
                    act.wait_ge(dve_jobs, HEAD.done("D", ("mn", c)))
                    nc.scalar.activation(qk[:, H + c, :], qk[:, c, :], ACT.Square).then_inc(act_jobs, 1)
                elif kind == "vr":
                    nc.scalar.activation(qk[:, H + c, :].rearrange("p (b c) -> p b c", b=2), halves(b), ACT.Sqrt,
                                         bias=eps).then_inc(act_jobs, 1)
                elif kind == "gc":
                    if c >= 2:
                        act.wait_ge(dve_jobs, HEAD.done("D", ("hc", c - 2)))
                    nc.scalar.activation(gate_c[c % 2].rearrange("p (b c) -> p b c", b=2), halves(b),
                                         ACT.Copy).then_inc(act_jobs, 1)
                elif kind == "co":
                    nc.scalar.activation(co_out, b[0:10, 0:512], ACT.Copy).then_inc(act_jobs, 1)
                elif kind == "wo":
                    m = TILES[c][1]
                    act.wait_ge(h_done, WO_ORDER.index(c) + 1)
                    link(nc.scalar.activation(junk[0:m, :], xh[0:m, c, :], ACT.Square,
                                              accum_out=stats[0:m, 15 + c:16 + c]))
                    nc.scalar.activation(stats[0:m, 20 + c:21 + c], stats[0:m, 15 + c:16 + c], ACT.Sqrt,
                                         scale=1.0 / D, bias=eps[0:m, :]).then_inc(act_jobs, 1)
                elif kind == "xt":
                    r0, m = TILES[c]
                    nc.scalar.activation(uT[:, :, r0:r0 + m], b.rearrange("p (k t) -> p k t", k=KD)[:, :, 0:m],
                                         ACT.Copy).then_inc(act_jobs, 1)
                elif kind == "rt":
                    nc.scalar.activation(log_t[:, c * HALF:(c + 1) * HALF], b[0:NR, 0:HALF],
                                         ACT.Copy).then_inc(act_jobs, 1)
                elif kind == "pt":
                    if c == 0:
                        nc.scalar.activation(pT[:, :, 0:SEQ], b.rearrange("p (k t) -> p k t", k=2),
                                             ACT.Copy).then_inc(act_jobs, 1)
                    else:
                        nc.scalar.activation(pT[:, :, SEQ:T], b[:, 0:2 * NB].rearrange("p (k t) -> p k t", k=2),
                                             ACT.Copy).then_inc(act_jobs, 1)
                elif kind == "pp":
                    m = TILES[c][1]
                    if m == P:
                        nc.scalar.activation(pp[:, c, :], b, ACT.Copy).then_inc(act_jobs, 1)
                    else:
                        for g in range(4):
                            ins = nc.scalar.activation(pp[0:m, c, g * 256:(g + 1) * 256],
                                                       b[32 * g:32 * g + m, 0:256], ACT.Copy)
                        ins.then_inc(act_jobs, 1)

            def evac_rows(b, count, t_done, out_sem):
                act.wait_ge(t_done, count)
                nc.scalar.activation(xgT[b], ps[:, b, :], ACT.Copy).then_inc(out_sem, 1)

            def silu(b, count, g_sem, out_sem):
                act.wait_ge(g_sem, count)
                nc.scalar.activation(sg[b], ps[:, 2 + b, 0:256], ACT.Silu).then_inc(out_sem, 1)

            def evac_out(b, count, d_sem, out_sem):
                act.wait_ge(d_sem, count)
                nc.scalar.activation(out_sb[b], ps[:, 6 + b, :], ACT.Copy).then_inc(out_sem, 1)

            def pair_of_experts(i, first, last):
                for b in range(2):
                    e = i * 2 + b
                    if not (last and b == 1):
                        evac_rows(1 - b, e + 2, xt_done, xgT_ready)
                    silu(b, e + 1, gu_done, silu_done)
                    if not first:
                        act.wait_ge(out_stored[b], i * 16)
                    evac_out(b, e + 1, down_done, out_ready)

            evac_rows(0, 1, xt_done, xgT_ready)
            pair_of_experts(0, True, False)
            with act.Fori(1, NE // 2 - 1) as i:
                pair_of_experts(i, False, False)
            pair_of_experts(NE // 2 - 1, False, True)

            n_over = act.value_load(over_expert[0:1, OVER:OVER + 1], min_val=0, max_val=OVER)
            with act.If(n_over > 0):
                act.wait_ge(out_stored[0], 16 * (NE // 2))
                with act.Fori(0, OVER) as q:
                    evac_rows(0, q + 1, ov["xt"], ov["xgT"])
                    silu(0, q + 1, ov["gu"], ov["silu"])
                    evac_out(0, q + 1, ov["down"], ov["out"])
            with act.Else():
                act.wait_ge(index_done, 1)

            act.wait_ge(out_ready, NE)

            def row_norm(t):
                m = TILES[t][1]
                act.wait_ge(hy_done, t + 1)
                if t:
                    act.wait_ge(hy_sq, t)
                nc.scalar.activation(xs3[t % 2][0:m, :], xh[0:m, t, :], ACT.Square,
                                     accum_out=stats[0:m, 25 + t:26 + t]).then_inc(hy_sq, 1)
                act.wait_ge(hy_sq, t + 1)
                nc.scalar.activation(stats[0:m, 30 + t:31 + t], stats[0:m, 25 + t:26 + t], ACT.Sqrt, scale=1.0 / D,
                                     bias=eps[0:m, :]).then_inc(hy_root, 1)
                act.wait_ge(hy_rstd, t + 1)
                nc.scalar.activation(xs3[t % 2][0:m, :], xh[0:m, t, :], ACT.Copy,
                                     scale=stats[0:m, 35 + t:36 + t]).then_inc(u_ready, 1)

            row_norm(0)
            for n, (kind, t) in enumerate(TAIL):
                if kind != "pg":
                    if t + 1 < NT:
                        if t:
                            act.wait_ge(pe_tail, REST.pe(("u", t - 1)))
                        row_norm(t + 1)
                    continue
                m = TILES[t][1]
                act.wait_ge(pe_tail, n + 1)
                if t >= 2:
                    act.wait_ge(f_done, t - 1)
                if m == P:
                    nc.scalar.activation(gate[t % 2], pair(n), ACT.Sigmoid).then_inc(act_tail, 1)
                else:
                    for g in range(4):
                        ins = nc.scalar.activation(gate[t % 2][0:m, g * 256:(g + 1) * 256],
                                                   pair(n)[32 * g:32 * g + m, 0:256], ACT.Sigmoid)
                    ins.then_inc(act_tail, 1)
                act.wait_ge(f_done, t + 1)
                link(nc.scalar.activation(gate[t % 2][0:m, :], xh[0:m, t, :], ACT.Square,
                                          accum_out=stats[0:m, t:t + 1]))
                nc.scalar.activation(stats[0:m, 5 + t:6 + t], stats[0:m, t:t + 1], ACT.Sqrt, scale=1.0 / D,
                                     bias=eps[0:m, :]).then_inc(f_root, 1)

        @block.vector
        def _(dve):
            steps = [0]

            def link(ins):
                steps[0] += 1
                ins.then_inc(dve_step, 1)
                dve.wait_ge(dve_step, steps[0])

            V = nc.vector
            link(V.memset(stats[:, :], 1.0))

            def wide(ap, shape):
                return ap.unsqueeze(2).to_broadcast(shape)

            def first_largest(src, top, hot, table, shape):
                link(V.tensor_reduce(top, src, AX.X, ALU.max))
                link(V.tensor_tensor(hot, src, top.to_broadcast(shape), ALU.is_equal))
                link(V.tensor_tensor(hot, hot, table, ALU.mult))
                link(V.tensor_reduce(w1[1], hot, AX.X, ALU.max))
                link(V.tensor_tensor(hot, hot, w1[1].to_broadcast(shape), ALU.is_equal))

            shape4, shape8 = [P, NT, NG], [P, NT, EPG]
            hot_g, hot_1, hot_2, top_g, top_1, top_2 = w4[1], w8[1], w8[2], w1[5], w1[0], w1[2]
            n10 = NT * 2

            def route_choose():
                d4 = col["desc4"].unsqueeze(1).to_broadcast(shape4)
                d8 = col["desc8"].unsqueeze(1).to_broadcast(shape8)
                first_largest(logit[:, :, 0:NG], top_g, hot_g, d4, shape4)
                live = col["live"].unsqueeze(2).to_broadcast(shape4)
                link(V.tensor_tensor(hot_g, hot_g, live, ALU.mult))
                wide_g = hot_g.unsqueeze(3).to_broadcast([P, NT, NG, EPG])
                link(V.tensor_tensor(w32.rearrange("p t (g e) -> p t g e", g=NG),
                                     logit[:, :, NG:NR].rearrange("p t (g e) -> p t g e", g=NG), wide_g, ALU.mult))
                link(V.tensor_reduce(w8[0].unsqueeze(3), w32.rearrange("p t (g e) -> p t e g", g=NG), AX.X, ALU.add))
                first_largest(w8[0], top_1, hot_1, d8, shape8)
                link(V.scalar_tensor_tensor(w8[3], hot_1, -1e30, w8[0], ALU.mult, ALU.add))
                first_largest(w8[3], top_2, hot_2, d8, shape8)
                link(V.tensor_tensor(w8[4], hot_1, hot_2, ALU.add))
                V.tensor_tensor(chosen.rearrange("p t (g e) -> p t g e", g=NG), wide_g,
                                w8[4].unsqueeze(2).to_broadcast([P, NT, NG, EPG]), ALU.mult).then_inc(chosen_done, 1)
                V.tensor_tensor(w4[0], logit[:, :, 0:NG], top_g.to_broadcast(shape4), ALU.subtract).then_inc(lg_ready, 1)
                V.tensor_tensor(w8[3], w8[0], top_1.to_broadcast(shape8), ALU.subtract).then_inc(lg_ready, 1)
                for k, hot in enumerate((hot_1, hot_2)):
                    link(V.tensor_tensor(pick[:, k, :, :].rearrange("p t (g e) -> p t g e", g=NG), wide_g,
                                         hot.unsqueeze(2).to_broadcast([P, NT, NG, EPG]), ALU.mult))
                of_choice(sel[1], io32.unsqueeze(1).unsqueeze(1).to_broadcast([P, 2, NT, NE]))

            def of_choice(out, table):
                link(V.tensor_tensor(w64, pick, table, ALU.mult))
                link(V.tensor_reduce(out.rearrange("p (k t) -> p k t", k=2).unsqueeze(3), w64, AX.X, ALU.add))

            def route_weights():
                dve.wait_ge(ex_done, 2)
                link(V.tensor_reduce(w1[3], w4[0], AX.X, ALU.add))
                link(V.reciprocal(w1[3], w1[3]))
                link(V.tensor_reduce(w1[4], w8[3], AX.X, ALU.add))
                link(V.reciprocal(w1[4], w1[4]))
                link(V.tensor_tensor(w8[3], w8[3], w1[4].to_broadcast(shape8), ALU.mult))
                for top, hot in ((top_1, hot_1), (top_2, hot_2)):
                    link(V.tensor_tensor(w8[4], w8[3], hot, ALU.mult))
                    link(V.tensor_reduce(top, w8[4], AX.X, ALU.add))
                link(V.tensor_tensor(w1[4], top_1, top_2, ALU.add))
                link(V.reciprocal(w1[4], w1[4]))
                link(V.tensor_tensor(w1[4], w1[4], w1[3], ALU.mult))
                link(V.tensor_tensor(wk[:, :, 0:1], top_1, w1[4], ALU.mult))
                link(V.tensor_tensor(wk[:, :, 1:2], top_2, w1[4], ALU.mult))

            def route_further():
                link(V.tensor_tensor(over8, total.unsqueeze(2).to_broadcast([P, NE, 8]),
                                     col["thr"].unsqueeze(1).to_broadcast([P, NE, 8]), ALU.is_gt))
                link(V.tensor_reduce(over_n.unsqueeze(2), over8, AX.X, ALU.add))
                link(V.tensor_copy(scan[0][:, 16:16 + NE], over_n))
                src, dst = 0, 1
                for s in (1, 2, 4, 8, 16):
                    link(V.tensor_tensor(scan[dst][:, 16:16 + NE], scan[src][:, 16:16 + NE],
                                         scan[src][:, 16 - s:16 + NE - s], ALU.add))
                    src, dst = dst, src
                incl, excl = scan[src][:, 16:16 + NE], scan[dst][:, 0:NE]
                link(V.tensor_tensor(excl, incl, over_n, ALU.subtract))
                of_choice(sel[2], excl.unsqueeze(1).unsqueeze(1).to_broadcast([P, 2, NT, NE]))
                return incl

            def route_places(ranks):
                of_choice(sel[0], ranks)
                link(V.tensor_tensor(sel8, sel[0].unsqueeze(2).to_broadcast([P, n10, 8]),
                                     col["thr"].unsqueeze(1).to_broadcast([P, n10, 8]), ALU.is_ge))
                link(V.tensor_reduce(sel[3].unsqueeze(2), sel8, AX.X, ALU.add))
                link(V.scalar_tensor_tensor(sel[0], sel[3], -float(ROWS), sel[0], ALU.mult, ALU.add))
                link(V.scalar_tensor_tensor(sel[2], sel[3], float(NE - 1), sel[2], ALU.add, ALU.add))
                link(V.tensor_tensor(sel[2], sel[2], sel[1], ALU.subtract))
                link(V.scalar_tensor_tensor(sel[2], sel[3], 0.0, sel[2], ALU.is_gt, ALU.mult))
                link(V.tensor_tensor(sel[2], sel[2], sel[1], ALU.add))
                link(V.tensor_tensor(row_hot, sel[0].unsqueeze(2).to_broadcast([P, n10, P]),
                                     io128.unsqueeze(1).to_broadcast([P, n10, P]), ALU.is_equal))
                link(V.tensor_tensor(tile_hot, sel[2].unsqueeze(2).to_broadcast([P, n10, NTILE]),
                                     col["io48"].unsqueeze(1).to_broadcast([P, n10, NTILE]), ALU.is_equal))
                V.tensor_tensor(tile_hot, tile_hot, col["valp"].unsqueeze(2).to_broadcast([P, n10, NTILE]),
                                ALU.mult).then_inc(hot_done, 1)

            def route_experts(incl):
                link(V.tensor_tensor(ovx, incl[0:1, :].unsqueeze(1).to_broadcast([1, OVER, NE]),
                                     io16[0:1, :].unsqueeze(2).to_broadcast([1, OVER, NE]), ALU.is_le))
                link(V.tensor_reduce(ovc[:, 0:OVER].unsqueeze(2), ovx, AX.X, ALU.add))
                link(V.tensor_scalar(ovc[:, 0:OVER], ovc[:, 0:OVER], float(NE - 1), None, ALU.min))
                link(V.tensor_copy(ovc[:, OVER:OVER + 1], incl[0:1, NE - 1:NE]))
                link(V.tensor_copy(over_expert[:, :], ovc))

            dve.wait_ge(consts_loaded, 16 * 3)
            for t in range(NT):
                dve.wait_ge(root_done, t + 1)
                m = TILES[t][1]
                V.reciprocal(stats[0:m, 10 + t:11 + t], stats[0:m, 5 + t:6 + t]).then_inc(rstd_done, 1)

            done = 0
            for n, (kind, c) in enumerate(JOBS):
                if "D" not in READERS[kind]:
                    continue
                b = pair(n)
                if kind == "lg":
                    dve.wait_ge(pe_jobs, HEAD.pe(("wo", WO_ORDER[-1])))
                    link(V.memset(logit, 0.0))
                    link(V.memset(scan[0][:, 0:16], 0.0))
                    link(V.memset(scan[1][:, 0:16], 0.0))
                    dve.wait_ge(route_loaded, 16 * 4)
                dve.wait_ge(pe_jobs, n + 1)
                if done:
                    dve.wait_ge(dve_jobs, done)
                done += 1
                if kind == "buf":
                    V.tensor_copy(conv_hist[:, :, :, :].rearrange("p c b r -> p c (b r)"),
                                  b[:, 0:CC * 16].rearrange("p (c n) -> p c n", c=CC)).then_inc(dve_jobs, 1)
                elif kind == "x":
                    r0, m = TILES[c]
                    tmp = u_tmp[c % 2].rearrange("p (k t) -> p k t", k=KD)[:, :, 0:m]
                    if c:
                        dve.wait_ge(u_split, c)
                    V.tensor_tensor(tmp, b.rearrange("p (k t) -> p k t", k=KD)[:, :, 0:m],
                                    wide(col["gmix"], [P, KD, m]), ALU.mult).then_inc(dve_jobs, 1)
                    dve.wait_ge(dve_jobs, done)
                    link(V.tensor_copy(u_hi[:, :, r0:r0 + m], tmp))
                    V.tensor_tensor(u_lo[:, :, r0:r0 + m], tmp, u_hi[:, :, r0:r0 + m], ALU.subtract).then_inc(
                        u_split, 1)
                elif kind in "qk":
                    turn = c if kind == "q" else H + c
                    r, dst = rot[turn % 2], qk[:, turn, :]
                    two = "p (b c) -> p b c"
                    if turn == 0:
                        dve.wait_ge(xs_done, NT)
                        dve.wait_ge(u_split, NT)
                        dve.wait_ge(rope_loaded, 32)
                    dve.wait_ge(act_jobs, HEAD.done("A", (kind, c)))
                    dve.wait_ge(half_copied, turn + 1)
                    link(V.tensor_tensor(dst.rearrange(two, b=2), halves(b), cos_t[:, :].rearrange(two, b=2), ALU.mult))
                    link(V.tensor_tensor(r, r, sin_t[:, :], ALU.mult))
                    V.tensor_tensor(dst, dst, r, ALU.add).then_inc(dve_jobs, 1)
                elif kind == "vb":
                    s3 = state[c % 4].rearrange("p (h e) -> p h e", h=H)
                    kv = kv_tmp.rearrange("p (h e) -> p h e", h=H)
                    kcol = qk[:, H:2 * H, SEQ + c:SEQ + c + 1].to_broadcast([P, H, P])
                    link(V.tensor_tensor(kv, b[:, 0:512].rearrange("p (h e) -> p h e", h=H), kcol, ALU.mult))
                    dve.wait_ge(state_scaled, c + 1)
                    V.scalar_tensor_tensor(state[c % 4], kv_tmp, SCALE, state[c % 4], ALU.mult,
                                           ALU.add).then_inc(dve_jobs, 1)
                elif kind == "so":
                    V.tensor_copy(qk[:, 0:H, SEQ + c:SEQ + c + 1], b[:, 0:H].unsqueeze(2)).then_inc(dve_jobs, 1)
                elif kind in ("scA", "scB"):
                    if (kind, c) == ("scA", 0):
                        dve.wait_ge(decay_loaded, 16 * 3)
                    dst = masked[c % 2]
                    if kind == "scA":
                        link(V.tensor_tensor(dst[:, 0:512], b[:, 0:512], decay[:, c, 0:512], ALU.mult))
                        V.tensor_tensor(dst[:, 512:896], b[:, 512:896], decay[:, c, 0:384],
                                        ALU.mult).then_inc(dve_jobs, 1)
                    else:
                        link(V.tensor_tensor(dst[:, 896:1152], b[:, 0:256], decay[:, c, 0:256], ALU.mult))
                        V.tensor_tensor(dst[:, 1152:1280], b[:, 512:640], decay[:, c, 0:128],
                                        ALU.mult).then_inc(dve_jobs, 1)
                elif kind == "kt":
                    V.tensor_tensor(kd[c % 2].rearrange("p (t d) -> p t d", t=4),
                                    b[:, 0:512].rearrange("p (t d) -> p t d", t=4),
                                    wide(col["kdec"][:, 4 * c:4 * c + 4], [P, 4, P]), ALU.mult).then_inc(dve_jobs, 1)
                elif kind == "mn":
                    o3 = qk[:, c, :].rearrange("p (b c) -> p b c", b=2)
                    V.tensor_tensor(o3, o3, halves(b), ALU.subtract).then_inc(dve_jobs, 1)
                elif kind == "vr":
                    r = qk[:, H + c, :]
                    dve.wait_ge(act_jobs, HEAD.done("A", ("vr", c)))
                    if c == 0:
                        for i in range(4):
                            dve.wait_ge(state_stored[i], 32)
                    link(V.reciprocal(r, r))
                    link(V.tensor_tensor(r, r, qk[:, c, :], ALU.mult))
                    V.scalar_tensor_tensor(mixT[:, CC + c, :], r, col["gn"][:, c:c + 1], gT[:, c, :], ALU.mult,
                                           ALU.mult).then_inc(dve_jobs, 1)
                elif kind == "hc":
                    z = zc[c % 2]
                    zs = z[:, 514:538].rearrange("p (b r) -> p b r", r=3)
                    link(V.memset(z[:, 0:2], 0.0))
                    link(V.tensor_copy(zs[:, :, 0:2], conv_hist[:, c, :, :]))
                    dve.wait_ge(act_jobs, HEAD.done("A", ("gc", c)))
                    g = gate_c[c % 2]
                    link(V.tensor_tensor(z[:, 2:262], b[:, 0:260], g[:, 0:260], ALU.mult))
                    link(V.tensor_tensor(z[:, 262:514], b[:, 512:764], g[:, 260:512], ALU.mult))
                    link(V.tensor_tensor(zs[:, :, 2:3], b[:, 764:772].unsqueeze(2), g[:, 512:520].unsqueeze(2),
                                         ALU.mult))
                    link(V.tensor_copy(new_z[:, c, 0:2], z[:, 512:514]))
                    V.tensor_copy(new_z[:, c, 2:10].unsqueeze(2), zs[:, :, 2:3]).then_inc(dve_jobs, 1)
                elif kind == "gb":
                    z, y = zc[c % 2], mixT[:, c, :]
                    zs = z[:, 514:538].rearrange("p (b r) -> p b r", r=3)
                    ys = y[:, SEQ:T].unsqueeze(2)
                    w = col["convw"][:, 3 * c:3 * c + 3]
                    link(V.tensor_scalar(y[:, 0:SEQ], z[:, 0:SEQ], w[:, 0:1], None, ALU.mult))
                    link(V.tensor_scalar(ys, zs[:, :, 0:1], w[:, 0:1], None, ALU.mult))
                    for r in (1, 2):
                        link(V.scalar_tensor_tensor(y[:, 0:SEQ], z[:, r:r + SEQ], w[:, r:r + 1], y[:, 0:SEQ],
                                                    ALU.mult, ALU.add))
                        link(V.scalar_tensor_tensor(ys, zs[:, :, r:r + 1], w[:, r:r + 1], ys, ALU.mult, ALU.add))
                    V.tensor_tensor(y.rearrange("p (b c) -> p b c", b=2), y.rearrange("p (b c) -> p b c", b=2),
                                    halves(b), ALU.mult).then_inc(dve_jobs, 1)
                elif kind == "wo":
                    m = TILES[c][1]
                    if m == P:
                        V.tensor_tensor(xh[:, c, :], xh[:, c, :], b, ALU.add).then_inc(h_done, 1)
                    else:
                        for g in range(4):
                            at = slice(g * 256, (g + 1) * 256)
                            ins = V.tensor_tensor(xh[0:m, c, at], xh[0:m, c, at], b[32 * g:32 * g + m, 0:256],
                                                  ALU.add)
                        ins.then_inc(h_done, 1)
                    dve.wait_ge(act_jobs, HEAD.done("A", ("wo", c)))
                    link(V.reciprocal(stats[0:m, 10 + c:11 + c], stats[0:m, 20 + c:21 + c]))
                    turn = WO_ORDER.index(c)
                    if turn == 0:
                        dve.wait_ge(late_loaded, 16 * 4)
                    if turn >= 2:
                        dve.wait_ge(pe_jobs, HEAD.pe(("xt", WO_ORDER[turn - 2])))
                        dve.wait_ge(xn_stored[turn % 2], 16 * (turn // 2))
                    dve.wait_ge(h_done, turn + 1)
                    V.scalar_tensor_tensor(xn[turn % 2][0:m, :], xh[0:m, c, :], stats[0:m, 10 + c:11 + c],
                                           g_ffn_b[0:m, :], ALU.mult, ALU.mult).then_inc(dve_jobs, 1)
                elif kind == "lg":
                    bias = col["bias"].unsqueeze(1)
                    link(V.tensor_tensor(logit[:, 0:4, :], b[:, 0:4 * NR].rearrange("p (t c) -> p t c", t=4),
                                         bias.to_broadcast([P, 4, NR]), ALU.add))
                    V.tensor_tensor(logit[0:NB, 4, :], b[0:NB, 512:512 + NR], col["bias"][0:NB, :],
                                    ALU.add).then_inc(dve_jobs, 1)
                    dve.wait_ge(dve_jobs, done)
                    route_choose()
                elif kind == "tot":
                    V.tensor_copy(total, b[:, 0:NE]).then_inc(dve_jobs, 1)
                    dve.wait_ge(dve_jobs, done)
                    incl = route_further()
                elif kind == "rk":
                    V.tensor_copy(rank, b[:, 0:NT * NE].rearrange("p (t c) -> p t c", t=NT)).then_inc(dve_jobs, 1)
                    dve.wait_ge(dve_jobs, done)
                    route_places(rank.unsqueeze(1).to_broadcast([P, 2, NT, NE]))
                    route_experts(incl)
                elif kind == "ix":
                    at_x, at_y = slice(0, NTILE), slice(NTILE, 2 * NTILE)
                    V.tensor_copy(ixf[0][:, at_y], b[:, 0:NTILE]).then_inc(dve_jobs, 1)
                    dve.wait_ge(dve_jobs, done)
                    link(V.tensor_scalar(index[:, at_x], ixf[0][:, at_y], -1.0, None, ALU.add))
                    link(V.tensor_scalar(index[:, at_y], index[:, at_x], 1, None, ALU.arith_shift_right))
                    link(V.tensor_scalar(ixf[1][:, at_y], ixf[0][:, at_y], 0.0, NOWHERE, ALU.is_equal, ALU.mult))
                    link(V.tensor_scalar(ixf[0][:, at_x], index[:, at_y], 2.0, col["half"], ALU.mult, ALU.add))
                    link(V.tensor_tensor(index[:, at_x], ixf[0][:, at_x], ixf[1][:, at_y], ALU.add))
                    link(V.tensor_scalar(ixf[0][:, at_y], ixf[0][:, at_y], 2.0, col["nh2"], ALU.mult, ALU.add))
                    V.tensor_tensor(index[:, at_y], ixf[0][:, at_y], ixf[1][:, at_y], ALU.add).then_inc(index_done, 1)
                    route_weights()

            def mult_up(b, count, s_sem, out_sem):
                dve.wait_ge(s_sem, count)
                V.tensor_tensor(hs[b], sg[b], ps[:, 2 + b, 256:512], ALU.mult).then_inc(out_sem, 1)

            def evac_h(b, count, t_sem, out_sem):
                dve.wait_ge(t_sem, count)
                V.tensor_copy(hT[b], ps[:, 4 + b, 0:256]).then_inc(out_sem, 1)

            with dve.Fori(0, NE // 2) as i:
                for b in range(2):
                    e = i * 2 + b
                    mult_up(b, e + 1, silu_done, hs_done)
                    evac_h(b, e + 1, ht_done, hT_ready)

            n_over = dve.value_load(over_expert[0:1, OVER:OVER + 1], min_val=0, max_val=OVER)
            with dve.If(n_over > 0):
                with dve.Fori(0, OVER) as q:
                    mult_up(0, q + 1, ov["silu"], ov["hs"])
                    evac_h(0, q + 1, ov["ht"], ov["hT"])
            with dve.Else():
                dve.wait_ge(index_done, 1)

            def combine(t):
                m = TILES[t][1]
                dve.wait_ge(y_loaded[t % 2], 16 * (t // 2 + 1))
                yb, h = y_buf[t % 2], xh[0:m, t, :]
                link(V.scalar_tensor_tensor(h, yb[0:m, 0:D], wk[0:m, t, 0:1], h, ALU.mult, ALU.add))
                V.scalar_tensor_tensor(h, yb[0:m, D:2 * D], wk[0:m, t, 1:2], h, ALU.mult, ALU.add).then_inc(hy_done, 1)
                dve.wait_ge(hy_root, t + 1)
                V.reciprocal(stats[0:m, 35 + t:36 + t], stats[0:m, 30 + t:31 + t]).then_inc(hy_rstd, 1)

            combine(0)
            evicted = 0
            for n, (kind, t) in enumerate(TAIL):
                m = TILES[t][1]
                if kind == "u":
                    if t + 1 < NT:
                        combine(t + 1)
                    dve.wait_ge(pe_tail, n + 1)
                    if t >= 2:
                        dve.wait_ge(pe_tail, REST.pe(("pg", t - 2)))
                    V.tensor_tensor(u3T[t % 2].rearrange("p (k t) -> p k t", k=KD)[:, :, 0:m],
                                    pair(n).rearrange("p (k t) -> p k t", k=KD)[:, :, 0:m],
                                    wide(col["gple"], [P, KD, m]), ALU.mult).then_inc(dve_tail, 1)
                else:
                    h = xh[0:m, t, :]
                    dve.wait_ge(act_tail, t + 1)
                    dve.wait_ge(hy_done, t + 1)
                    link(V.tensor_tensor(pp[0:m, t, :], pp[0:m, t, :], gate[t % 2][0:m, :], ALU.mult))
                    V.tensor_tensor(h, h, pp[0:m, t, :], ALU.add).then_inc(f_done, 1)
                    dve.wait_ge(f_root, t + 1)
                    link(V.reciprocal(stats[0:m, 10 + t:11 + t], stats[0:m, 5 + t:6 + t]))
                    dve.wait_ge(f_done, t + 1)
                    V.scalar_tensor_tensor(h, h, stats[0:m, 10 + t:11 + t], g_fin_b[0:m, :], ALU.mult,
                                           ALU.mult).then_inc(y_done, 1)

        @block.tensor
        def _(pe):
            mm, tr = nc.tensor.matmul, nc.tensor.transpose

            def over_tokens(out, w_of, src, ks, m=P):
                for half in range(2):
                    for k in range(ks):
                        last = mm(halves(out)[0:m, half, :], w_of(k), src(k, half * HALF), start=(k == 0), stop=(k == ks - 1))
                return last

            def over_tokens_split(out, n):
                wh, wl = (x[n % 2].rearrange("p (k c) -> p k c", k=KD) for x in (w_hi, w_lo))
                for half in range(2):
                    cols = slice(half * HALF, (half + 1) * HALF)
                    for k in range(KD):
                        for s, (w, u) in enumerate(((wh, u_hi), (wh, u_lo), (wl, u_hi))):
                            last = mm(halves(out)[:, half, :], w[:, k, :], u[:, k, cols],
                                      start=(k == 0 and s == 0), stop=(k == KD - 1 and s == 2))
                return last

            def few_rows(out, src, w_of, ks):
                for k in range(ks):
                    for g in range(4):
                        last = mm(out[32 * g:32 * g + NB, 0:256], src(k), w_of(k, g), start=(k == 0),
                                  stop=(k == ks - 1))
                return last

            def u_cols(k, c0):
                return uT[:, k, c0:c0 + HALF]

            pe.wait_ge(consts_loaded, 16 * 3)
            for n, (kind, c) in enumerate(JOBS):
                b = pair(n)
                prev, readers = HEAD.free(n)
                if "A" in readers:
                    pe.wait_ge(act_jobs, HEAD.done("A", prev))
                if "D" in readers:
                    pe.wait_ge(dve_jobs, HEAD.done("D", prev))

                def after(engine, job):
                    pe.wait_ge(act_jobs if engine == "A" else dve_jobs, HEAD.done(engine, job))

                if kind == "buf":
                    for k in range(CC):
                        last = tr(b[:, 16 * k:16 * k + 16], buf_rows[:, k * P:(k + 1) * P], ident[0:16, 0:16])
                elif kind == "x":
                    m = TILES[c][1]
                    pe.wait_ge(xs_done, c + 1)
                    for k in range(KD):
                        last = tr(b[:, k * P:k * P + m], xs[c % 2][0:m, k * P:(k + 1) * P], ident[0:m, 0:m])
                elif (kind, c) in CHUNKS:
                    chunk = CHUNKS.index((kind, c))
                    if chunk == 0:
                        pe.wait_ge(u_split, NT)
                    pe.wait_ge(w_hi_ready, chunk + 1)
                    pe.wait_ge(w_lo_ready, chunk + 1)
                    last = over_tokens_split(b, chunk)
                elif kind == "vt":
                    r0, m = TILES[c]
                    after("A", ("v", H - 1))
                    for h in range(H):
                        last = tr(b[0:m, h * P:(h + 1) * P], vT[:, h, r0:r0 + m], ident[:, :])
                elif kind == "vb":
                    after("A", ("vt", NT - 1))
                    last = mm(b[:, 0:512], ident[0:NB, c:c + 1].to_broadcast([NB, P]), v_rows[0:NB, 4, :],
                              start=True, stop=True)
                elif kind == "so":
                    after("D", ("vb", c))
                    for h in range(H):
                        last = mm(b[:, h:h + 1], state[c % 4][:, h * P:(h + 1) * P], qk[:, h, SEQ + c:SEQ + c + 1],
                                  start=True, stop=True)
                elif kind in ("scA", "scB"):
                    kT, qT = qk[:, H + c, :], qk[:, c, :]
                    for half, j in enumerate((0, 1) if kind == "scA" else (2, 3)):
                        width = SEQ - j * P
                        last = mm(b[:, half * 512:half * 512 + width], kT[:, j * P:(j + 1) * P], qT[:, j * P:SEQ],
                                  start=True, stop=True)
                elif kind == "kt":
                    for j in range(4):
                        last = tr(b[:, j * P:(j + 1) * P], qk[:, H + c, j * P:(j + 1) * P], ident[:, :])
                elif kind == "pv":
                    after("D", ("scB", c))
                    at = 0
                    for j in range(4):
                        width = SEQ - j * P
                        last = mm(b[:, j * P:SEQ], v_rows[:, j, c * P:(c + 1) * P], masked[c % 2][:, at:at + width],
                                  start=(j == 0), stop=(j == 3))
                        at += width
                elif kind == "st":
                    after("D", ("kt", c))
                    for j in range(4):
                        last = mm(b[:, 0:P], kd[c % 2][:, j * P:(j + 1) * P], v_rows[:, j, c * P:(c + 1) * P],
                                  start=(j == 0), stop=(j == 3))
                elif kind == "mn":
                    if c == 0:
                        pe.wait_ge(decay_loaded, 16 * 3)
                    after("A", ("pv", c))
                    after("D", ("so", NB - 1))
                    last = over_tokens(b, lambda k: meanw[:, :], lambda k, c0: qk[:, c, c0:c0 + HALF], 1)
                elif kind == "vr":
                    after("A", ("mn", c))
                    last = over_tokens(b, lambda k: meanw[:, :], lambda k, c0: qk[:, H + c, c0:c0 + HALF], 1)
                elif kind == "co":
                    after("D", ("gb", CC - 1))
                    for k in range(CC):
                        last = tr(b[0:10, k * P:(k + 1) * P], new_z[:, k, :], ident[:, :])
                elif kind == "wo":
                    r0, m = TILES[c]
                    wo = [head_slot(U_O + half).rearrange("p (k c) -> p k c", k=KD) for half in range(2)]
                    order = (4, 5, 6, 7, 0, 1, 2, 3)
                    if m < P:
                        for half in range(2):
                            head_wait(pe, U_O + half)
                        after("D", ("gb", CC - 1))
                        last = few_rows(b, lambda k: mixT[:, k, r0:r0 + m],
                                        lambda k, g: wo[g // 2][:, k, g % 2 * 256:g % 2 * 256 + 256], KD)
                    else:
                        for half in range(2):
                            for k in order:
                                last = mm(b[:, half * 512:half * 512 + 512], mixT[:, k, r0:r0 + m],
                                          wo[half][:, k, :], start=(k == order[0]), stop=(k == order[-1]))
                elif kind == "xt":
                    m = TILES[c][1]
                    after("D", ("wo", c))
                    for k in range(KD):
                        rows = xn[WO_ORDER.index(c) % 2]
                        last = tr(b[:, k * P:k * P + m], rows[0:m, k * P:(k + 1) * P], ident[0:m, 0:m])
                elif kind == "rt":
                    after("A", ("xt", (2, 3)[c]))
                    for k in range(KD):
                        last = mm(b[0:NR, 0:HALF], w_r[:, k, :], u_cols(k, c * HALF), start=(k == 0),
                                  stop=(k == KD - 1))
                elif kind == "lg":
                    after("A", ("rt", 1))
                    for t in range(4):
                        last = tr(b[:, t * NR:(t + 1) * NR], log_t[:, t * P:(t + 1) * P], ident[0:NR, 0:NR])
                    last = tr(b[0:NB, 512:512 + NR], log_t[:, SEQ:T], ident[0:NR, 0:NR])
                elif kind == "pt":
                    if c == 0:
                        pe.wait_ge(late_loaded, 16 * 4)
                        for t in range(4):
                            for k in range(2):
                                last = tr(b[:, k * 512 + t * P:k * 512 + (t + 1) * P], p_rows[:, t, k * P:(k + 1) * P],
                                          ident[:, :])
                    else:
                        for k in range(2):
                            last = tr(b[:, k * NB:(k + 1) * NB], p_rows[0:NB, 4, k * P:(k + 1) * P],
                                      ident[0:NB, 0:NB])
                elif kind == "pp":
                    r0, m = TILES[c]
                    after("A", ("pt", 1))
                    pe.wait_ge(pp_loaded, 16)
                    w = w_pp.rearrange("p (k c) -> p k c", k=2)
                    if m < P:
                        last = few_rows(b, lambda k: pT[:, k, r0:r0 + m],
                                        lambda k, g: w[:, k, g * 256:(g + 1) * 256], 2)
                    for half in range(2 if m == P else 0):
                        for k in range(2):
                            last = mm(b[0:m, half * 512:half * 512 + 512], pT[:, k, r0:r0 + m],
                                      w[:, k, half * 512:half * 512 + 512], start=(k == 0), stop=(k == 1))
                elif kind == "rk":
                    for t in range(NT):
                        for s in range(t + 1):
                            last = mm(b[:, t * NE:(t + 1) * NE], lt16[:, int(s < t), :], chosen[:, s, :],
                                      start=(s == 0), stop=(s == t))
                elif kind == "tot":
                    pe.wait_ge(chosen_done, 1)
                    for s in range(NT):
                        last = mm(b[:, 0:NE], lt16[:, 1, :], chosen[:, s, :], start=(s == 0), stop=(s == NT - 1))
                elif kind == "ix":
                    pe.wait_ge(hot_done, 1)
                    for s in range(2 * NT):
                        last = mm(b[:, 0:NTILE], row_hot[:, s, :], tile_hot[:, s, :], start=(s == 0), stop=(s == 2 * NT - 1))
                last.then_inc(pe_jobs, 1)

            def rows_t(b, in_wait, out_sem):
                pe.wait_ge(*in_wait)
                for k in range(4):
                    last = tr(ps[:, b, k * P:(k + 1) * P], xg[b][:, k * P:(k + 1) * P], ident[:, :])
                last.then_inc(out_sem, 1)

            def gate_up(b, slots, out_sem):
                xv = xgT[b].rearrange("p (k h r) -> p h k r", h=2, r=ROWS)
                for k in range(KD):
                    for side in range(2):
                        w = slots[side].rearrange("p (k c) -> p k c", k=KD)
                        last = mm(ps[side * 64:side * 64 + 64, 2 + b, :], xv[:, k // 4, k % 4, :], w[:, k, :],
                                  start=(k == 0), stop=(k == KD - 1))
                last.then_inc(out_sem, 1)

            def hidden_t(b, out_sem):
                for k in range(2):
                    last = tr(ps[:, 4 + b, k * P:(k + 1) * P], hs[b][:, k * P:(k + 1) * P], ident[:, :])
                last.then_inc(out_sem, 1)

            def down(b, slot, out_sem):
                w = slot.rearrange("p (k c) -> p k c", k=4)
                for q in range(4):
                    side_in, k = divmod(q, 2)
                    hv = hT[b][:, k * P + side_in * 64:k * P + side_in * 64 + 64]
                    for side in range(2):
                        last = mm(ps[side * 64:side * 64 + 64, 6 + b, :], hv, w[:, q, side * 512:side * 512 + 512],
                                  start=(q == 0), stop=(q == 3))
                last.then_inc(out_sem, 1)

            def pair_of_experts(i, first, last):
                for b in range(2):
                    e = i * 2 + b
                    if not (last and b == 1):
                        rows_t(1 - b, (xg_loaded[1 - b], i * 16 + 16 * (1 + b)), xt_done)
                    pe.wait_ge(xgT_ready, e + 1)
                    slots = []
                    for j in range(3):
                        slot = exp_slot(3 * b + j)
                        slots.append(ring[:, slot, :])
                        if j < 2:
                            pe.wait_ge(slot_filled[slot], i * 16 + 16 * exp_fills(3 * b + j))
                    gate_up(b, slots[0:2], gu_done)
                    pe.wait_ge(hs_done, e + 1)
                    hidden_t(b, ht_done)
                    pe.wait_ge(hT_ready, e + 1)
                    pe.wait_ge(slot_filled[exp_slot(3 * b + 2)], i * 16 + 16 * exp_fills(3 * b + 2))
                    if not first:
                        pe.wait_ge(out_ready, e - 1)
                    down(b, slots[2], down_done)

            pe.wait_ge(act_jobs, HEAD.count("A", len(JOBS)))
            pe.wait_ge(dve_jobs, HEAD.count("D", len(JOBS)))
            rows_t(0, (xg_loaded[0], 16), xt_done)
            pair_of_experts(0, True, False)
            with pe.Fori(1, NE // 2 - 1) as i:
                pair_of_experts(i, False, False)
            pair_of_experts(NE // 2 - 1, False, True)

            n_over = pe.value_load(over_expert[0:1, OVER:OVER + 1], min_val=0, max_val=OVER)
            with pe.If(n_over > 0):
                pe.wait_ge(out_ready, NE)
                with pe.Fori(0, OVER) as q:
                    rows_t(0, (ov["xg"], q * 16 + 16), ov["xt"])
                    pe.wait_ge(ov["xgT"], q + 1)
                    pe.wait_ge(ov["w"], q * 48 + 48)
                    gate_up(0, [ring[:, OVER_SLOTS[0], :], ring[:, OVER_SLOTS[1], :]], ov["gu"])
                    pe.wait_ge(ov["hs"], q + 1)
                    hidden_t(0, ov["ht"])
                    pe.wait_ge(ov["hT"], q + 1)
                    down(0, ring[:, OVER_SLOTS[2], :], ov["down"])
                    pe.wait_ge(ov["out"], q + 1)
            with pe.Else():
                pe.wait_ge(index_done, 1)

            pe.wait_ge(out_ready, NE)
            for n, (kind, t) in enumerate(TAIL):
                b = pair(n)
                m = TILES[t][1]
                prev, readers = REST.free(n)
                if prev:
                    if prev[0] == "u":
                        pe.wait_ge(dve_tail, prev[1] + 1)
                    else:
                        pe.wait_ge(act_tail, prev[1] + 1)
                if kind == "u":
                    pe.wait_ge(u_ready, t + 1)
                    for k in range(KD):
                        last = tr(b[:, k * P:k * P + m], xs3[t % 2][0:m, k * P:(k + 1) * P], ident[0:m, 0:m])
                else:
                    pe.wait_ge(dve_tail, t + 1)
                    uv = u3T[t % 2].rearrange("p (k t) -> p k t", k=KD)
                    wg = [ring[:, slot, :].rearrange("p (k c) -> p k c", k=KD) for slot in GATE_SLOTS]
                    for half in range(2):
                        pe.wait_ge(slot_filled[GATE_SLOTS[half]], 16 * (exp_fills(half) + NE // 2))
                        if m < P:
                            continue
                        for k in range(KD):
                            last = mm(b[:, half * 512:half * 512 + 512], uv[:, k, 0:m], wg[half][:, k, :],
                                      start=(k == 0), stop=(k == KD - 1))
                    if m < P:
                        last = few_rows(b, lambda k: uv[:, k, 0:m],
                                        lambda k, g: wg[g // 2][:, k, g % 2 * 256:g % 2 * 256 + 256], KD)
                last.then_inc(pe_tail, 1)


def small_constants():
    p = np.arange(P, dtype=np.float32)
    lg = np.log(np.float32(1.0) - np.float32(2.0) ** (np.float32(-5.0) - np.arange(H, dtype=np.float32)))
    lg = lg.astype(np.float32)
    inv = np.float32(1.0) / np.float32(10000.0) ** (np.arange(0, P, 2, dtype=np.float32) / np.float32(P))
    pos = np.concatenate([np.arange(SEQ), np.full(NB, PAST)]).astype(np.float32)
    ang = (pos[None, :] * inv.astype(np.float32)[:, None]).astype(np.float32)
    cos = np.cos(ang).astype(np.float32)
    sin = np.sin(ang).astype(np.float32)
    diff = np.arange(SEQ)[None, :] - np.arange(P)[:, None]
    decay = np.stack([np.where(diff >= 0, np.exp(np.float64(g) * np.maximum(diff, 0)), 0.0) for g in lg], 1) * SCALE
    left = (SEQ - 1 - np.arange(SEQ)).reshape(4, P).T
    kdec = np.stack([np.exp(np.float64(g) * left) for g in lg], 1) * SCALE
    token = np.zeros((P, NT), np.float32)
    for t, (r0, m) in enumerate(TILES):
        token[:m, t] = r0 + np.arange(m) + 1
    valp = np.stack([np.where(token > 0, (token - 1) * 2 + k + 1, 0) for k in range(2)], 1)
    c = dict(
        kdec=kdec.reshape(P, 16), gam=np.tile(np.exp(lg.astype(np.float64)), (P, 1)),
        desc4=np.tile(np.arange(NG, 0, -1), (P, 1)), desc8=np.tile(np.arange(EPG, 0, -1), (P, 1)),
        thr=np.tile(np.arange(1, 9) * ROWS, (P, 1)),
        live=token > 0, valp=valp.reshape(P, 10), half=(np.arange(P) // 64).reshape(P, 1),
        nh2=(np.arange(P) // 64 - 2).reshape(P, 1), eps=np.full((P, 1), EPS), io48=np.tile(np.arange(NTILE), (P, 1)))
    c = {k: x.astype(np.float32) for k, x in c.items()}
    big = dict(
        cos=np.concatenate([cos, cos]), sin=np.concatenate([-sin, sin]),
        decay=decay.reshape(P, H * SEQ).astype(np.float32), ident=np.eye(P, dtype=np.float32),
        meanw=np.full((P, P), 1.0 / P, np.float32),
        lt16=np.stack([(p[:, None] < p[None, :]), np.ones((P, P))], 1).astype(np.float16),
        io128=np.tile(np.arange(P) % ROWS, (P, 1)).astype(np.float32),
        io32=np.tile(np.arange(NE), (P, 1)).astype(np.float32),
        io16=np.tile(np.arange(OVER), (P, 1)).astype(np.float32))
    return c, big


def columns(vector):
    return np.ascontiguousarray(vector.reshape(-1, P).T)


def k_major(w, width):
    k, n = w.shape
    return np.ascontiguousarray(w.reshape(k // P, P, n // width, width).transpose(2, 1, 0, 3).reshape(
        n // width, P, (k // P) * width))


def layout(i):
    c, arrays = small_constants()
    g = lambda name: np.asarray(i[name])
    c["gmix"], c["gple"] = columns(g("g_mix")[0]), columns(g("g_ple")[0])
    c["convw"] = g("conv_w")[0].reshape(3, CC, P).transpose(2, 1, 0).reshape(P, 12)
    c["gn"] = columns(g("ret_gn")[0])
    bias = np.concatenate([g("b_router_group")[0], g("b_router_expert")[0].reshape(-1)])
    c["bias"] = np.broadcast_to(bias, (P, NR))
    order = ["gmix", "gple", "convw", "gn", "kdec", "gam", "bias", "desc4", "desc8", "thr", "live", "valp", "half", "nh2",
             "eps", "io48"]
    arrays["small"] = np.ascontiguousarray(np.concatenate([c[k] for k in order], 1))
    arrays["x"] = np.concatenate([g("x_prompt")[0], g("x_sample")[:, 0]], 0)
    arrays["p"] = np.concatenate([g("p_prompt")[0, 0], g("p_sample")[0, :, 0]], 0)
    arrays["state_conv"] = np.ascontiguousarray(g("state_conv")[0])
    arrays["state_ret"] = np.ascontiguousarray(g("state_ret")[0])
    w_in = k_major(g("w_in")[0], P).reshape(WIN_UNITS, 4, P, D).transpose(0, 2, 1, 3).reshape(WIN_UNITS, P, UNIT)
    arrays["w_in"] = np.ascontiguousarray(w_in[[3, 4, 5, 6, 1, 2, 0]])
    arrays["w_o"] = k_major(g("w_o")[0], 512)
    arrays["w_ple_gate"] = k_major(g("w_ple_gate")[0], 512)
    arrays["w_ple_proj"] = k_major(g("w_ple_proj")[0], D)[0]
    w_r = np.concatenate([g("w_router_group")[0], g("w_router_expert")[0]], 1)
    arrays["w_r"] = np.ascontiguousarray(w_r.reshape(KD, P, NR).transpose(1, 0, 2))
    exp = np.empty((NE, 3, P, UNIT), np.float32)
    gu = exp[:, :2].reshape(NE, 2, P, KD, 2, 256)
    for s, name in enumerate(("w_gate", "w_up")):
        gu[:, :, :, :, s, :] = g(name)[0].reshape(NE, KD, P, 2, 256).transpose(0, 3, 2, 1, 4)
    exp[:, 2] = g("w_down")[0].reshape(NE, 4, P, D).transpose(0, 2, 1, 3).reshape(NE, P, UNIT)
    arrays["w_exp"] = exp.reshape(NE * 3, P, UNIT)
    arrays["g_ffn"] = g("g_ffn")
    arrays["g_final"] = g("g_final").reshape(1, D)
    return arrays


OUTS = dict(y=(T, D), conv_p=(2, 512), ret_p=(H, P, P), conv_s=(NB, 2, 512), ret_s=(NB, H, P, P))


def kernel(**inputs):
    import concourse.bacc as bacc
    from concourse.bass_utils import run_bass_kernel_spmd

    nc = bacc.Bacc("TRN2", target_bir_lowering=False, num_devices=1)
    arrays = {f"in_{k}": v for k, v in layout(inputs).items()}
    ins = {k[3:]: nc.dram_tensor(k, v.shape, mybir.dt.from_np(v.dtype), kind="ExternalInput").ap()
           for k, v in arrays.items()}
    outs = {k: nc.dram_tensor(f"out_{k}", s, F32, kind="ExternalOutput").ap() for k, s in OUTS.items()}
    build(nc, ins, outs)
    r = run_bass_kernel_spmd(nc, [arrays], core_ids=[0]).results[0]
    y = r["out_y"]
    return (y[:SEQ].reshape(1, SEQ, D), y[SEQ:].reshape(NB, 1, D), r["out_conv_p"].reshape(1, 1, 2, 512),
            r["out_ret_p"].reshape(1, 1, H, P, P), r["out_conv_s"].reshape(1, NB, 2, 512),
            r["out_ret_s"].reshape(1, NB, H, P, P))
```

```python
from contextlib import ExitStack

import numpy as np

import concourse.bass as bass
from concourse import mybir

F32 = mybir.dt.float32
F32R = mybir.dt.float32r
F16 = mybir.dt.float16
I32 = mybir.dt.int32
ALU = mybir.AluOpType
ACT = mybir.ActivationFunctionType
AX = mybir.AxisListType

P = 128
D = 1024
KD = D // P
SEQ = 512
NB = 8
T = SEQ + NB
HALF = T // 2
TILES = [(t * P, min(P, T - t * P)) for t in range(5)]
NT = len(TILES)
PAST = 4096
H = 4
CC = 4
WIN_UNITS = 7
NG, EPG = 4, 8
NE = NG * EPG
NR = NG + NE
FF = 512
PLE = 256
EPS = 1e-6
ROWS = 64
OVER = 2 * T // ROWS
NTILE = NE + OVER
NOWHERE = 4096.0
RING = 6
UNIT = 4096
SCALE = float(P) ** -0.5


def job_list():
    jobs = [("buf", 0)] + [("x", t) for t in range(NT)]
    jobs += [(kind, h) for kind in "qv" for h in range(H)]
    for h, t in enumerate((NT - 1, 0, 1, 2)):
        jobs += [("k", h), ("vt", t)]
    jobs += [("g", 0), ("vt", 3)]
    jobs += [("vb", 0), ("g", 1), ("vb", 1), ("vb", 2), ("vb", 3), ("g", 2), ("so", 0), ("g", 3)]
    jobs += [("vb", b) for b in range(4, NB)]
    for s in range(H):
        jobs += [("scA", s), ("scB", s), ("kt", s)]
        if s < 2:
            jobs.append((("so", 1), ("ot", 0))[s])
        if s >= 1:
            jobs += [("pv", s - 1), ("st", s - 1)]
        if s >= 2:
            jobs.append(("mn", s - 2))
        if s >= 3:
            jobs.append(("vr", s - 3))
    conv = iter([(k, c) for c in range(CC) for k in ("gc", "hc", "gb")])
    jobs += [("pv", 3), ("st", 3)]
    for job in (("mn", 2), ("vr", 1), ("mn", 3), ("vr", 2), ("vr", 3)):
        jobs += [next(conv), job]
    jobs += list(conv)
    jobs += [("wo", 0), ("wo", 4), ("co", 0), ("wo", 1), ("xt", 0), ("xt", 4), ("wo", 2), ("xt", 1), ("wo", 3),
             ("xt", 2), ("rt", 0), ("xt", 3), ("rt", 1), ("lg", 0), ("pt", 0), ("pt", 1), ("pp", 0),
             ("tot", 0), ("rk", 0), ("pp", 1), ("pp", 2), ("ix", 0), ("pp", 3), ("pp", 4)]
    return jobs


READERS = dict(buf="D", x="D", q="AD", k="AD", v="A", vt="A", g="A", vb="D", so="D", ot="D", scA="D", scB="D", kt="D", pv="A",
               st="A", mn="DA", vr="AD", gc="A", hc="D", gb="D", co="A", wo="D", xt="A", rt="A", lg="D",
               pt="A", pp="A", rk="D", tot="D", ix="D", u="D", pa="A", pb="A", pg="A")
JOBS = job_list()
CHUNKS = [j for j in JOBS if j[0] in ("q", "k", "v", "g", "gc", "hc", "gb")]
UNIT_OF = dict(q=0, v=1, k=2, g=3, gc=4, hc=5, gb=6)
TAIL_TILES = [NT - 1] + list(range(NT - 1))
TAIL = [("u", 0), ("u", 1), ("pg", 0)]
for _n in range(1, NT):
    TAIL += [("pa", _n)] + ([("u", _n + 1)] if _n + 1 < NT else []) + [("pb", _n)]
GATES = [_job for _job in TAIL if _job[0] != "u"]


def gates(n):
    return sum(_job[1] < n for _job in GATES)


class Plan:

    def __init__(self, jobs):
        self.jobs = jobs
        self.at = {j: n for n, j in enumerate(jobs)}

    def pe(self, job):
        return self.at[job] + 1

    def count(self, engine, n):
        return sum(engine in READERS[k] for k, _ in self.jobs[:n + 1])

    def done(self, engine, job):
        return self.count(engine, self.at[job])

    def free(self, n):
        return (self.jobs[n - 4], READERS[self.jobs[n - 4][0]]) if n >= 4 else (None, "")


HEAD, REST = Plan(JOBS), Plan(TAIL)
WO_HIGH = {("hc", 2): (0,), ("gb", 2): (1,), ("hc", 3): (2, 3)}
HEAD_SLOT = [0, 1, 2, 3, 0, 1, 2, 3, 0]
FIRST_SLOTS, SECOND_SLOTS, PAIR_SLOTS = [4, 5, 1, 2, 3, 0], [None, None, 1, 4, 5, 0], [2, 3, 1, 4, 5, 0]
GATE_SLOTS = PAIR_SLOTS[0:2]
WO_PARTS = ((UNIT // 2, UNIT), (0, UNIT // 2))
WO_ORDER = [0, 4, 1, 2, 3]


def build(nc, a, o):
    y_rows = nc.dram_tensor("y_rows", [2 * T, D], F32, kind="Internal").ap()
    xn_rows = nc.dram_tensor("xn_rows", [T, D], F32, kind="Internal").ap()
    y_half = y_rows.rearrange("r (n c) -> (r n) c", n=2)
    xn_half = xn_rows.rearrange("r (n c) -> (r n) c", n=2)
    y_tok = y_rows.rearrange("(t k) c -> t (k c)", k=2)

    with ExitStack() as ctx:
        def sb(name, shape, dt=F32):
            return ctx.enter_context(nc.sbuf_tensor(name, shape, dt))

        def sem(name):
            return ctx.enter_context(nc.semaphore(name))

        ps = ctx.enter_context(nc.psum_tensor("ps", [P, 8, 512], F32))
        psf = ps[:, :, :].rearrange("p b c -> p (b c)")

        def pair(n):
            return psf[:, (n % 4) * 1024:(n % 4) * 1024 + 1024]

        def halves(ap):
            return ap.rearrange("p (b c) -> p b c", b=2)[:, :, 0:HALF]

        ring_at = -(-nc.sbuf_base // 32) * 32
        arena = sb("arena", [P, RING * UNIT + 64])
        ring = arena[:, 0:RING * UNIT].rearrange("p (s c) -> p s c", s=RING)
        xh = sb("xh", [P, NT, D])
        region_u_at = -(-nc.sbuf_base // 32) * 32
        region_u = sb("region_u", [P, KD * T])
        region_m_at = -(-nc.sbuf_base // 32) * 32
        region_m = sb("region_m", [P, KD * T])
        region_q_at = -(-nc.sbuf_base // 32) * 32
        region_q = sb("region_q", [P, 12 * T])
        region_v_at = -(-nc.sbuf_base // 32) * 32
        region_v = sb("region_v", [P, NT * 512])
        region_z_at = -(-nc.sbuf_base // 32) * 32
        region_z = sb("region_z", [P, 2128])
        cos_t = sb("cos_t", [P, T])
        sin_t = sb("sin_t", [P, T])
        region_d = sb("region_d", [P, H * SEQ])
        ident = sb("ident", [P, P])
        meanw = sb("meanw", [P, P])
        w_r = sb("w_r", [P, KD, NR])
        small = sb("small", [P, 256])
        stats = sb("stats", [P, 48])
        conv_hist = sb("conv_hist", [P, CC, NB, 2])
        new_z = sb("new_z", [P, CC, 10])
        wk = sb("wk", [P, NT, 2])
        index = sb("index", [P, 2 * NTILE], I32)
        over_expert = sb("over_expert", [1, OVER + 1], I32)
        gcol = sb("gcol", [P, 2], I32)
        scol = sb("scol", [P, 2], I32)

        cuts = dict(gmix=8, gffn=8, gple=8, convw=12, gn=4, kdec=16, gam=4, bias=36, desc4=4, desc8=8, thr=8, live=5,
                    valp=10, half=1, nh2=1, eps=1, io48=NTILE)
        at, col = 0, {}
        for name, width in cuts.items():
            col[name] = small[:, at:at + width]
            at += width
        assert at <= 256

        uT = region_u[:, :].rearrange("p (k t) -> p k t", k=KD)
        def at_r(name, n, offset):
            return nc.alloc_sbuf_tensor_at(name, [P, n], F32R, offset=offset)

        u_hi = at_r("u_hi", KD * T, region_u_at)[:, :].rearrange("p (k t) -> p k t", k=KD)
        high = ring_at + 4 * UNIT * 4
        u_lo = at_r("u_lo", KD * T, high)[:, :].rearrange("p (k t) -> p k t", k=KD)
        high += KD * T * 4
        w_hi = [at_r(f"w_hi{i}", D, high + i * D * 4)[:, :] for i in range(2)]
        w_lo = [at_r(f"w_lo{i}", D, high + (2 + i) * D * 4)[:, :] for i in range(2)]
        wo_hi = [at_r("wo_hi0", UNIT, region_q_at)[:, :], at_r("wo_hi1", UNIT, ring_at + UNIT * 4)[:, :]]
        wo_lo = [at_r(f"wo_lo{i}", UNIT, ring_at + HEAD_SLOT[WIN_UNITS + i] * UNIT * 4)[:, :] for i in range(2)]
        ret_hi = at_r("ret_hi", H * T, region_v_at)[:, :]
        conv_hi = at_r("conv_hi", CC * T, region_q_at + 8 * T * 4)[:, :]
        mix_few = region_v[:, H * T:H * T + KD * NB].rearrange("p (k t) -> p k t", k=KD)
        mix_lo = at_r("mix_lo", KD * T, region_m_at)[:, :]
        gate_hi = [at_r(f"gate_hi{i}", UNIT, ring_at + slot * UNIT * 4)[:, :]
                   for i, slot in enumerate(PAIR_SLOTS[3:5])]
        gate_lo = [at_r("gate_lo0", UNIT, ring_at + UNIT * 4)[:, :], None]
        gate_lo_1 = [at_r("gate_lo10", UNIT // 2, region_z_at)[:, :],
                     at_r("gate_lo11", UNIT // 2, region_m_at + UNIT // 2 * 4)[:, :]]
        u3_hi = [at_r(f"u3_hi{i}", D, ring_at + i * D * 4)[:, :] for i in range(2)]
        u3_lo = [at_r(f"u3_lo{i}", D, ring_at + (2 + i) * D * 4)[:, :] for i in range(2)]
        mixT = region_m[:, :].rearrange("p (k t) -> p k t", k=KD)
        qk = region_q[:, 0:8 * T].rearrange("p (h t) -> p h t", h=8)
        gT = region_q[:, 8 * T:12 * T].rearrange("p (h t) -> p h t", h=4)
        pp = region_q[:, 0:NT * D].rearrange("p (t c) -> p t c", t=NT)
        v_rows = region_v[:, :].rearrange("p (t c) -> p t c", t=NT)
        xs = [region_m[:, i * D:(i + 1) * D] for i in range(2)]
        junk = region_q[:, 0:D]
        u_tmp = [region_q[:, (1 + i) * D:(2 + i) * D] for i in range(2)]
        vT = region_m[:, 0:4 * T].rearrange("p (h t) -> p h t", h=H)
        buf_rows = region_v[0:16, 0:512]
        rot = [region_z[:, i * T:(i + 1) * T] for i in range(2)]
        state = [region_m[:, 4 * T + i * 512:4 * T + (i + 1) * 512] for i in range(4)]
        kv_tmp = region_z[:, 1280:1792]
        masked = [region_z[:, 0:1280], region_m[:, 0:1280]]
        kd = [region_z[:, 1280:1792], region_m[:, 1280:1792]]
        q_mask = region_z[:, 1792:1792 + H * NB * NB].rearrange("p (h n) -> p h n", h=H)
        o_few = sin_t[0:NB, 0:H * P]
        decay = region_d[:, :].rearrange("p (h r) -> p h r", h=H)
        gate_c = [region_z[:, i * T:(i + 1) * T] for i in range(2)]
        zc = [region_z[:, 1040 + i * 538:1040 + (i + 1) * 538] for i in range(2)]
        xn = [region_z[:, i * D:(i + 1) * D] for i in range(2)]
        g_ffn_b = region_d[:, 0:D]
        g_fin_b = region_d[:, D:2 * D]
        p_rows = region_v[:, 0:NT * PLE].rearrange("p (t c) -> p t c", t=NT)
        pT = region_v[:, NT * PLE:NT * PLE + 2 * T].rearrange("p (k t) -> p k t", k=2)
        st_out = cos_t[:, 0:512].rearrange("p (h e) -> p h e", h=H)
        co_out = sin_t[0:10, 0:512]

        cursor = [0]

        def scratch(n, dt=F32):
            words = n if dt == F32 else (n + 1) // 2
            ap = region_m[:, cursor[0]:cursor[0] + words]
            cursor[0] += words
            if dt != F32:
                ap = ap.bitcast(dt)
            return ap

        log_t = scratch(T)[0:NR, :]
        logit = scratch(NT * NR).rearrange("p (t c) -> p t c", t=NT)
        w4 = [scratch(NT * NG).rearrange("p (t c) -> p t c", t=NT) for _ in range(3)]
        w8 = [scratch(NT * EPG).rearrange("p (t c) -> p t c", t=NT) for _ in range(5)]
        w1 = [scratch(NT).rearrange("p (t c) -> p t c", t=NT) for _ in range(6)]
        w32 = scratch(NT * NE).rearrange("p (t c) -> p t c", t=NT)
        pick = scratch(2 * NT * NE).rearrange("p (k t e) -> p k t e", k=2, t=NT)
        w64 = scratch(2 * NT * NE).rearrange("p (k t e) -> p k t e", k=2, t=NT)
        rank = scratch(NT * NE).rearrange("p (t c) -> p t c", t=NT)
        chosen = scratch(NT * NE, dt=F16).rearrange("p (t c) -> p t c", t=NT)
        total = scratch(NE)
        over8 = scratch(NE * 8).rearrange("p (e c) -> p e c", c=8)
        scan = [scratch(16 + NE) for _ in range(2)]
        over_n = scratch(NE)
        sel = [scratch(NT * 2) for _ in range(4)]
        sel8 = scratch(NT * 2 * 8).rearrange("p (n c) -> p n c", c=8)
        ovx = scratch(OVER * NE)[0:1, :].rearrange("p (n e) -> p n e", e=NE)
        ovc = scratch(OVER + 1)[0:1, :]
        row_hot = region_u[:, 1024:1664].bitcast(F16).rearrange("p (n c) -> p n c", c=P)
        tile_hot = region_u[:, 1664:1904].bitcast(F16).rearrange("p (n c) -> p n c", c=NTILE)
        ixf = [scratch(2 * NTILE) for _ in range(2)]
        io128 = scratch(P)
        io32 = scratch(NE)
        lt16 = scratch(2 * P, dt=F16).rearrange("p (s c) -> p s c", s=2)
        io16 = scratch(OVER)
        spare_m = KD * T - 512
        assert cursor[0] <= spare_m, cursor[0]

        moe = 0
        xg, xgT, hs, sg, hT = [], [], [], [], []
        for lst, width in ((xg, 512), (xgT, 512), (sg, 256), (hs, 256), (hT, 256)):
            for _ in range(2):
                lst.append(region_u[:, moe:moe + width])
                moe += width
        assert moe <= KD * T
        out_sb = [region_v[:, i * 512:(i + 1) * 512] for i in range(2)]

        spare = [[(region_d[:, 0:1024], (0, 1024)), (region_q[:, NT * D:NT * D + 1024], (1024, 2048)),
                  (region_m[:, spare_m:spare_m + 512], (2048, 2560)), (region_u[:, 3584:4096], (2560, 3072)),
                  (cos_t[:, 0:512], (3072, 3584)), (sin_t[:, 0:512], (3584, 4096))],
                 [(region_m[:, 0:512], (0, 512)), (region_z[:, 0:2048], (512, 2560)),
                  (region_v[:, 1024:2560], (2560, 4096))]]
        y_buf = [region_v[:, 0:2048], region_m[:, 0:2048]]
        u3T = [region_u[:, i * D:(i + 1) * D] for i in range(2)]
        gate = [region_u[:, 2 * D + i * D:3 * D + i * D] for i in range(2)]

        def gate_low(half, k):
            part, at = (gate_lo[0], k * 512) if half == 0 else (gate_lo_1[k // 4], k % 4 * 512)
            return part[:, at:at + 512]


        slot_filled = [sem(f"slot_filled{i}") for i in range(RING)]
        x_loaded = [sem(f"x_loaded{i}") for i in range(NT)]
        first_chunk = [sem(f"first_chunk{i}") for i in range(4)]
        pp_loaded = sem("pp_loaded")
        rope_loaded = sem("rope_loaded")
        w_hi_ready, w_lo_ready = sem("w_hi_ready"), sem("w_lo_ready")
        u_split = sem("u_split")
        small_loaded, consts_loaded = sem("small_loaded"), sem("consts_loaded")
        decay_loaded = sem("decay_loaded")
        state_loaded = [sem(f"state_loaded{i}") for i in range(4)]
        state_scaled = sem("state_scaled")
        state_stored = [sem(f"state_stored{i}") for i in range(4)]
        late_loaded, p_loaded = sem("late_loaded"), sem("p_loaded")
        wo_hi_ready, wo_lo_ready, ret_hi_ready, mix_split = (
            sem("wo_hi_ready"), [sem(f"wo_lo{i}_ready") for i in range(2)], sem("ret_hi_ready"), sem("mix_split"))
        route_loaded = sem("route_loaded")
        xn_stored = [sem(f"xn_stored{i}") for i in range(2)]
        misc_stored = sem("misc_stored")
        root_done = sem("root_done")
        rstd_done = sem("rstd_done")
        xs_done = sem("xs_done")
        act_step = sem("act_step")
        dve_step = sem("dve_step")
        pool_step = sem("pool_step")
        pool_turn, sp_turn = sem("pool_turn"), sem("sp_turn")
        pe_jobs, act_jobs, dve_jobs = sem("pe_jobs"), sem("act_jobs"), sem("dve_jobs")
        half_copied = sem("half_copied")
        h_done, ffn_root_done = sem("h_done"), sem("ffn_root_done")
        lg_ready, ex_done = sem("lg_ready"), sem("ex_done")
        chosen_done, hot_done, index_done = sem("chosen_done"), sem("hot_done"), sem("index_done")
        route_done = sem("route_done")
        spare_loaded = [sem(f"spare_loaded{i}") for i in range(2)]
        xg_cleared = sem("xg_cleared")
        xg_loaded = [sem(f"xg_loaded{i}") for i in range(2)]
        out_stored = [sem(f"out_stored{i}") for i in range(2)]
        xt_done, xgT_ready, gu_done, silu_done = sem("xt_done"), sem("xgT_ready"), sem("gu_done"), sem("silu_done")
        hs_done, ht_done, hT_ready, down_done, out_ready = (
            sem("hs_done"), sem("ht_done"), sem("hT_ready"), sem("down_done"), sem("out_ready"))
        ov = {n: sem("over_" + n) for n in ("w", "xg", "xt", "xgT", "gu", "silu", "hs", "ht", "hT", "down", "out",
                                            "stored")}
        y_loaded = [sem(f"y_loaded{i}") for i in range(2)]
        hy_done, hy_root, hy_rstd = sem("hy_done"), sem("hy_root"), sem("hy_rstd")
        gate_hi_ready, gate_lo_ready = sem("gate_hi_ready"), sem("gate_lo_ready")
        u3_ready, u3_hi_ready = sem("u3_ready"), sem("u3_hi_ready")
        pe_tail, act_tail, dve_tail = sem("pe_tail"), sem("act_tail"), sem("dve_tail")
        f_done, f_root, y_done, y_stored = sem("f_done"), sem("f_root"), sem("y_done"), sem("y_stored")

        def head_slot(n):
            return ring[:, HEAD_SLOT[n], :]

        def head_wait(eng, n):
            eng.wait_ge(slot_filled[HEAD_SLOT[n]], 16 * HEAD_SLOT[1:n + 1].count(HEAD_SLOT[n]))

        def chunk_of(n):
            kind, c = CHUNKS[n]
            return head_slot(UNIT_OF[kind])[:, c * D:(c + 1) * D]

        def pair_fill(i, j):
            slots = (FIRST_SLOTS, SECOND_SLOTS)[i] if isinstance(i, int) and i < 2 else PAIR_SLOTS
            slot = slots[j]
            fills = HEAD_SLOT[1:].count(slot) + 1 - int(slots is PAIR_SLOTS and slot in GATE_SLOTS)
            return slot, i * 16 + 16 * fills

        U_O = WIN_UNITS
        OVER_SLOTS = PAIR_SLOTS[2:5]
        w_pp = ring[:, FIRST_SLOTS[5], 0:2 * D]

        block = ctx.enter_context(nc.Block())

        @block.sync
        def _(sp):
            for t, (r0, m) in enumerate(TILES):
                sp.dma_start(xh[0:m, t, :], a["x"][r0:r0 + m, :]).then_inc(x_loaded[t], 16)
            for c in range(4):
                sp.dma_start(head_slot(0)[:, c * D:(c + 1) * D], a["w_in"][0, :, c * D:(c + 1) * D]).then_inc(
                    first_chunk[c], 16)
            sp.dma_start(cos_t[:, :], a["cos"]).then_inc(rope_loaded, 16)
            sp.dma_start(sin_t[:, :], a["sin"]).then_inc(rope_loaded, 16)
            for n in range(1, len(HEAD_SLOT)):
                before = [m for m in range(n) if HEAD_SLOT[m] == HEAD_SLOT[n]]
                if before:
                    last = max(i for i, (kind, _) in enumerate(CHUNKS) if UNIT_OF[kind] == before[-1])
                    sp.wait_ge(w_lo_ready, last + 1)
                src = a["w_in"][n] if n < WIN_UNITS else a["w_o"][n - WIN_UNITS]
                sp.dma_start(head_slot(n), src).then_inc(slot_filled[HEAD_SLOT[n]], 16)
            def load_first(*units):
                for j in units:
                    slot = FIRST_SLOTS[j]
                    sp.dma_start(ring[:, slot, :], a["w_exp"][j]).then_inc(slot_filled[slot], 16)

            sp.wait_ge(pe_jobs, HEAD.pe(CHUNKS[-1]))
            load_first(0, 1, 3)
            sp.wait_ge(pe_jobs, HEAD.pe(("wo", WO_ORDER[-1])))
            sp.wait_ge(route_loaded, 16 * 4)
            sp.dma_start(w_pp, a["w_ple_proj"]).then_inc(pp_loaded, 16)
            load_first(2, 4)
            for i in range(2):
                if i == 0:
                    sp.wait_ge(pe_jobs, HEAD.pe(("rt", 1)))
                    sp.wait_ge(dve_jobs, HEAD.done("D", ("wo", WO_ORDER[-1])))
                    sp.wait_ge(misc_stored, 16 * 4)
                else:
                    sp.wait_ge(pe_jobs, HEAD.pe(JOBS[-1]))
                    load_first(5)
                    sp.wait_ge(route_done, 1)
                    sp.wait_ge(xn_stored[0], 16 * 3)
                    sp.wait_ge(xn_stored[1], 16 * 2)
                for ap, (c0, c1) in spare[i]:
                    sp.dma_start(ap, a["w_exp"][6 + i, :, c0:c1]).then_inc(spare_loaded[i], 16)
            for j in (3, 4, 2, 5):
                sp.wait_ge(*{3: (gu_done, 1), 4: (gu_done, 1), 2: (down_done, 1), 5: (down_done, 2)}[j])
                slot = SECOND_SLOTS[j]
                sp.dma_start(ring[:, slot, :], a["w_exp"][6 + j]).then_inc(slot_filled[slot], 16)

            def load_pair(i):
                for j in range(6):
                    slot = PAIR_SLOTS[j]
                    if isinstance(i, int) and j < 2:
                        sp.wait_ge(gu_done, 2)
                    else:
                        sp.wait_ge(down_done if j % 3 == 2 else gu_done, i * 2 + (j // 3 - 1))
                    src = a["w_exp"][bass.ds(i * 6 + j, 1)].rearrange("a p c -> (a p) c")
                    sp.dma_start(ring[:, slot, :], src).then_inc(slot_filled[slot], 16)

            load_pair(2)
            with sp.Fori(3, NE // 2) as i:
                load_pair(i)
            for n, slot in enumerate(GATE_SLOTS):
                sp.wait_ge(gu_done, NE - 1)
                sp.dma_start(ring[:, slot, :], a["w_ple_gate"][n]).then_inc(slot_filled[slot], 16)

            sp.wait_ge(index_done, 1)
            sp.wait_ge(down_done, NE)
            n_over = sp.value_load(over_expert[0:1, OVER:OVER + 1], min_val=0, max_val=OVER)
            with sp.If(n_over > 0):
                with sp.Fori(0, OVER) as q:
                    e = sp.value_load(over_expert[0:1, bass.ds(q, 1)], min_val=0, max_val=NE - 1)
                    for j in range(3):
                        src = a["w_exp"][bass.ds(e * 3 + j, 1)].rearrange("a p c -> (a p) c")
                        sp.dma_start(ring[:, OVER_SLOTS[j], :], src).then_inc(ov["w"], 16)
                    sp.wait_ge(ov["down"], q + 1)
                    sp.sem_inc(sp_turn, 1)
                sp.wait_ge(ov["stored"], 16 * OVER)
            with sp.Else():
                sp.wait_ge(index_done, 1)

            sp.wait_ge(out_stored[0], 16 * (NE // 2))
            sp.wait_ge(out_stored[1], 16 * (NE // 2))
            for n, t in enumerate(TAIL_TILES):
                r0, m = TILES[t]
                if n >= 2:
                    sp.wait_ge(hy_done, n - 1)
                sp.dma_start(y_buf[n % 2][0:m, :], y_tok[r0:r0 + m, :]).then_inc(y_loaded[n % 2], 16)
            for n, t in enumerate(TAIL_TILES):
                r0, m = TILES[t]
                sp.wait_ge(y_done, n + 1)
                sp.dma_start(o["y"][r0:r0 + m, :], xh[0:m, t, :]).then_inc(y_stored, 16)
            sp.wait_ge(y_stored, 16 * NT)
            sp.wait_ge(misc_stored, 16 * 4)
            for i in range(4):
                sp.wait_ge(state_stored[i], 32)

        @block.gpsimd
        def _(pool):
            def load_state(b):
                if b >= 4:
                    pool.wait_ge(state_stored[b % 4], 16 * (b // 4))
                    pool.wait_ge(pe_jobs, HEAD.pe(("so", 0)))
                pool.dma_start(state[b % 4].rearrange("p (h e) -> p h e", h=H), a["state_ret"][b].rearrange(
                    "h d e -> d h e")).then_inc(state_loaded[b % 4], 16)

            def low_half(n):
                pool.wait_ge(w_hi_ready, n + 1)
                if n >= 2:
                    pool.wait_ge(pe_jobs, HEAD.pe(CHUNKS[n - 2]))
                nc.gpsimd.tensor_tensor(w_lo[n % 2], chunk_of(n), w_hi[n % 2], ALU.subtract).then_inc(w_lo_ready, 1)

            gam = col["gam"].unsqueeze(2).to_broadcast([P, H, P])

            def scale_state(b):
                s3 = state[b % 4].rearrange("p (h e) -> p h e", h=H)
                pool.wait_ge(state_loaded[b % 4], 16 * (b // 4 + 1))
                nc.gpsimd.tensor_tensor(s3, s3, gam, ALU.mult).then_inc(state_scaled, 1)

            def store_state(b):
                pool.wait_ge(dve_jobs, HEAD.done("D", ("vb", b)))
                pool.dma_start(o["ret_s"][b].rearrange("h d e -> d h e"),
                               state[b % 4].rearrange("p (h e) -> p h e", h=H)).then_inc(state_stored[b % 4], 16)

            for n in range(len(CHUNKS)):
                low_half(n)
                if n < 4:
                    load_state(n)
                if n == 4:
                    pool.wait_ge(small_loaded, 16)
                if 4 <= n < 8:
                    scale_state(n - 4)
                if n == 14:
                    for b in range(4):
                        store_state(b)
                if n == 15:
                    for b in range(4, NB):
                        load_state(b)
                    for b in range(4, NB):
                        scale_state(b)
                if n == 17:
                    for b in range(4, NB):
                        store_state(b)

            for q in range(2):
                at = slice(*WO_PARTS[q])
                pool.wait_ge(wo_hi_ready, 3 + q)
                nc.gpsimd.tensor_tensor(wo_lo[1][:, at], head_slot(U_O + 1)[:, at], wo_hi[1][:, at],
                                        ALU.subtract).then_inc(wo_lo_ready[1], 1)

            pool.wait_ge(dve_jobs, HEAD.done("D", ("scB", H - 1)))
            pool.dma_start(g_ffn_b, a["g_ffn"].to_broadcast([P, D])).then_inc(late_loaded, 16)
            pool.dma_start(g_fin_b, a["g_final"].to_broadcast([P, D])).then_inc(late_loaded, 16)
            pool.wait_ge(act_jobs, HEAD.done("A", ("st", H - 1)))
            pool.dma_start(o["ret_p"].rearrange("h d e -> d h e"), st_out).then_inc(misc_stored, 16)
            pool.dma_start(o["conv_s"][:, 0, :], a["state_conv"][:, 1, :]).then_inc(misc_stored, 16)
            pool.wait_ge(act_jobs, HEAD.done("A", ("co", 0)))
            pool.dma_start(o["conv_p"], co_out[0:2, :]).then_inc(misc_stored, 16)
            pool.dma_start(o["conv_s"][:, 1, :], co_out[2:10, :]).then_inc(misc_stored, 16)
            def store_rows(t):
                r0, m = TILES[t]
                n = WO_ORDER.index(t)
                pool.wait_ge(dve_jobs, HEAD.done("D", ("wo", t)))
                pool.dma_start(xn_rows[r0:r0 + m, :], xn[n % 2][0:m, :]).then_inc(xn_stored[n % 2], 16)

            for t in WO_ORDER[:-1]:
                store_rows(t)
            pool.wait_ge(pe_jobs, HEAD.pe(("wo", WO_ORDER[-1])))
            for dst, name in ((io128, "io128"), (io32, "io32"), (io16, "io16"), (lt16, "lt16")):
                pool.dma_start(dst, a[name]).then_inc(route_loaded, 16)
            pool.dma_start(p_rows[:, 0:4, :], a["p"][0:SEQ].rearrange("(t p) c -> p t c", p=P)).then_inc(p_loaded, 16)
            pool.dma_start(p_rows[0:NB, 4, :], a["p"][SEQ:T]).then_inc(p_loaded, 16)
            store_rows(WO_ORDER[-1])

            pool.wait_ge(pe_jobs, HEAD.pe(("rt", 1)))
            nc.gpsimd.memset(xg[0], 0.0).then_inc(xg_cleared, 1)
            nc.gpsimd.memset(xg[1], 0.0).then_inc(xg_cleared, 1)
            pool.wait_ge(xg_cleared, 2)
            pool.wait_ge(xn_stored[0], 16 * 3)
            pool.wait_ge(xn_stored[1], 16 * 2)
            pool.wait_ge(index_done, 1)

            steps = [0]

            def copied(ins):
                steps[0] += 1
                ins.then_inc(pool_step, 1)
                pool.wait_ge(pool_step, steps[0])

            def start_gather(b, loaded):
                pool.sem_inc(pool_turn, 1)
                pool.indirect_dma_start(out=xg[b], out_offset=None, in_=xn_half,
                                        in_offset=bass.IndirectOffsetOnAxis(ap=gcol[:, b:b + 1], axis=0),
                                        bounds_check=2 * T - 1, oob_is_err=False).then_inc(loaded, 16)

            def start_scatter(b, stored):
                pool.sem_inc(pool_turn, 1)
                pool.indirect_dma_start(out=y_half, out_offset=bass.IndirectOffsetOnAxis(ap=scol[:, b:b + 1], axis=0),
                                        in_=out_sb[b], in_offset=None,
                                        bounds_check=4 * T - 1, oob_is_err=False).then_inc(stored, 16)

            for b in range(2):
                copied(nc.gpsimd.tensor_copy(gcol[:, b:b + 1], index[:, b:b + 1]))
                start_gather(b, xg_loaded[b])

            def pair_of_experts(i, more):
                for b in range(2):
                    e = i * 2 + b
                    if more:
                        pool.wait_ge(xt_done, e + 1)
                        pool.wait_ge(xg_loaded[b], i * 16 + 16)
                        nc.gpsimd.tensor_copy(gcol[:, b:b + 1], index[:, bass.ds(e + 2, 1)]).then_inc(pool_step, 1)
                        pool.wait_ge(pool_step, e * 2 + 3)
                        start_gather(b, xg_loaded[b])
                    if not isinstance(i, int) or i > 0:
                        pool.wait_ge(out_stored[b], i * 16)
                    nc.gpsimd.tensor_copy(scol[:, b:b + 1], index[:, bass.ds(e + NTILE, 1)]).then_inc(pool_step, 1)
                    pool.wait_ge(pool_step, e * 2 + 4 if more else e + NE + 1)
                    pool.wait_ge(out_ready, e + 1)
                    start_scatter(b, out_stored[b])

            pair_of_experts(0, True)
            with pool.Fori(1, NE // 2 - 1) as i:
                pair_of_experts(i, True)
            pair_of_experts(NE // 2 - 1, False)
            base = 2 * NE

            n_over = pool.value_load(over_expert[0:1, OVER:OVER + 1], min_val=0, max_val=OVER)
            with pool.If(n_over > 0):
                pool.wait_ge(out_stored[0], 16 * (NE // 2))
                pool.wait_ge(xg_loaded[0], 16 * (NE // 2))
                with pool.Fori(0, OVER) as q:
                    nc.gpsimd.tensor_copy(gcol[:, 0:1], index[:, bass.ds(q + NE, 1)]).then_inc(pool_step, 1)
                    nc.gpsimd.tensor_copy(scol[:, 0:1], index[:, bass.ds(q + NE + NTILE, 1)]).then_inc(pool_step, 1)
                    pool.wait_ge(pool_step, q * 2 + (base + 2))
                    start_gather(0, ov["xg"])
                    pool.wait_ge(ov["out"], q + 1)
                    start_scatter(0, ov["stored"])
                    pool.wait_ge(ov["stored"], q * 16 + 16)
            with pool.Else():
                pool.wait_ge(index_done, 1)

            for half, dst in enumerate((gate_lo[0][:, 2048:4096], gate_lo_1[1])):
                pool.wait_ge(gate_hi_ready, half + 3)
                nc.gpsimd.tensor_tensor(dst, ring[:, GATE_SLOTS[half], 2048:4096],
                                        gate_hi[half][:, 2048:4096], ALU.subtract).then_inc(gate_lo_ready, 1)

        @block.scalar
        def _(act):
            act.dma_start(small[:, 0:a["small"].shape[1]], a["small"]).then_inc(small_loaded, 16)
            act.dma_start(ident[:, :], a["ident"]).then_inc(consts_loaded, 16)
            act.dma_start(buf_rows, a["state_conv"].rearrange("b r c -> (b r) c")).then_inc(consts_loaded, 16)

            steps = [0]

            def link(ins):
                steps[0] += 1
                ins.then_inc(act_step, 1)
                act.wait_ge(act_step, steps[0])

            eps = col["eps"]
            def high_half(n):
                if n < 4:
                    act.wait_ge(first_chunk[n], 16)
                else:
                    head_wait(act, UNIT_OF[CHUNKS[n][0]])
                if n >= 2:
                    act.wait_ge(pe_jobs, HEAD.pe(CHUNKS[n - 2]))
                    act.wait_ge(w_lo_ready, n - 1)
                nc.scalar.activation(w_hi[n % 2], chunk_of(n), ACT.Copy).then_inc(w_hi_ready, 1)

            def ffn_root(c):
                m, turn = TILES[c][1], WO_ORDER.index(c)
                act.wait_ge(h_done, turn + 1)
                if turn >= 2:
                    act.wait_ge(xn_stored[turn % 2], 16 * (turn // 2))
                link(nc.scalar.activation(xn[turn % 2][0:m, :], xh[0:m, c, :], ACT.Square,
                                          accum_out=stats[0:m, 15 + c:16 + c]))
                nc.scalar.activation(stats[0:m, 20 + c:21 + c], stats[0:m, 15 + c:16 + c], ACT.Sqrt,
                                     scale=1.0 / D, bias=eps[0:m, :]).then_inc(ffn_root_done, 1)

            for t, (r0, m) in enumerate(TILES):
                if t == 0:
                    act.wait_ge(dve_step, 1)
                    link(nc.scalar.activation(stats[:, 40:41], stats[:, 41:42], ACT.Sqrt))
                act.wait_ge(x_loaded[t], 16)
                link(nc.scalar.activation(junk[0:m, :], xh[0:m, t, :], ACT.Square, accum_out=stats[0:m, t:t + 1]))
                if t == 0:
                    act.wait_ge(small_loaded, 16)
                nc.scalar.activation(stats[0:m, 5 + t:6 + t], stats[0:m, t:t + 1], ACT.Sqrt, scale=1.0 / D,
                                     bias=eps[0:m, :]).then_inc(root_done, 1)
                act.wait_ge(rstd_done, t + 1)
                if t >= 2:
                    act.wait_ge(pe_jobs, HEAD.pe(("x", t - 2)))
                nc.scalar.activation(xs[t % 2][0:m, :], xh[0:m, t, :], ACT.Copy,
                                     scale=stats[0:m, 10 + t:11 + t]).then_inc(xs_done, 1)
                if t == 2:
                    high_half(0)

            act.dma_start(region_d[:, :], a["decay"]).then_inc(decay_loaded, 16)
            act.dma_start(meanw[:, :], a["meanw"]).then_inc(decay_loaded, 16)
            act.dma_start(w_r[:, :, :], a["w_r"]).then_inc(decay_loaded, 16)

            high_half(1)
            done = 0
            for n, (kind, c) in enumerate(JOBS):
                chunk = CHUNKS.index((kind, c)) if (kind, c) in CHUNKS else None
                if chunk is not None and chunk + 2 < len(CHUNKS):
                    high_half(chunk + 2)
                if (kind, c) in WO_HIGH:
                    for q in WO_HIGH[(kind, c)]:
                        half, at = q // 2, slice(*WO_PARTS[q % 2])
                        head_wait(act, U_O + half)
                        act.wait_ge(dve_jobs, HEAD.done("D", ("vr", H - 1)))
                        if half:
                            act.wait_ge(w_lo_ready, CHUNKS.index(("hc", CC - 1)) + 1)
                        nc.scalar.activation(wo_hi[half][:, at], head_slot(U_O + half)[:, at],
                                             ACT.Copy).then_inc(wo_hi_ready, 1)
                if kind == "wo" and c != WO_ORDER[-1]:
                    ffn_root(c)
                if "A" not in READERS[kind]:
                    continue
                b = pair(n)
                if (kind, c) == ("pp", 0):
                    for s, w in ((1, w4[0]), (2, w8[3])):
                        act.wait_ge(lg_ready, s)
                        nc.scalar.activation(w, w, ACT.Exp).then_inc(ex_done, 1)
                act.wait_ge(pe_jobs, n + 1)
                if done:
                    act.wait_ge(act_jobs, done)
                done += 1
                if kind in "qk":
                    turn = c if kind == "q" else H + c
                    if turn >= 2:
                        prev = ("q", turn - 2) if turn - 2 < H else ("k", turn - 2 - H)
                        act.wait_ge(dve_jobs, HEAD.done("D", prev))
                    r = rot[turn % 2].rearrange("p (b c) -> p b c", b=2)
                    nc.scalar.activation(r[0:64], halves(b)[64:128], ACT.Copy).then_inc(half_copied, 1)
                    nc.scalar.activation(r[64:128], halves(b)[0:64], ACT.Copy).then_inc(act_jobs, 1)
                elif kind == "v":
                    nc.scalar.activation(vT[:, c, :].rearrange("p (b c) -> p b c", b=2), halves(b),
                                         ACT.Copy).then_inc(act_jobs, 1)
                elif kind == "vt":
                    m = TILES[c][1]
                    nc.scalar.activation(v_rows[0:m, c, :], b[0:m, 0:512], ACT.Copy).then_inc(act_jobs, 1)
                elif kind == "g":
                    nc.scalar.activation(gT[:, c, :].rearrange("p (b c) -> p b c", b=2), halves(b),
                                         ACT.Silu).then_inc(act_jobs, 1)
                elif kind == "pv":
                    nc.scalar.activation(qk[:, c, 0:SEQ], b[:, 0:SEQ], ACT.Copy).then_inc(act_jobs, 1)
                elif kind == "st":
                    act.wait_ge(dve_jobs, HEAD.done("D", ("k", H - 1)))
                    nc.scalar.activation(st_out[:, c, :], b[:, 0:P], ACT.Copy).then_inc(act_jobs, 1)
                elif kind == "mn":
                    act.wait_ge(dve_jobs, HEAD.done("D", ("mn", c)))
                    nc.scalar.activation(qk[:, H + c, :], qk[:, c, :], ACT.Square).then_inc(act_jobs, 1)
                elif kind == "vr":
                    nc.scalar.activation(qk[:, H + c, :].rearrange("p (b c) -> p b c", b=2), halves(b), ACT.Sqrt,
                                         bias=eps).then_inc(act_jobs, 1)
                elif kind == "gc":
                    if c >= 2:
                        act.wait_ge(dve_jobs, HEAD.done("D", ("hc", c - 2)))
                    nc.scalar.activation(gate_c[c % 2].rearrange("p (b c) -> p b c", b=2), halves(b),
                                         ACT.Copy).then_inc(act_jobs, 1)
                    if c == 2:
                        act.wait_ge(dve_jobs, HEAD.done("D", ("vr", H - 1)))
                        act.wait_ge(pe_jobs, HEAD.pe(("st", H - 1)))
                        nc.scalar.activation(ret_hi, region_m[:, CC * T:KD * T], ACT.Copy).then_inc(ret_hi_ready, 1)
                elif kind == "co":
                    nc.scalar.activation(co_out, b[0:10, 0:512], ACT.Copy).then_inc(act_jobs, 1)
                elif kind == "xt":
                    r0, m = TILES[c]
                    nc.scalar.activation(uT[:, :, r0:r0 + m], b.rearrange("p (k t) -> p k t", k=KD)[:, :, 0:m],
                                         ACT.Copy).then_inc(act_jobs, 1)
                    if c == WO_ORDER[-1]:
                        ffn_root(c)
                elif kind == "rt":
                    nc.scalar.activation(log_t[:, c * HALF:(c + 1) * HALF], b[0:NR, 0:HALF],
                                         ACT.Copy).then_inc(act_jobs, 1)
                elif kind == "pt":
                    if c == 0:
                        nc.scalar.activation(pT[:, :, 0:SEQ], b.rearrange("p (k t) -> p k t", k=2),
                                             ACT.Copy).then_inc(act_jobs, 1)
                    else:
                        nc.scalar.activation(pT[:, :, SEQ:T], b[:, 0:2 * NB].rearrange("p (k t) -> p k t", k=2),
                                             ACT.Copy).then_inc(act_jobs, 1)
                elif kind == "pp":
                    m = TILES[c][1]
                    if m == P:
                        nc.scalar.activation(pp[:, c, :], b, ACT.Copy).then_inc(act_jobs, 1)
                    else:
                        for g in range(4):
                            ins = nc.scalar.activation(pp[0:m, c, g * 256:(g + 1) * 256],
                                                       b[32 * g:32 * g + m, 0:256], ACT.Copy)
                        ins.then_inc(act_jobs, 1)

            def evac_rows(b, count, t_done, out_sem):
                act.wait_ge(t_done, count)
                nc.scalar.activation(xgT[b], ps[:, b, :], ACT.Copy).then_inc(out_sem, 1)

            def silu(b, count, g_sem, out_sem):
                act.wait_ge(g_sem, count)
                nc.scalar.activation(sg[b], ps[:, 2 + b, 0:256], ACT.Silu).then_inc(out_sem, 1)

            def evac_out(b, count, d_sem, out_sem):
                act.wait_ge(d_sem, count)
                nc.scalar.activation(out_sb[b], ps[:, 6 + b, :], ACT.Copy).then_inc(out_sem, 1)

            def pair_of_experts(i, first, last):
                for b in range(2):
                    e = i * 2 + b
                    silu(b, e + 1, gu_done, silu_done)
                    if not (last and b == 1):
                        evac_rows(1 - b, e + 2, xt_done, xgT_ready)
                    if not first:
                        act.wait_ge(out_stored[b], i * 16)
                    evac_out(b, e + 1, down_done, out_ready)

            evac_rows(0, 1, xt_done, xgT_ready)
            pair_of_experts(0, True, False)
            with act.Fori(1, NE // 2 - 1) as i:
                pair_of_experts(i, False, False)
            pair_of_experts(NE // 2 - 1, False, True)

            n_over = act.value_load(over_expert[0:1, OVER:OVER + 1], min_val=0, max_val=OVER)
            with act.If(n_over > 0):
                act.wait_ge(out_stored[0], 16 * (NE // 2))
                with act.Fori(0, OVER) as q:
                    evac_rows(0, q + 1, ov["xt"], ov["xgT"])
                    silu(0, q + 1, ov["gu"], ov["silu"])
                    evac_out(0, q + 1, ov["down"], ov["out"])
            with act.Else():
                act.wait_ge(index_done, 1)

            act.wait_ge(out_ready, NE)
            act.wait_ge(down_done, NE)
            for q in range(4):
                half, at = q % 2, slice(q // 2 * 2048, q // 2 * 2048 + 2048)
                act.wait_ge(slot_filled[GATE_SLOTS[half]], pair_fill(NE // 2, half)[1])
                nc.scalar.activation(gate_hi[half][:, at], ring[:, GATE_SLOTS[half], at],
                                     ACT.Copy).then_inc(gate_hi_ready, 1)

            def high_rows(n):
                width = KD * TILES[TAIL_TILES[n]][1]
                act.wait_ge(u3_ready, n + 1)
                if n >= 2:
                    act.wait_ge(pe_tail, REST.pe(GATES[gates(n - 1) - 1]))
                nc.scalar.activation(u3_hi[n % 2][:, 0:width], u3T[n % 2][:, 0:width],
                                     ACT.Copy).then_inc(u3_hi_ready, 1)

            def gate_root(n):
                t = TAIL_TILES[n]
                m = TILES[t][1]
                act.wait_ge(hy_done, n + 1)
                link(nc.scalar.activation(gate[n % 2][0:m, :], xh[0:m, t, :], ACT.Square,
                                          accum_out=stats[0:m, 25 + t:26 + t]))
                nc.scalar.activation(stats[0:m, 30 + t:31 + t], stats[0:m, 25 + t:26 + t], ACT.Sqrt,
                                     scale=1.0 / D, bias=eps[0:m, :]).then_inc(hy_root, 1)

            def final_root(n):
                t = TAIL_TILES[n]
                m = TILES[t][1]
                if n == NT - 1:
                    link(nc.scalar.activation(stats[:, 40:41], eps, ACT.Sqrt))
                act.wait_ge(f_done, gates(n + 1))
                link(nc.scalar.activation(gate[n % 2][0:m, :], xh[0:m, t, :], ACT.Square,
                                          accum_out=stats[0:m, t:t + 1]))
                nc.scalar.activation(stats[0:m, 5 + t:6 + t], stats[0:m, t:t + 1], ACT.Sqrt, scale=1.0 / D,
                                     bias=eps[0:m, :]).then_inc(f_root, 1)

            def sigmoid(kind, n):
                t, b, g = TAIL_TILES[n], pair(REST.at[(kind, n)]), gate[n % 2]
                m = TILES[t][1]
                act.wait_ge(pe_tail, REST.pe((kind, n)))
                act.wait_ge(hy_rstd, n + 1)
                if n >= 2 and kind != "pb":
                    act.wait_ge(f_done, gates(n - 1))
                rstd = stats[0:m, 35 + t:36 + t]
                if m == P:
                    at = slice(0, 512) if kind == "pa" else slice(512, D)
                    nc.scalar.activation(g[:, at], b[:, at], ACT.Sigmoid, scale=rstd).then_inc(act_tail, 1)
                else:
                    for c in range(4):
                        ins = nc.scalar.activation(g[0:m, c * 256:(c + 1) * 256], b[32 * c:32 * c + m, 0:256],
                                                   ACT.Copy)
                    link(ins)
                    nc.scalar.activation(g[0:m, :], g[0:m, :], ACT.Sigmoid, scale=rstd).then_inc(act_tail, 1)

            high_rows(0)
            gate_root(0)
            for n in range(NT):
                if n + 1 < NT:
                    high_rows(n + 1)
                sigmoid("pa" if n else "pg", n)
                if n:
                    final_root(n - 1)
                if n + 1 < NT:
                    gate_root(n + 1)
                if n:
                    sigmoid("pb", n)
            final_root(NT - 1)

        @block.vector
        def _(dve):
            steps = [0]

            def link(ins):
                steps[0] += 1
                ins.then_inc(dve_step, 1)
                dve.wait_ge(dve_step, steps[0])

            V = nc.vector
            link(V.memset(stats[:, :], 1.0))

            def wide(ap, shape):
                return ap.unsqueeze(2).to_broadcast(shape)

            def first_largest(src, top, hot, table, shape):
                link(V.tensor_reduce(top, src, AX.X, ALU.max))
                link(V.tensor_tensor(hot, src, top.to_broadcast(shape), ALU.is_equal))
                link(V.tensor_tensor(hot, hot, table, ALU.mult))
                link(V.tensor_reduce(w1[1], hot, AX.X, ALU.max))
                link(V.tensor_tensor(hot, hot, w1[1].to_broadcast(shape), ALU.is_equal))

            shape4, shape8 = [P, NT, NG], [P, NT, EPG]
            hot_g, hot_1, hot_2, top_g, top_1, top_2 = w4[1], w8[1], w8[2], w1[5], w1[0], w1[2]
            n10 = NT * 2

            def route_choose():
                d4 = col["desc4"].unsqueeze(1).to_broadcast(shape4)
                d8 = col["desc8"].unsqueeze(1).to_broadcast(shape8)
                first_largest(logit[:, :, 0:NG], top_g, hot_g, d4, shape4)
                live = col["live"].unsqueeze(2).to_broadcast(shape4)
                link(V.tensor_tensor(hot_g, hot_g, live, ALU.mult))
                wide_g = hot_g.unsqueeze(3).to_broadcast([P, NT, NG, EPG])
                link(V.tensor_tensor(w32.rearrange("p t (g e) -> p t g e", g=NG),
                                     logit[:, :, NG:NR].rearrange("p t (g e) -> p t g e", g=NG), wide_g, ALU.mult))
                link(V.tensor_reduce(w8[0].unsqueeze(3), w32.rearrange("p t (g e) -> p t e g", g=NG), AX.X, ALU.add))
                first_largest(w8[0], top_1, hot_1, d8, shape8)
                link(V.scalar_tensor_tensor(w8[3], hot_1, -1e30, w8[0], ALU.mult, ALU.add))
                first_largest(w8[3], top_2, hot_2, d8, shape8)
                link(V.tensor_tensor(w8[4], hot_1, hot_2, ALU.add))
                V.tensor_tensor(chosen.rearrange("p t (g e) -> p t g e", g=NG), wide_g,
                                w8[4].unsqueeze(2).to_broadcast([P, NT, NG, EPG]), ALU.mult).then_inc(chosen_done, 1)
                V.tensor_tensor(w4[0], logit[:, :, 0:NG], top_g.to_broadcast(shape4), ALU.subtract).then_inc(lg_ready, 1)
                V.tensor_tensor(w8[3], w8[0], top_1.to_broadcast(shape8), ALU.subtract).then_inc(lg_ready, 1)
                for k, hot in enumerate((hot_1, hot_2)):
                    link(V.tensor_tensor(pick[:, k, :, :].rearrange("p t (g e) -> p t g e", g=NG), wide_g,
                                         hot.unsqueeze(2).to_broadcast([P, NT, NG, EPG]), ALU.mult))
                of_choice(sel[1], io32.unsqueeze(1).unsqueeze(1).to_broadcast([P, 2, NT, NE]))

            def of_choice(out, table):
                link(V.tensor_tensor(w64, pick, table, ALU.mult))
                link(V.tensor_reduce(out.rearrange("p (k t) -> p k t", k=2).unsqueeze(3), w64, AX.X, ALU.add))

            def route_weights():
                dve.wait_ge(ex_done, 2)
                link(V.tensor_reduce(w1[3], w4[0], AX.X, ALU.add))
                link(V.reciprocal(w1[3], w1[3]))
                link(V.tensor_reduce(w1[4], w8[3], AX.X, ALU.add))
                link(V.reciprocal(w1[4], w1[4]))
                link(V.tensor_tensor(w8[3], w8[3], w1[4].to_broadcast(shape8), ALU.mult))
                for top, hot in ((top_1, hot_1), (top_2, hot_2)):
                    link(V.tensor_tensor(w8[4], w8[3], hot, ALU.mult))
                    link(V.tensor_reduce(top, w8[4], AX.X, ALU.add))
                link(V.tensor_tensor(w1[4], top_1, top_2, ALU.add))
                link(V.reciprocal(w1[4], w1[4]))
                link(V.tensor_tensor(w1[4], w1[4], w1[3], ALU.mult))
                link(V.tensor_tensor(wk[:, :, 0:1], top_1, w1[4], ALU.mult))
                V.tensor_tensor(wk[:, :, 1:2], top_2, w1[4], ALU.mult).then_inc(route_done, 1)

            def route_further():
                link(V.tensor_tensor(over8, total.unsqueeze(2).to_broadcast([P, NE, 8]),
                                     col["thr"].unsqueeze(1).to_broadcast([P, NE, 8]), ALU.is_gt))
                link(V.tensor_reduce(over_n.unsqueeze(2), over8, AX.X, ALU.add))
                link(V.tensor_copy(scan[0][:, 16:16 + NE], over_n))
                src, dst = 0, 1
                for s in (1, 2, 4, 8, 16):
                    link(V.tensor_tensor(scan[dst][:, 16:16 + NE], scan[src][:, 16:16 + NE],
                                         scan[src][:, 16 - s:16 + NE - s], ALU.add))
                    src, dst = dst, src
                incl, excl = scan[src][:, 16:16 + NE], scan[dst][:, 0:NE]
                link(V.tensor_tensor(excl, incl, over_n, ALU.subtract))
                of_choice(sel[2], excl.unsqueeze(1).unsqueeze(1).to_broadcast([P, 2, NT, NE]))
                return incl

            def route_places(ranks):
                of_choice(sel[0], ranks)
                link(V.tensor_tensor(sel8, sel[0].unsqueeze(2).to_broadcast([P, n10, 8]),
                                     col["thr"].unsqueeze(1).to_broadcast([P, n10, 8]), ALU.is_ge))
                link(V.tensor_reduce(sel[3].unsqueeze(2), sel8, AX.X, ALU.add))
                link(V.scalar_tensor_tensor(sel[0], sel[3], -float(ROWS), sel[0], ALU.mult, ALU.add))
                link(V.scalar_tensor_tensor(sel[2], sel[3], float(NE - 1), sel[2], ALU.add, ALU.add))
                link(V.tensor_tensor(sel[2], sel[2], sel[1], ALU.subtract))
                link(V.scalar_tensor_tensor(sel[2], sel[3], 0.0, sel[2], ALU.is_gt, ALU.mult))
                link(V.tensor_tensor(sel[2], sel[2], sel[1], ALU.add))
                link(V.tensor_tensor(row_hot, sel[0].unsqueeze(2).to_broadcast([P, n10, P]),
                                     io128.unsqueeze(1).to_broadcast([P, n10, P]), ALU.is_equal))
                link(V.tensor_tensor(tile_hot, sel[2].unsqueeze(2).to_broadcast([P, n10, NTILE]),
                                     col["io48"].unsqueeze(1).to_broadcast([P, n10, NTILE]), ALU.is_equal))
                V.tensor_tensor(tile_hot, tile_hot, col["valp"].unsqueeze(2).to_broadcast([P, n10, NTILE]),
                                ALU.mult).then_inc(hot_done, 1)

            def route_experts(incl):
                link(V.tensor_tensor(ovx, incl[0:1, :].unsqueeze(1).to_broadcast([1, OVER, NE]),
                                     io16[0:1, :].unsqueeze(2).to_broadcast([1, OVER, NE]), ALU.is_le))
                link(V.tensor_reduce(ovc[:, 0:OVER].unsqueeze(2), ovx, AX.X, ALU.add))
                link(V.tensor_scalar(ovc[:, 0:OVER], ovc[:, 0:OVER], float(NE - 1), None, ALU.min))
                link(V.tensor_copy(ovc[:, OVER:OVER + 1], incl[0:1, NE - 1:NE]))
                link(V.tensor_copy(over_expert[:, :], ovc))

            def wo_low_half(q):
                at = slice(*WO_PARTS[q])
                dve.wait_ge(wo_hi_ready, q + 1)
                V.tensor_tensor(wo_lo[0][:, at], head_slot(U_O)[:, at], wo_hi[0][:, at],
                                ALU.subtract).then_inc(wo_lo_ready[0], 1)

            def x_rstd(t):
                m = TILES[t][1]
                dve.wait_ge(root_done, t + 1)
                V.reciprocal(stats[0:m, 10 + t:11 + t], stats[0:m, 5 + t:6 + t]).then_inc(rstd_done, 1)

            x_rstd(0)
            dve.wait_ge(small_loaded, 16)
            x_rstd(1)
            done = 0
            for n, (kind, c) in enumerate(JOBS):
                if "D" not in READERS[kind]:
                    continue
                b = pair(n)
                if kind == "lg":
                    dve.wait_ge(pe_jobs, HEAD.pe(("wo", WO_ORDER[-1])))
                    link(V.memset(logit, 0.0))
                    link(V.memset(scan[0][:, 0:16], 0.0))
                    link(V.memset(scan[1][:, 0:16], 0.0))
                    dve.wait_ge(route_loaded, 16 * 4)
                dve.wait_ge(pe_jobs, n + 1)
                if done:
                    dve.wait_ge(dve_jobs, done)
                done += 1
                if kind == "buf":
                    V.tensor_copy(conv_hist[:, :, :, :].rearrange("p c b r -> p c (b r)"),
                                  b[:, 0:CC * 16].rearrange("p (c n) -> p c n", c=CC)).then_inc(dve_jobs, 1)
                elif kind == "x":
                    r0, m = TILES[c]
                    tmp = u_tmp[c % 2].rearrange("p (k t) -> p k t", k=KD)[:, :, 0:m]
                    if c:
                        dve.wait_ge(u_split, c)
                    V.tensor_tensor(tmp, b.rearrange("p (k t) -> p k t", k=KD)[:, :, 0:m],
                                    wide(col["gmix"], [P, KD, m]), ALU.mult).then_inc(dve_jobs, 1)
                    if c + 2 < NT:
                        x_rstd(c + 2)
                    dve.wait_ge(dve_jobs, done)
                    link(V.tensor_copy(u_hi[:, :, r0:r0 + m], tmp))
                    V.tensor_tensor(u_lo[:, :, r0:r0 + m], tmp, u_hi[:, :, r0:r0 + m], ALU.subtract).then_inc(
                        u_split, 1)
                elif kind in "qk":
                    turn = c if kind == "q" else H + c
                    r, dst = rot[turn % 2], qk[:, turn, :]
                    two = "p (b c) -> p b c"
                    if turn == 0:
                        dve.wait_ge(xs_done, NT)
                        dve.wait_ge(u_split, NT)
                        dve.wait_ge(rope_loaded, 32)
                    dve.wait_ge(act_jobs, HEAD.done("A", (kind, c)))
                    dve.wait_ge(half_copied, turn + 1)
                    link(V.tensor_tensor(dst.rearrange(two, b=2), halves(b), cos_t[:, :].rearrange(two, b=2), ALU.mult))
                    link(V.tensor_tensor(r, r, sin_t[:, :], ALU.mult))
                    V.tensor_tensor(dst, dst, r, ALU.add).then_inc(dve_jobs, 1)
                    if (kind, c) == ("q", H - 1):
                        dve.wait_ge(dve_jobs, done)
                        link(V.memset(q_mask, 0.0))
                        link(V.tensor_copy(q_mask[:, :, 0:NB * NB:NB + 1], qk[:, 0:H, SEQ:T]))
                elif kind == "vb":
                    s3 = state[c % 4].rearrange("p (h e) -> p h e", h=H)
                    kv = kv_tmp.rearrange("p (h e) -> p h e", h=H)
                    kcol = qk[:, H:2 * H, SEQ + c:SEQ + c + 1].to_broadcast([P, H, P])
                    link(V.tensor_tensor(kv, b[:, 0:512].rearrange("p (h e) -> p h e", h=H), kcol, ALU.mult))
                    dve.wait_ge(state_scaled, c + 1)
                    V.scalar_tensor_tensor(state[c % 4], kv_tmp, SCALE, state[c % 4], ALU.mult,
                                           ALU.add).then_inc(dve_jobs, 1)
                elif kind == "so":
                    for h in range(H):
                        dst, src = o_few[:, h * P:(h + 1) * P], b[32 * h:32 * h + NB, 0:P]
                        if c == 0:
                            ins = V.tensor_copy(dst, src)
                        else:
                            ins = V.tensor_tensor(dst, dst, src, ALU.add)
                    ins.then_inc(dve_jobs, 1)
                elif kind == "ot":
                    V.tensor_copy(qk[:, 0:H, SEQ:T], b[:, 0:H * NB].rearrange("p (h n) -> p h n", h=H)).then_inc(
                        dve_jobs, 1)
                elif kind in ("scA", "scB"):
                    if (kind, c) == ("scA", 0):
                        dve.wait_ge(decay_loaded, 16 * 3)
                        link(V.tensor_tensor(w_r[:, :, :], w_r[:, :, :], wide(col["gffn"], [P, KD, NR]), ALU.mult))
                    dst = masked[c % 2]
                    if kind == "scA":
                        link(V.tensor_tensor(dst[:, 0:512], b[:, 0:512], decay[:, c, 0:512], ALU.mult))
                        V.tensor_tensor(dst[:, 512:896], b[:, 512:896], decay[:, c, 0:384],
                                        ALU.mult).then_inc(dve_jobs, 1)
                    else:
                        link(V.tensor_tensor(dst[:, 896:1152], b[:, 0:256], decay[:, c, 0:256], ALU.mult))
                        V.tensor_tensor(dst[:, 1152:1280], b[:, 512:640], decay[:, c, 0:128],
                                        ALU.mult).then_inc(dve_jobs, 1)
                elif kind == "kt":
                    V.tensor_tensor(kd[c % 2].rearrange("p (t d) -> p t d", t=4),
                                    b[:, 0:512].rearrange("p (t d) -> p t d", t=4),
                                    wide(col["kdec"][:, 4 * c:4 * c + 4], [P, 4, P]), ALU.mult).then_inc(dve_jobs, 1)
                elif kind == "mn":
                    o3 = qk[:, c, :].rearrange("p (b c) -> p b c", b=2)
                    V.tensor_tensor(o3, o3, halves(b), ALU.subtract).then_inc(dve_jobs, 1)
                elif kind == "vr":
                    r = qk[:, H + c, :]
                    dve.wait_ge(act_jobs, HEAD.done("A", ("vr", c)))
                    if c == 0:
                        for i in range(4):
                            dve.wait_ge(state_stored[i], 32)
                    link(V.reciprocal(r, r))
                    link(V.tensor_tensor(r, r, qk[:, c, :], ALU.mult))
                    V.scalar_tensor_tensor(mixT[:, CC + c, :], r, col["gn"][:, c:c + 1], gT[:, c, :], ALU.mult,
                                           ALU.mult).then_inc(dve_jobs, 1)
                elif kind == "hc":
                    z = zc[c % 2]
                    zs = z[:, 514:538].rearrange("p (b r) -> p b r", r=3)
                    link(V.memset(z[:, 0:2], 0.0))
                    link(V.tensor_copy(zs[:, :, 0:2], conv_hist[:, c, :, :]))
                    dve.wait_ge(act_jobs, HEAD.done("A", ("gc", c)))
                    g = gate_c[c % 2]
                    link(V.tensor_tensor(z[:, 2:262], b[:, 0:260], g[:, 0:260], ALU.mult))
                    link(V.tensor_tensor(z[:, 262:514], b[:, 512:764], g[:, 260:512], ALU.mult))
                    link(V.tensor_tensor(zs[:, :, 2:3], b[:, 764:772].unsqueeze(2), g[:, 512:520].unsqueeze(2),
                                         ALU.mult))
                    link(V.tensor_copy(new_z[:, c, 0:2], z[:, 512:514]))
                    V.tensor_copy(new_z[:, c, 2:10].unsqueeze(2), zs[:, :, 2:3]).then_inc(dve_jobs, 1)
                    dve.wait_ge(dve_jobs, done)
                    y = mixT[:, c, :]
                    ys = y[:, SEQ:T].unsqueeze(2)
                    w = col["convw"][:, 3 * c:3 * c + 3]
                    link(V.tensor_scalar(y[:, 0:SEQ], z[:, 0:SEQ], w[:, 0:1], None, ALU.mult))
                    link(V.tensor_scalar(ys, zs[:, :, 0:1], w[:, 0:1], None, ALU.mult))
                    for r in (1, 2):
                        link(V.scalar_tensor_tensor(y[:, 0:SEQ], z[:, r:r + SEQ], w[:, r:r + 1], y[:, 0:SEQ],
                                                    ALU.mult, ALU.add))
                        link(V.scalar_tensor_tensor(ys, zs[:, :, r:r + 1], w[:, r:r + 1], ys, ALU.mult, ALU.add))
                    if c == 2:
                        dve.wait_ge(pe_jobs, HEAD.pe(("st", H - 1)))
                        link(V.tensor_copy(mix_few[:, CC:KD, :], mixT[:, CC:KD, SEQ:T]))
                        dve.wait_ge(ret_hi_ready, 1)
                        V.tensor_tensor(mix_lo[:, CC * T:KD * T], region_m[:, CC * T:KD * T], ret_hi,
                                        ALU.subtract).then_inc(mix_split, 1)
                    if c == 3:
                        wo_low_half(1)
                elif kind == "gb":
                    y = mixT[:, c, :]
                    V.tensor_tensor(y.rearrange("p (b c) -> p b c", b=2), y.rearrange("p (b c) -> p b c", b=2),
                                    halves(b), ALU.mult).then_inc(dve_jobs, 1)
                    if c >= 2:
                        at = slice(0, 3 * T) if c == 2 else slice(3 * T, 4 * T)
                        ks = slice(0, 3) if c == 2 else slice(3, 4)
                        dve.wait_ge(dve_jobs, done)
                        link(V.tensor_copy(mix_few[:, ks, :], mixT[:, ks, SEQ:T]))
                        link(V.tensor_copy(conv_hi[:, at], region_m[:, at]))
                        V.tensor_tensor(mix_lo[:, at], region_m[:, at], conv_hi[:, at],
                                        ALU.subtract).then_inc(mix_split, 1)
                    if c == 2:
                        wo_low_half(0)
                elif kind == "wo":
                    m = TILES[c][1]
                    if m == P:
                        V.tensor_tensor(xh[:, c, :], xh[:, c, :], b, ALU.add).then_inc(h_done, 1)
                    else:
                        for g in range(4):
                            at = slice(g * 256, (g + 1) * 256)
                            ins = V.tensor_tensor(xh[0:m, c, at], xh[0:m, c, at], b[32 * g:32 * g + m, 0:256],
                                                  ALU.add)
                        ins.then_inc(h_done, 1)
                    dve.wait_ge(ffn_root_done, WO_ORDER.index(c) + 1)
                    link(V.reciprocal(stats[0:m, 10 + c:11 + c], stats[0:m, 20 + c:21 + c]))
                    turn = WO_ORDER.index(c)
                    if turn == 0:
                        dve.wait_ge(late_loaded, 16 * 2)
                    if turn >= 2:
                        dve.wait_ge(xn_stored[turn % 2], 16 * (turn // 2))
                    dve.wait_ge(h_done, turn + 1)
                    V.scalar_tensor_tensor(xn[turn % 2][0:m, :], xh[0:m, c, :], stats[0:m, 10 + c:11 + c],
                                           g_ffn_b[0:m, :], ALU.mult, ALU.mult).then_inc(dve_jobs, 1)
                elif kind == "lg":
                    bias = col["bias"].unsqueeze(1)
                    link(V.tensor_tensor(logit[:, 0:4, :], b[:, 0:4 * NR].rearrange("p (t c) -> p t c", t=4),
                                         wide(stats[:, 10:14], [P, 4, NR]), ALU.mult))
                    link(V.scalar_tensor_tensor(logit[0:NB, 4, :], b[0:NB, 512:512 + NR], stats[0:NB, 14:15],
                                                col["bias"][0:NB, :], ALU.mult, ALU.add))
                    V.tensor_tensor(logit[:, 0:4, :], logit[:, 0:4, :], bias.to_broadcast([P, 4, NR]),
                                    ALU.add).then_inc(dve_jobs, 1)
                    dve.wait_ge(dve_jobs, done)
                    route_choose()
                elif kind == "tot":
                    V.tensor_copy(total, b[:, 0:NE]).then_inc(dve_jobs, 1)
                    dve.wait_ge(dve_jobs, done)
                    incl = route_further()
                elif kind == "rk":
                    V.tensor_copy(rank, b[:, 0:NT * NE].rearrange("p (t c) -> p t c", t=NT)).then_inc(dve_jobs, 1)
                    dve.wait_ge(dve_jobs, done)
                    route_places(rank.unsqueeze(1).to_broadcast([P, 2, NT, NE]))
                    route_experts(incl)
                elif kind == "ix":
                    at_x, at_y = slice(0, NTILE), slice(NTILE, 2 * NTILE)
                    V.tensor_copy(ixf[0][:, at_y], b[:, 0:NTILE]).then_inc(dve_jobs, 1)
                    dve.wait_ge(dve_jobs, done)
                    link(V.tensor_scalar(index[:, at_x], ixf[0][:, at_y], -1.0, None, ALU.add))
                    link(V.tensor_scalar(index[:, at_y], index[:, at_x], 1, None, ALU.arith_shift_right))
                    link(V.tensor_scalar(ixf[1][:, at_y], ixf[0][:, at_y], 0.0, NOWHERE, ALU.is_equal, ALU.mult))
                    link(V.tensor_scalar(ixf[0][:, at_x], index[:, at_y], 2.0, col["half"], ALU.mult, ALU.add))
                    link(V.tensor_tensor(index[:, at_x], ixf[0][:, at_x], ixf[1][:, at_y], ALU.add))
                    link(V.tensor_scalar(ixf[0][:, at_y], ixf[0][:, at_y], 2.0, col["nh2"], ALU.mult, ALU.add))
                    V.tensor_tensor(index[:, at_y], ixf[0][:, at_y], ixf[1][:, at_y], ALU.add).then_inc(index_done, 1)
                    route_weights()

            def mult_up(b, count, s_sem, out_sem):
                dve.wait_ge(s_sem, count)
                V.tensor_tensor(hs[b], sg[b], ps[:, 2 + b, 256:512], ALU.mult).then_inc(out_sem, 1)

            def evac_h(b, count, t_sem, out_sem):
                dve.wait_ge(t_sem, count)
                V.tensor_copy(hT[b], ps[:, 4 + b, 0:256]).then_inc(out_sem, 1)

            with dve.Fori(0, NE // 2) as i:
                for b in range(2):
                    e = i * 2 + b
                    mult_up(b, e + 1, silu_done, hs_done)
                    evac_h(b, e + 1, ht_done, hT_ready)

            n_over = dve.value_load(over_expert[0:1, OVER:OVER + 1], min_val=0, max_val=OVER)
            with dve.If(n_over > 0):
                with dve.Fori(0, OVER) as q:
                    mult_up(0, q + 1, ov["silu"], ov["hs"])
                    evac_h(0, q + 1, ov["ht"], ov["hT"])
            with dve.Else():
                dve.wait_ge(index_done, 1)

            def combine(n, k):
                t = TAIL_TILES[n]
                m = TILES[t][1]
                yb, h = y_buf[n % 2], xh[0:m, t, :]
                if k == 0:
                    dve.wait_ge(y_loaded[n % 2], 16 * (n // 2 + 1))
                ins = V.scalar_tensor_tensor(h, yb[0:m, k * D:(k + 1) * D], wk[0:m, t, k:k + 1], h, ALU.mult, ALU.add)
                if k:
                    ins.then_inc(hy_done, 1)
                else:
                    link(ins)

            def split_rows(n):
                b = pair(REST.at[("u", n)])
                m = TILES[TAIL_TILES[n]][1]
                width = KD * m
                dve.wait_ge(pe_tail, REST.pe(("u", n)))
                if n >= 2:
                    dve.wait_ge(dve_tail, n - 1)
                    dve.wait_ge(pe_tail, REST.pe(GATES[gates(n - 1) - 1]))
                V.tensor_tensor(u3T[n % 2][:, 0:width].rearrange("p (k t) -> p k t", k=KD),
                                b.rearrange("p (k t) -> p k t", k=KD)[:, :, 0:m],
                                wide(col["gple"], [P, KD, m]), ALU.mult).then_inc(u3_ready, 1)
                dve.wait_ge(u3_ready, n + 1)
                more = n + 1 < NT
                if more and n != 1:
                    combine(n + 1, 0)
                dve.wait_ge(u3_hi_ready, n + 1)
                V.tensor_tensor(u3_lo[n % 2][:, 0:width], u3T[n % 2][:, 0:width], u3_hi[n % 2][:, 0:width],
                                ALU.subtract).then_inc(dve_tail, 1)
                if more and n == 1:
                    combine(n + 1, 0)
                if more:
                    combine(n + 1, 1)

            def gate_rstd(n):
                t = TAIL_TILES[n]
                m = TILES[t][1]
                dve.wait_ge(hy_root, n + 1)
                V.reciprocal(stats[0:m, 35 + t:36 + t], stats[0:m, 30 + t:31 + t]).then_inc(hy_rstd, 1)

            def gated(kind, n):
                t = TAIL_TILES[n]
                m = TILES[t][1]
                g, x, h = gate[n % 2][0:m, :], pp[0:m, t, :], xh[0:m, t, :]
                at = dict(pa=slice(0, 512), pb=slice(512, D), pg=slice(0, D))[kind]
                dve.wait_ge(act_tail, GATES.index((kind, n)) + 1)
                dve.wait_ge(hy_done, n + 1)
                link(V.tensor_tensor(x[:, at], x[:, at], g[:, at], ALU.mult))
                V.tensor_tensor(h[:, at], h[:, at], x[:, at], ALU.add).then_inc(f_done, 1)

            def final_norm(n):
                t = TAIL_TILES[n]
                m = TILES[t][1]
                h = xh[0:m, t, :]
                dve.wait_ge(f_root, n + 1)
                link(V.reciprocal(stats[0:m, 10 + t:11 + t], stats[0:m, 5 + t:6 + t]))
                dve.wait_ge(f_done, gates(n + 1))
                V.scalar_tensor_tensor(h, h, stats[0:m, 10 + t:11 + t], g_fin_b[0:m, :], ALU.mult,
                                       ALU.mult).then_inc(y_done, 1)

            for half, dst in enumerate((gate_lo[0][:, 0:2048], gate_lo_1[0])):
                dve.wait_ge(gate_hi_ready, half + 1)
                V.tensor_tensor(dst, ring[:, GATE_SLOTS[half], 0:2048],
                                gate_hi[half][:, 0:2048], ALU.subtract).then_inc(gate_lo_ready, 1)
            combine(0, 0)
            combine(0, 1)
            split_rows(0)
            gate_rstd(0)
            for n in range(NT):
                if n + 1 < NT:
                    split_rows(n + 1)
                gated("pa" if n else "pg", n)
                if n:
                    final_norm(n - 1)
                if n + 1 < NT:
                    gate_rstd(n + 1)
                if n:
                    gated("pb", n)
            final_norm(NT - 1)

        @block.tensor
        def _(pe):
            mm, tr = nc.tensor.matmul, nc.tensor.transpose

            def over_tokens(out, w_of, src, ks, m=P):
                for half in range(2):
                    for k in range(ks):
                        last = mm(halves(out)[0:m, half, :], w_of(k), src(k, half * HALF), start=(k == 0), stop=(k == ks - 1))
                return last

            def over_tokens_split(out, n):
                wh, wl = (x[n % 2].rearrange("p (k c) -> p k c", k=KD) for x in (w_hi, w_lo))
                for half in range(2):
                    if n == 0 and half == 1:
                        pe.wait_ge(u_split, NT)
                    cols = slice(half * HALF, (half + 1) * HALF)
                    for k in range(KD):
                        for s, (w, u) in enumerate(((wh, u_hi), (wh, u_lo), (wl, u_hi))):
                            last = mm(halves(out)[:, half, :], w[:, k, :], u[:, k, cols],
                                      start=(k == 0 and s == 0), stop=(k == KD - 1 and s == 2))
                return last

            def few_rows(out, src, w_of, ks):
                for k in range(ks):
                    for g in range(4):
                        last = mm(out[32 * g:32 * g + NB, 0:256], src(k), w_of(k, g), start=(k == 0),
                                  stop=(k == ks - 1))
                return last

            def u_cols(k, c0):
                return uT[:, k, c0:c0 + HALF]

            pe.wait_ge(consts_loaded, 16 * 2)
            for n, (kind, c) in enumerate(JOBS):
                b = pair(n)
                prev, readers = HEAD.free(n)
                if "A" in readers:
                    pe.wait_ge(act_jobs, HEAD.done("A", prev))
                if prev and prev[0] == "wo":
                    pe.wait_ge(h_done, WO_ORDER.index(prev[1]) + 1)
                elif "D" in readers:
                    pe.wait_ge(dve_jobs, HEAD.done("D", prev))

                def after(engine, job):
                    pe.wait_ge(act_jobs if engine == "A" else dve_jobs, HEAD.done(engine, job))

                if kind == "buf":
                    for k in range(CC):
                        last = tr(b[:, 16 * k:16 * k + 16], buf_rows[:, k * P:(k + 1) * P], ident[0:16, 0:16])
                elif kind == "x":
                    m = TILES[c][1]
                    pe.wait_ge(xs_done, c + 1)
                    for k in range(KD):
                        last = tr(b[:, k * P:k * P + m], xs[c % 2][0:m, k * P:(k + 1) * P], ident[0:m, 0:m])
                elif (kind, c) in CHUNKS:
                    chunk = CHUNKS.index((kind, c))
                    if chunk == 0:
                        pe.wait_ge(u_split, 3)
                    pe.wait_ge(w_hi_ready, chunk + 1)
                    pe.wait_ge(w_lo_ready, chunk + 1)
                    last = over_tokens_split(b, chunk)
                elif kind == "vt":
                    r0, m = TILES[c]
                    after("A", ("v", H - 1))
                    for h in range(H):
                        last = tr(b[0:m, h * P:(h + 1) * P], vT[:, h, r0:r0 + m], ident[:, :])
                elif kind == "vb":
                    after("A", ("vt", NT - 1))
                    last = mm(b[:, 0:512], ident[0:NB, c:c + 1].to_broadcast([NB, P]), v_rows[0:NB, 4, :],
                              start=True, stop=True)
                elif kind == "so":
                    after("D", ("vb", 4 * c + 3))
                    for i in range(4 * c, 4 * c + 4):
                        for h in range(H):
                            last = mm(b[32 * h:32 * h + NB, 0:P], q_mask[:, h, i * NB:(i + 1) * NB],
                                      state[i % 4][:, h * P:(h + 1) * P], start=(i % 4 == 0), stop=(i % 4 == 3))
                elif kind == "ot":
                    after("D", ("so", 1))
                    for h in range(H):
                        last = tr(b[:, h * NB:(h + 1) * NB], o_few[:, h * P:(h + 1) * P], ident[0:NB, 0:NB])
                elif kind in ("scA", "scB"):
                    kT, qT = qk[:, H + c, :], qk[:, c, :]
                    for half, j in enumerate((0, 1) if kind == "scA" else (2, 3)):
                        width = SEQ - j * P
                        last = mm(b[:, half * 512:half * 512 + width], kT[:, j * P:(j + 1) * P], qT[:, j * P:SEQ],
                                  start=True, stop=True)
                elif kind == "kt":
                    for j in range(4):
                        last = tr(b[:, j * P:(j + 1) * P], qk[:, H + c, j * P:(j + 1) * P], ident[:, :])
                elif kind == "pv":
                    after("D", ("scB", c))
                    at = 0
                    for j in range(4):
                        width = SEQ - j * P
                        last = mm(b[:, j * P:SEQ], v_rows[:, j, c * P:(c + 1) * P], masked[c % 2][:, at:at + width],
                                  start=(j == 0), stop=(j == 3))
                        at += width
                elif kind == "st":
                    after("D", ("kt", c))
                    for j in range(4):
                        last = mm(b[:, 0:P], kd[c % 2][:, j * P:(j + 1) * P], v_rows[:, j, c * P:(c + 1) * P],
                                  start=(j == 0), stop=(j == 3))
                elif kind == "mn":
                    if c == 0:
                        pe.wait_ge(decay_loaded, 16 * 3)
                    after("A", ("pv", c))
                    after("D", ("ot", 0))
                    last = over_tokens(b, lambda k: meanw[:, :], lambda k, c0: qk[:, c, c0:c0 + HALF], 1)
                elif kind == "vr":
                    after("A", ("mn", c))
                    last = over_tokens(b, lambda k: meanw[:, :], lambda k, c0: qk[:, H + c, c0:c0 + HALF], 1)
                elif kind == "co":
                    after("D", ("gb", CC - 1))
                    for k in range(CC):
                        last = tr(b[0:10, k * P:(k + 1) * P], new_z[:, k, :], ident[:, :])
                elif kind == "wo":
                    r0, m = TILES[c]
                    wh, wl = ([x.rearrange("p (k c) -> p k c", k=KD) for x in g] for g in (wo_hi, wo_lo))
                    lo = mix_lo.rearrange("p (k t) -> p k t", k=KD)
                    first = c == WO_ORDER[0]

                    def mix_hi(k):
                        src, at = (conv_hi, k * T) if k < CC else (ret_hi, (k - CC) * T)
                        return src[:, at + r0:at + r0 + m]

                    for half in range(2 if m == P else 0):
                        for n_k, k in enumerate((4, 5, 6, 7, 0, 1, 2, 3)):
                            if first and n_k % 4 == 0:
                                pe.wait_ge(wo_lo_ready[half], n_k // 4 + 1)
                                pe.wait_ge(mix_split, 1 if n_k == 0 else 3)
                            for i, (u, w) in enumerate(((mix_hi(k), wh), (lo[:, k, r0:r0 + m], wh), (mix_hi(k), wl))):
                                last = mm(b[:, half * 512:half * 512 + 512], u, w[half][:, k, :],
                                          start=(n_k == 0 and i == 0), stop=(n_k == KD - 1 and i == 2))
                    if m < P:
                        last = few_rows(b, lambda k: mix_few[:, k % KD, :],
                                        lambda k, g: (wh, wl)[k // KD][g // 2][
                                            :, k % KD, g % 2 * 256:g % 2 * 256 + 256].bitcast(F32), 2 * KD)
                elif kind == "xt":
                    m = TILES[c][1]
                    pe.wait_ge(h_done, WO_ORDER.index(c) + 1)
                    for k in range(KD):
                        last = tr(b[:, k * P:k * P + m], xh[0:m, c, k * P:(k + 1) * P], ident[0:m, 0:m])
                elif kind == "rt":
                    after("A", ("xt", (2, 3)[c]))
                    for k in range(KD):
                        last = mm(b[0:NR, 0:HALF], w_r[:, k, :], u_cols(k, c * HALF), start=(k == 0),
                                  stop=(k == KD - 1))
                elif kind == "lg":
                    after("A", ("rt", 1))
                    for t in range(4):
                        last = tr(b[:, t * NR:(t + 1) * NR], log_t[:, t * P:(t + 1) * P], ident[0:NR, 0:NR])
                    last = tr(b[0:NB, 512:512 + NR], log_t[:, SEQ:T], ident[0:NR, 0:NR])
                elif kind == "pt":
                    if c == 0:
                        pe.wait_ge(p_loaded, 16 * 2)
                        for t in range(4):
                            for k in range(2):
                                last = tr(b[:, k * 512 + t * P:k * 512 + (t + 1) * P], p_rows[:, t, k * P:(k + 1) * P],
                                          ident[:, :])
                    else:
                        for k in range(2):
                            last = tr(b[:, k * NB:(k + 1) * NB], p_rows[0:NB, 4, k * P:(k + 1) * P],
                                      ident[0:NB, 0:NB])
                elif kind == "pp":
                    r0, m = TILES[c]
                    after("A", ("pt", 1))
                    pe.wait_ge(pp_loaded, 16)
                    w = w_pp.rearrange("p (k c) -> p k c", k=2)
                    if m < P:
                        last = few_rows(b, lambda k: pT[:, k, r0:r0 + m],
                                        lambda k, g: w[:, k, g * 256:(g + 1) * 256], 2)
                    for half in range(2 if m == P else 0):
                        for k in range(2):
                            last = mm(b[0:m, half * 512:half * 512 + 512], pT[:, k, r0:r0 + m],
                                      w[:, k, half * 512:half * 512 + 512], start=(k == 0), stop=(k == 1))
                elif kind == "rk":
                    for t in range(NT):
                        for s in range(t + 1):
                            last = mm(b[:, t * NE:(t + 1) * NE], lt16[:, int(s < t), :], chosen[:, s, :],
                                      start=(s == 0), stop=(s == t))
                elif kind == "tot":
                    pe.wait_ge(chosen_done, 1)
                    for s in range(NT):
                        last = mm(b[:, 0:NE], lt16[:, 1, :], chosen[:, s, :], start=(s == 0), stop=(s == NT - 1))
                elif kind == "ix":
                    pe.wait_ge(hot_done, 1)
                    for s in range(2 * NT):
                        last = mm(b[:, 0:NTILE], row_hot[:, s, :], tile_hot[:, s, :], start=(s == 0), stop=(s == 2 * NT - 1))
                last.then_inc(pe_jobs, 1)

            def rows_t(b, in_wait, out_sem):
                pe.wait_ge(*in_wait)
                for k in range(4):
                    last = tr(ps[:, b, k * P:(k + 1) * P], xg[b][:, k * P:(k + 1) * P], ident[:, :])
                last.then_inc(out_sem, 1)

            def in_ring(slot):
                return lambda k: ring[:, slot, k * 512:k * 512 + 512]

            def in_spare(i):
                def rows(k):
                    ap, (c0, _) = next(x for x in spare[i] if x[1][0] <= k * 512 < x[1][1])
                    return ap[:, k * 512 - c0:k * 512 - c0 + 512]
                return rows

            def gate_up(b, units, out_sem):
                xv = xgT[b].rearrange("p (k h r) -> p h k r", h=2, r=ROWS)
                for k in range(KD):
                    for side in range(2):
                        last = mm(ps[side * 64:side * 64 + 64, 2 + b, :], xv[:, k // 4, k % 4, :], units[side](k),
                                  start=(k == 0), stop=(k == KD - 1))
                last.then_inc(out_sem, 1)

            def hidden_t(b, out_sem):
                for k in range(2):
                    last = tr(ps[:, 4 + b, k * P:(k + 1) * P], hs[b][:, k * P:(k + 1) * P], ident[:, :])
                last.then_inc(out_sem, 1)

            def down(b, slot, out_sem):
                w = slot.rearrange("p (k c) -> p k c", k=4)
                for q in range(4):
                    side_in, k = divmod(q, 2)
                    hv = hT[b][:, k * P + side_in * 64:k * P + side_in * 64 + 64]
                    for side in range(2):
                        last = mm(ps[side * 64:side * 64 + 64, 6 + b, :], hv, w[:, q, side * 512:side * 512 + 512],
                                  start=(q == 0), stop=(q == 3))
                last.then_inc(out_sem, 1)

            def pair_of_experts(i, first, last):
                for b in range(2):
                    e = i * 2 + b
                    pe.wait_ge(xgT_ready, e + 1)
                    units = []
                    for j in range(2):
                        slot, filled = pair_fill(i, 3 * b + j)
                        if slot is None:
                            pe.wait_ge(spare_loaded[j], 16 * len(spare[j]))
                            units.append(in_spare(j))
                        else:
                            pe.wait_ge(slot_filled[slot], filled)
                            units.append(in_ring(slot))
                    gate_up(b, units, gu_done)
                    pe.wait_ge(hs_done, e + 1)
                    hidden_t(b, ht_done)
                    if not (last and b == 1):
                        rows_t(1 - b, (xg_loaded[1 - b], i * 16 + 16 * (1 + b)), xt_done)
                    pe.wait_ge(hT_ready, e + 1)
                    slot, filled = pair_fill(i, 3 * b + 2)
                    pe.wait_ge(slot_filled[slot], filled)
                    if not first:
                        pe.wait_ge(out_ready, e - 1)
                    down(b, ring[:, slot, :], down_done)

            pe.wait_ge(act_jobs, HEAD.count("A", len(JOBS)))
            pe.wait_ge(dve_jobs, HEAD.count("D", len(JOBS)))
            rows_t(0, (xg_loaded[0], 16), xt_done)
            pair_of_experts(0, True, False)
            pair_of_experts(1, False, False)
            with pe.Fori(2, NE // 2 - 1) as i:
                pair_of_experts(i, False, False)
            pair_of_experts(NE // 2 - 1, False, True)

            n_over = pe.value_load(over_expert[0:1, OVER:OVER + 1], min_val=0, max_val=OVER)
            with pe.If(n_over > 0):
                pe.wait_ge(out_ready, NE)
                with pe.Fori(0, OVER) as q:
                    rows_t(0, (ov["xg"], q * 16 + 16), ov["xt"])
                    pe.wait_ge(ov["xgT"], q + 1)
                    pe.wait_ge(ov["w"], q * 48 + 48)
                    gate_up(0, [in_ring(slot) for slot in OVER_SLOTS[0:2]], ov["gu"])
                    pe.wait_ge(ov["hs"], q + 1)
                    hidden_t(0, ov["ht"])
                    pe.wait_ge(ov["hT"], q + 1)
                    down(0, ring[:, OVER_SLOTS[2], :], ov["down"])
                    pe.wait_ge(ov["out"], q + 1)
            with pe.Else():
                pe.wait_ge(index_done, 1)

            pe.wait_ge(out_ready, NE)
            for n, (kind, turn) in enumerate(TAIL):
                b = pair(n)
                t = TAIL_TILES[turn]
                m = TILES[t][1]
                prev, _ = REST.free(n)
                if prev:
                    if prev[0] == "u":
                        pe.wait_ge(u3_ready, prev[1] + 1)
                    else:
                        pe.wait_ge(act_tail, GATES.index(prev) + 1)
                if kind == "u":
                    pe.wait_ge(hy_done, turn + 1)
                    for k in range(KD):
                        last = tr(b[:, k * P:k * P + m], xh[0:m, t, k * P:(k + 1) * P], ident[0:m, 0:m])
                else:
                    pe.wait_ge(u3_hi_ready, turn + 1)
                    pe.wait_ge(dve_tail, turn + 1)
                    uh, ul = (x[turn % 2][:, 0:KD * m].rearrange("p (k t) -> p k t", k=KD) for x in (u3_hi, u3_lo))
                    if m < P:
                        for half, slot in enumerate(GATE_SLOTS):
                            pe.wait_ge(slot_filled[slot], pair_fill(NE // 2, half)[1])
                        wg = [ring[:, slot, :].rearrange("p (k c) -> p k c", k=KD) for slot in GATE_SLOTS]
                        uv = u3T[turn % 2][:, 0:KD * m].rearrange("p (k t) -> p k t", k=KD)
                        last = few_rows(b, lambda k: uv[:, k, :],
                                        lambda k, g: wg[g // 2][:, k, g % 2 * 256:g % 2 * 256 + 256], KD)
                    for half in dict(pa=(0,), pb=(1,), pg=())[kind]:
                        if turn == 1:
                            pe.wait_ge(gate_lo_ready, 4)
                        for k in range(KD):
                            high = gate_hi[half][:, k * 512:k * 512 + 512]
                            for i, (u, w) in enumerate(((uh, high), (ul, high), (uh, gate_low(half, k)))):
                                last = mm(b[:, half * 512:half * 512 + 512], u[:, k, :], w,
                                          start=(k == 0 and i == 0), stop=(k == KD - 1 and i == 2))
                last.then_inc(pe_tail, 1)


def small_constants():
    p = np.arange(P, dtype=np.float32)
    lg = np.log(np.float32(1.0) - np.float32(2.0) ** (np.float32(-5.0) - np.arange(H, dtype=np.float32)))
    lg = lg.astype(np.float32)
    inv = np.float32(1.0) / np.float32(10000.0) ** (np.arange(0, P, 2, dtype=np.float32) / np.float32(P))
    pos = np.concatenate([np.arange(SEQ), np.full(NB, PAST)]).astype(np.float32)
    ang = (pos[None, :] * inv.astype(np.float32)[:, None]).astype(np.float32)
    cos = np.cos(ang).astype(np.float32)
    sin = np.sin(ang).astype(np.float32)
    diff = np.arange(SEQ)[None, :] - np.arange(P)[:, None]
    decay = np.stack([np.where(diff >= 0, np.exp(np.float64(g) * np.maximum(diff, 0)), 0.0) for g in lg], 1) * SCALE
    left = (SEQ - 1 - np.arange(SEQ)).reshape(4, P).T
    kdec = np.stack([np.exp(np.float64(g) * left) for g in lg], 1) * SCALE
    token = np.zeros((P, NT), np.float32)
    for t, (r0, m) in enumerate(TILES):
        token[:m, t] = r0 + np.arange(m) + 1
    valp = np.stack([np.where(token > 0, (token - 1) * 2 + k + 1, 0) for k in range(2)], 1)
    c = dict(
        kdec=kdec.reshape(P, 16), gam=np.tile(np.exp(lg.astype(np.float64)), (P, 1)),
        desc4=np.tile(np.arange(NG, 0, -1), (P, 1)), desc8=np.tile(np.arange(EPG, 0, -1), (P, 1)),
        thr=np.tile(np.arange(1, 9) * ROWS, (P, 1)),
        live=token > 0, valp=valp.reshape(P, 10), half=(np.arange(P) // 64).reshape(P, 1),
        nh2=(np.arange(P) // 64 - 2).reshape(P, 1), eps=np.full((P, 1), EPS), io48=np.tile(np.arange(NTILE), (P, 1)))
    c = {k: x.astype(np.float32) for k, x in c.items()}
    big = dict(
        cos=np.concatenate([cos, cos]), sin=np.concatenate([-sin, sin]),
        decay=decay.reshape(P, H * SEQ).astype(np.float32), ident=np.eye(P, dtype=np.float32),
        meanw=np.full((P, P), 1.0 / P, np.float32),
        lt16=np.stack([(p[:, None] < p[None, :]), np.ones((P, P))], 1).astype(np.float16),
        io128=np.tile(np.arange(P) % ROWS, (P, 1)).astype(np.float32),
        io32=np.tile(np.arange(NE), (P, 1)).astype(np.float32),
        io16=np.tile(np.arange(OVER), (P, 1)).astype(np.float32))
    return c, big


def columns(vector):
    return np.ascontiguousarray(vector.reshape(-1, P).T)


def k_major(w, width):
    k, n = w.shape
    return np.ascontiguousarray(w.reshape(k // P, P, n // width, width).transpose(2, 1, 0, 3).reshape(
        n // width, P, (k // P) * width))


def layout(i):
    c, arrays = small_constants()
    g = lambda name: np.asarray(i[name])
    c["gmix"], c["gffn"], c["gple"] = (columns(g(name)[0]) for name in ("g_mix", "g_ffn", "g_ple"))
    c["convw"] = g("conv_w")[0].reshape(3, CC, P).transpose(2, 1, 0).reshape(P, 12)
    c["gn"] = columns(g("ret_gn")[0])
    bias = np.concatenate([g("b_router_group")[0], g("b_router_expert")[0].reshape(-1)])
    c["bias"] = np.broadcast_to(bias, (P, NR))
    order = ["gmix", "gffn", "gple", "convw", "gn", "kdec", "gam", "bias", "desc4", "desc8", "thr", "live", "valp", "half", "nh2",
             "eps", "io48"]
    arrays["small"] = np.ascontiguousarray(np.concatenate([c[k] for k in order], 1))
    arrays["x"] = np.concatenate([g("x_prompt")[0], g("x_sample")[:, 0]], 0)
    arrays["p"] = np.concatenate([g("p_prompt")[0, 0], g("p_sample")[0, :, 0]], 0)
    arrays["state_conv"] = np.ascontiguousarray(g("state_conv")[0])
    arrays["state_ret"] = np.ascontiguousarray(g("state_ret")[0])
    w_in = k_major(g("w_in")[0], P).reshape(WIN_UNITS, 4, P, D).transpose(0, 2, 1, 3).reshape(WIN_UNITS, P, UNIT)
    arrays["w_in"] = np.ascontiguousarray(w_in[[3, 5, 4, 6, 1, 2, 0]])
    arrays["w_o"] = k_major(g("w_o")[0], 512)
    arrays["w_ple_gate"] = k_major(g("w_ple_gate")[0], 512)
    arrays["w_ple_proj"] = k_major(g("w_ple_proj")[0], D)[0]
    w_r = np.concatenate([g("w_router_group")[0], g("w_router_expert")[0]], 1)
    arrays["w_r"] = np.ascontiguousarray(w_r.reshape(KD, P, NR).transpose(1, 0, 2))
    exp = np.empty((NE, 3, P, UNIT), np.float32)
    gu = exp[:, :2].reshape(NE, 2, P, KD, 2, 256)
    for s, name in enumerate(("w_gate", "w_up")):
        gu[:, :, :, :, s, :] = g(name)[0].reshape(NE, KD, P, 2, 256).transpose(0, 3, 2, 1, 4)
    exp[:, 2] = g("w_down")[0].reshape(NE, 4, P, D).transpose(0, 2, 1, 3).reshape(NE, P, UNIT)
    arrays["w_exp"] = exp.reshape(NE * 3, P, UNIT)
    arrays["g_ffn"] = g("g_ffn")
    arrays["g_final"] = g("g_final").reshape(1, D)
    return arrays


OUTS = dict(y=(T, D), conv_p=(2, 512), ret_p=(H, P, P), conv_s=(NB, 2, 512), ret_s=(NB, H, P, P))


def kernel(**inputs):
    import concourse.bacc as bacc
    from concourse.bass_utils import run_bass_kernel_spmd

    nc = bacc.Bacc("TRN2", target_bir_lowering=False, num_devices=1)
    arrays = {f"in_{k}": v for k, v in layout(inputs).items()}
    ins = {k[3:]: nc.dram_tensor(k, v.shape, mybir.dt.from_np(v.dtype), kind="ExternalInput").ap()
           for k, v in arrays.items()}
    outs = {k: nc.dram_tensor(f"out_{k}", s, F32, kind="ExternalOutput").ap() for k, s in OUTS.items()}
    build(nc, ins, outs)
    r = run_bass_kernel_spmd(nc, [arrays], core_ids=[0]).results[0]
    y = r["out_y"]
    return (y[:SEQ].reshape(1, SEQ, D), y[SEQ:].reshape(NB, 1, D), r["out_conv_p"].reshape(1, 1, 2, 512),
            r["out_ret_p"].reshape(1, 1, H, P, P), r["out_conv_s"].reshape(1, NB, 2, 512),
            r["out_ret_s"].reshape(1, NB, H, P, P))
```
